# Optimizing a Trainium2 kernel written in Bass

```python
import jax
import jax.numpy as jnp
from jax import lax
import numpy as np

D_MODEL = 1024
BATCH = 1
SEQ = 256
DEPTH = 2

GRID_W = 64
CTX_LEN = 256
EPS = 1e-6

FOURIER_GROUPS = 4
FOURIER_GW = D_MODEL // 16
FOURIER_W = FOURIER_GROUPS * FOURIER_GW
CONV_W = D_MODEL // 4
CONV_K = 31
POOL_WINDOWS = (2, 4, 8, 16)
POOL_GW = D_MODEL // 16
POOL_W = len(POOL_WINDOWS) * POOL_GW
HEAD_DIM = 64
N_HEADS = D_MODEL // 128
N_KV_HEADS = N_HEADS // 4
Q_PER_KV = N_HEADS // N_KV_HEADS
Q_W = N_HEADS * HEAD_DIM
KV_W = N_KV_HEADS * HEAD_DIM
ROPE_THETA = 10000.0
Q_BLOCK = 128
N_BRANCH = 4

OFF_F = 0
OFF_C = OFF_F + FOURIER_W
OFF_P = OFF_C + 2 * CONV_W
OFF_Q = OFF_P + POOL_W
OFF_K = OFF_Q + Q_W
OFF_V = OFF_K + KV_W
OFF_G = OFF_V + KV_W
IN_W = OFF_G + N_BRANCH * D_MODEL

D_FF = ((8 * D_MODEL // 3 + 127) // 128) * 128
N_EXPERTS = 8
TOP_K = 2
D_FF_EXPERT = 7 * D_MODEL // 2
N_DENSE = (DEPTH + 1) // 2
N_MOE = DEPTH // 2

kernel_name = 'hybrid_parallel_fnet_conformer_pool_gqa_moe_dit'

def rmsnorm(x, g):
    xf = x.astype(jnp.float32)
    y = xf * lax.rsqrt(jnp.mean(xf * xf, axis=-1, keepdims=True) + EPS)
    return (y * g.astype(jnp.float32)).astype(x.dtype)

def modulation(cond, w_mod, b_mod):
    m = jax.nn.silu(cond) @ w_mod + b_mod
    return jnp.split(m, 6, axis=-1)

def axial_rope_tables(rows):
    n_freq = HEAD_DIM // 4
    freqs = ROPE_THETA ** (-jnp.arange(n_freq, dtype=jnp.float32) / n_freq)
    row = jnp.repeat(jnp.arange(rows, dtype=jnp.float32), GRID_W)
    col = jnp.tile(jnp.arange(GRID_W, dtype=jnp.float32), rows)
    ang_r = row[:, None] * freqs
    ang_c = col[:, None] * freqs
    return (jnp.cos(ang_r), jnp.sin(ang_r), jnp.cos(ang_c), jnp.sin(ang_c))

def _rotate_half(xh, cos, sin):
    x1, x2 = jnp.split(xh, 2, axis=-1)
    cos = cos[None, :, None, :]
    sin = sin[None, :, None, :]
    return jnp.concatenate([x1 * cos - x2 * sin, x1 * sin + x2 * cos], axis=-1)

def apply_axial_rope(x, rope):
    cos_r, sin_r, cos_c, sin_c = rope
    xf = x.astype(jnp.float32)
    half = HEAD_DIM // 2
    out = jnp.concatenate([_rotate_half(xf[..., :half], cos_r, sin_r),
                           _rotate_half(xf[..., half:], cos_c, sin_c)], axis=-1)
    return out.astype(x.dtype)

def q_heads(proj, q_norm_g):
    b, l = proj.shape[0], proj.shape[1]
    return rmsnorm(proj[..., OFF_Q:OFF_K].reshape(b, l, N_HEADS, HEAD_DIM), q_norm_g)

def kv_heads(proj_kv, k_norm_g):
    b, l = proj_kv.shape[0], proj_kv.shape[1]
    k = rmsnorm(proj_kv[..., :KV_W].reshape(b, l, N_KV_HEADS, HEAD_DIM), k_norm_g)
    v = proj_kv[..., KV_W:].reshape(b, l, N_KV_HEADS, HEAD_DIM)
    return k, v

def gqa_attend(qg, k, v):
    s = jnp.einsum('bqkgd,bskd->bkgqs', qg, k).astype(jnp.float32) * (HEAD_DIM ** -0.5)
    p = jax.nn.softmax(s, axis=-1).astype(v.dtype)
    return jnp.einsum('bkgqs,bskd->bqkgd', p, v)

def latent_attention(q, k_all, v_all):
    b, l = q.shape[0], q.shape[1]
    n_blocks = l // Q_BLOCK
    qb = q.reshape(b, n_blocks, Q_BLOCK, N_KV_HEADS, Q_PER_KV, HEAD_DIM).transpose(1, 0, 2, 3, 4, 5)
    ob = lax.map(lambda q_blk: gqa_attend(q_blk, k_all, v_all), qb)
    return ob.transpose(1, 0, 2, 3, 4, 5).reshape(b, l, Q_W)

def fourier_mix(u):
    b, l = u.shape[0], u.shape[1]
    ug = u.astype(jnp.float32).reshape(b, l, FOURIER_GROUPS, FOURIER_GW)
    f = jnp.fft.fft2(ug, axes=(1, 3), norm='ortho').real
    return f.reshape(b, l, FOURIER_W).astype(u.dtype)

def conv_module(u, conv_dw, conv_b, conv_norm_g):
    a, gate = jnp.split(u, 2, axis=-1)
    y = a * jax.nn.sigmoid(gate)
    y = lax.conv_general_dilated(
        y, conv_dw[:, None, :].astype(y.dtype), window_strides=(1,),
        padding=((CONV_K // 2, CONV_K // 2),),
        dimension_numbers=('NWC', 'WIO', 'NWC'), feature_group_count=CONV_W) + conv_b
    return jax.nn.silu(rmsnorm(y, conv_norm_g))

def pool_mix(u, pool_w, pool_scale):
    b, l = u.shape[0], u.shape[1]
    t = jnp.arange(l)
    uf = u.astype(jnp.float32)
    outs = []
    for i, w in enumerate(POOL_WINDOWS):
        xg = uf[..., i * POOL_GW:(i + 1) * POOL_GW]
        csum = jnp.concatenate([jnp.zeros((b, 1, POOL_GW), jnp.float32), jnp.cumsum(xg, axis=1)], axis=1)
        lo = jnp.clip(t - w // 2, 0, l)
        hi = jnp.clip(t + w // 2, 0, l)
        mean = (csum[:, hi] - csum[:, lo]) / (hi - lo).astype(jnp.float32)[None, :, None]
        outs.append(mean - xg)
    y = jnp.stack(outs, axis=2)
    y = jnp.einsum('blgc,gcd->blgd', y, pool_w.astype(jnp.float32)).reshape(b, l, POOL_W)
    return (y * pool_scale.astype(jnp.float32)).astype(u.dtype)

def merge_branches(proj, attn, lp):
    f = fourier_mix(proj[..., OFF_F:OFF_C]) @ lp['w_br_fourier']
    cv = conv_module(proj[..., OFF_C:OFF_P], lp['conv_dw'], lp['conv_b'], lp['conv_norm_g']) @ lp['w_br_conv']
    pl = pool_mix(proj[..., OFF_P:OFF_Q], lp['pool_w'], lp['pool_scale']) @ lp['w_br_pool']
    at = attn @ lp['w_br_attn']
    merged = sum(jax.nn.sigmoid(proj[..., OFF_G + i * D_MODEL:OFF_G + (i + 1) * D_MODEL]) * br
                 for i, br in enumerate((f, cv, pl, at)))
    return merged @ lp['w_out']

def swiglu(h, w1, w3, w2):
    return (jax.nn.silu(h @ w1) * (h @ w3)) @ w2

def moe_swiglu(h, router, w1, w3, w2):
    logits = (h @ router).astype(jnp.float32)
    top_v, top_i = lax.top_k(logits, TOP_K)
    wts = jax.nn.softmax(top_v, axis=-1)
    comb = jnp.sum(jax.nn.one_hot(top_i, N_EXPERTS, dtype=jnp.float32) * wts[..., None], axis=-2)
    return sum(comb[..., e:e + 1].astype(h.dtype) * swiglu(h, w1[e], w3[e], w2[e])
               for e in range(N_EXPERTS))

def channel_mixer(h, layer, ffn_w1, ffn_w3, ffn_w2, moe_router, moe_w1, moe_w3, moe_w2):
    j = layer // 2
    if layer % 2 == 0:
        return swiglu(h, ffn_w1[j], ffn_w3[j], ffn_w2[j])
    return moe_swiglu(h, moe_router[j], moe_w1[j], moe_w3[j], moe_w2[j])

def _normal(key, shape, scale):
    return jax.random.normal(key, shape, jnp.float32) * scale

def setup_inputs(seed: int = 0) -> dict:
    key = jax.random.key(seed)
    ks = jax.random.split(key, 28)
    L, D = DEPTH, D_MODEL
    return {
        'x': _normal(ks[0], (BATCH, SEQ, D), 1.0),
        'c': _normal(ks[1], (BATCH, D), 1.0),
        'ctx': _normal(ks[2], (BATCH, CTX_LEN, D), 1.0),
        'c_ctx': _normal(ks[3], (D,), 1.0),
        'w_mod': _normal(ks[4], (L, D, 6 * D), D ** -0.5),
        'b_mod': _normal(ks[5], (L, 6 * D), 0.02),
        'norm1_g': 1.0 + _normal(ks[6], (L, D), 0.02),
        'norm2_g': 1.0 + _normal(ks[7], (L, D), 0.02),
        'w_in': _normal(ks[8], (L, D, IN_W), D ** -0.5),
        'w_br_fourier': _normal(ks[9], (L, FOURIER_W, D), FOURIER_W ** -0.5),
        'conv_dw': _normal(ks[10], (L, CONV_K, CONV_W), CONV_K ** -0.5),
        'conv_b': _normal(ks[11], (L, CONV_W), 0.02),
        'conv_norm_g': 1.0 + _normal(ks[12], (L, CONV_W), 0.02),
        'w_br_conv': _normal(ks[13], (L, CONV_W, D), CONV_W ** -0.5),
        'pool_w': _normal(ks[14], (L, len(POOL_WINDOWS), POOL_GW, POOL_GW), POOL_GW ** -0.5),
        'pool_scale': 1.0 + _normal(ks[15], (L, POOL_W), 0.02),
        'w_br_pool': _normal(ks[16], (L, POOL_W, D), POOL_W ** -0.5),
        'q_norm_g': 1.0 + _normal(ks[17], (L, HEAD_DIM), 0.02),
        'k_norm_g': 1.0 + _normal(ks[18], (L, HEAD_DIM), 0.02),
        'w_br_attn': _normal(ks[19], (L, Q_W, D), Q_W ** -0.5),
        'w_out': _normal(ks[20], (L, D, D), D ** -0.5),
        'ffn_w1': _normal(ks[21], (N_DENSE, D, D_FF), D ** -0.5),
        'ffn_w3': _normal(ks[22], (N_DENSE, D, D_FF), D ** -0.5),
        'ffn_w2': _normal(ks[23], (N_DENSE, D_FF, D), D_FF ** -0.5),
        'moe_router': _normal(ks[24], (N_MOE, D, N_EXPERTS), D ** -0.5),
        'moe_w1': _normal(ks[25], (N_MOE, N_EXPERTS, D, D_FF_EXPERT), D ** -0.5),
        'moe_w3': _normal(ks[26], (N_MOE, N_EXPERTS, D, D_FF_EXPERT), D ** -0.5),
        'moe_w2': _normal(ks[27], (N_MOE, N_EXPERTS, D_FF_EXPERT, D), D_FF_EXPERT ** -0.5),
    }

def reference(x, c, ctx, c_ctx, w_mod, b_mod, norm1_g, norm2_g, w_in, w_br_fourier, conv_dw, conv_b,
              conv_norm_g, w_br_conv, pool_w, pool_scale, w_br_pool, q_norm_g, k_norm_g, w_br_attn, w_out,
              ffn_w1, ffn_w3, ffn_w2, moe_router, moe_w1, moe_w3, moe_w2):
    rows = x.shape[1] // GRID_W
    rope = axial_rope_tables(rows)
    xc = ctx
    for layer in range(DEPTH):
        lp = {
            'w_br_fourier': w_br_fourier[layer], 'conv_dw': conv_dw[layer], 'conv_b': conv_b[layer],
            'conv_norm_g': conv_norm_g[layer], 'w_br_conv': w_br_conv[layer], 'pool_w': pool_w[layer],
            'pool_scale': pool_scale[layer], 'w_br_pool': w_br_pool[layer], 'w_br_attn': w_br_attn[layer],
            'w_out': w_out[layer],
        }
        is_last = layer == DEPTH - 1
        w_in_l = w_in[layer]
        sh1, sc1, g1, sh2, sc2, g2 = [m[:, None, :] for m in modulation(c, w_mod[layer], b_mod[layer])]
        csh1, csc1, cg1, csh2, csc2, cg2 = modulation(c_ctx, w_mod[layer], b_mod[layer])

        hc = rmsnorm(xc, norm1_g[layer]) * (1 + csc1) + csh1
        if is_last:
            kc, vc = kv_heads(hc @ w_in_l[:, OFF_K:OFF_G], k_norm_g[layer])
        else:
            proj_c = hc @ w_in_l
            kc, vc = kv_heads(proj_c[..., OFF_K:OFF_G], k_norm_g[layer])
            qc = q_heads(proj_c, q_norm_g[layer])
            bc, lc = qc.shape[0], qc.shape[1]
            attn_c = gqa_attend(qc.reshape(bc, lc, N_KV_HEADS, Q_PER_KV, HEAD_DIM), kc, vc).reshape(bc, lc, Q_W)

        h = rmsnorm(x, norm1_g[layer]) * (1 + sc1) + sh1
        proj = h @ w_in_l
        q = apply_axial_rope(q_heads(proj, q_norm_g[layer]), rope)
        k, v = kv_heads(proj[..., OFF_K:OFF_G], k_norm_g[layer])
        k = apply_axial_rope(k, rope)
        attn = latent_attention(q, jnp.concatenate([k, kc], axis=1), jnp.concatenate([v, vc], axis=1))
        x = x + g1 * merge_branches(proj, attn, lp)

        h2 = rmsnorm(x, norm2_g[layer]) * (1 + sc2) + sh2
        x = x + g2 * channel_mixer(h2, layer, ffn_w1, ffn_w3, ffn_w2, moe_router, moe_w1, moe_w3, moe_w2)

        if not is_last:
            xc = xc + cg1 * merge_branches(proj_c, attn_c, lp)
            hc2 = rmsnorm(xc, norm2_g[layer]) * (1 + csc2) + csh2
            xc = xc + cg2 * channel_mixer(hc2, layer, ffn_w1, ffn_w3, ffn_w2, moe_router, moe_w1, moe_w3, moe_w2)
    return x


_drawn_inputs = setup_inputs


def setup_inputs(seed=0):
    import zlib

    import numpy as np

    out = dict(_drawn_inputs(seed))
    spreads = {}
    factors = {'norm1_g': 3.011,
     'conv_b': 4.17,
     'conv_norm_g': 4.052,
     'q_norm_g': 5.44,
     'k_norm_g': 3.236,
     'norm2_g': 2.821}
    for name, (base, spread) in spreads.items():
        noise = np.random.default_rng([zlib.crc32(name.encode()), seed]).standard_normal(out[name].shape)
        drawn = base * np.exp(spread * noise) if base else spread * noise
        out[name] = jnp.asarray(drawn.astype(out[name].dtype))
    for name, factor in factors.items():
        out[name] = (out[name] * factor).astype(out[name].dtype)
    return out
```

```python
from contextlib import ExitStack

import numpy as np

import concourse.bass as bass
from concourse import mybir

F32 = mybir.dt.float32
I32 = mybir.dt.int32
ALU = mybir.AluOpType
ACT = mybir.ActivationFunctionType
AX = mybir.AxisListType.X

P = 128
DEPTH, D, LAT, CTX = 2, 1024, 256, 256
T = LAT + CTX
KD = D // P
GRID_W = 64
EPS = 1e-6
HD = 64
NH, NKV = 8, 2
CONV_K = 31
HALO = CONV_K // 2
PADT = LAT + 2 * HALO
WINDOWS = (2, 4, 8, 16)
F_TILES = 2816 // P
E, FE_TILES = 8, 3584 // P
SLOTS = P

BLOCK_KV, BLOCK_Q, BLOCK_FC, BLOCK_GP = range(4)
BRANCH_ORDER = (0, 2, 3, 1)
BRANCH_K = (2, 2, 2, 4)
BLOCK_BRANCH, BLOCK_OUT = 4, 12
N_BLOCKS = 14
BLOCK_LEN = [KD * 256] + [KD * 512] * 3 + [(KD + BRANCH_K[i]) * 512 for i in BRANCH_ORDER for _ in range(2)] \
    + [KD * 512] * 2
SLOT_LEN = max(BLOCK_LEN)
RING = 3
MOD_BLOCKS = 6 * D // 512
MOE_UNROLL = 7
MOE_TURNS = FE_TILES // MOE_UNROLL
CHUNK = 3 * D

COLS = {}
_at = 0
for _name, _n in (("b_mod", 48), ("norm1", 8), ("norm2", 8), ("conv_b", 2), ("conv_g", 2), ("pool_scale", 2),
                  ("q_g", 1), ("k_g", 1), ("taps", 2 * CONV_K), ("pool_w", 2 * P)):
    COLS[_name] = (_at, _at + _n)
    _at += _n
VEC_LEN = _at
CONST = {}
_at = 0
for _name, _n in (("ident", P), ("ones", P), ("heads", P), ("rot", P), ("dup0", P), ("dup1", P), ("chan_cos", P),
                  ("chan_sin", P), ("below", P), ("iota", P), ("iota8", 8), ("eps", 1), ("seq", 2 * 512),
                  ("cos", LAT), ("sin", LAT)):
    CONST[_name] = (_at, _at + _n)
    _at += _n
CONST_LEN = _at
POOL_LEN = 2 * 2 * 512
N_SHIFTS = 2 * KD + 2 * KD + 2 * KD + KD
LOGITS, EQUAL, FIRST, REST, SECOND, MASK, COMB, RANK, TOP, GAP, ODDS, WEIGHT = range(12)


LAG = 3


def attention_units(layer):
    return [(s, g, qt, j) for s in range(2 - layer) for g in range(NKV) for qt in range(2) for j in range(4)]


def psum_order(layer):
    streams = range(2 - layer)
    order = ["norm1", "k", "v"] + [f"q{t}" for t in range(4)]
    order += [f"F{s}" for s in streams] + ["ca0", "ca1"]
    order += [f"heads{t}" for t in range(5)]
    order += ["cg0", "cg1"] + [f"P{s}" for s in streams]
    order += [f"rot{t}" for t in range(5)]
    order += [f"Y{s}{c}" for s in streams for c in range(2)] + [f"Z{s}{c}" for s in streams for c in range(2)]
    order += [f"f{s}{c}" for s in streams for c in range(2)] + [f"p{s}{c}" for s in streams for c in range(2)]
    order += ["dup0", "dup1"]
    n = len(attention_units(layer))
    for u in range(n + LAG + 1):
        if u < n:
            order.append(f"S{u}")
        if LAG <= u < n + LAG:
            order.append(f"T{u - LAG}")
        if u > LAG and (u - LAG - 1) % 4 == 3:
            order.append(f"V{(u - LAG - 1) // 4}")
    for i in BRANCH_ORDER:
        if i == 1:
            order.append("convnorm")
        for j in range(KD):
            order += [f"gate{i}{j}", f"branch{i}{j}"]
    return order + [f"out{j}" for j in range(KD)] + ["norm2"]


def last_use(layer, idx):
    if idx == BLOCK_KV:
        return "v"
    if idx == BLOCK_Q:
        return "q3"
    if idx == BLOCK_FC:
        return "ca1"
    if idx == BLOCK_GP:
        return f"P{1 - layer}"
    if idx < BLOCK_OUT:
        b, hf = divmod(idx - BLOCK_BRANCH, 2)
        return f"branch{BRANCH_ORDER[b]}{4 * hf + 3}"
    return f"out{4 * (idx - BLOCK_OUT) + 3}"


def build(nc, xT_in, consts_in, pool_in, vec_in, cond_in, router_in, mod_in, attn_in, ffn13_in, ffn2_in, moe_in, out):
    with ExitStack() as ctx:
        def sb(name, shape, dt=F32):
            return ctx.enter_context(nc.sbuf_tensor(name, shape, dt))

        sems = {}

        def S(name):
            if name not in sems:
                sems[name] = ctx.enter_context(nc.semaphore(name))
            return sems[name]

        xT = sb("xT", [P, KD, T])
        hT = sb("hT", [P, KD, T])
        const = sb("const", [P, CONST_LEN])
        vec = sb("vec", [P, DEPTH, VEC_LEN])
        cond = sb("cond", [P, 2 * KD])
        cs = sb("cs", [P, 2 * KD])
        router = sb("router", [P, KD, E])
        modT = sb("modT", [P, 48, 2])
        scale = sb("scale", [P, 2, KD, 2])
        sg = sb("sg", [P, 2, T])
        stat = sb("stat", [P, 4, 4])
        R = sb("R", [P, 16, 2, E])
        over_f = sb("over_f", [P, 1])
        over_i = sb("over_i", [1, 1], I32)

        W = sb("W", [P, MOE_UNROLL * CHUNK])
        slots = [W[:, s * SLOT_LEN:(s + 1) * SLOT_LEN] for s in range(RING)]
        at = RING * SLOT_LEN
        poolm = W[:, at:at + POOL_LEN].rearrange("p (c a t) -> p c a t", c=2, a=2)
        root = W[:, at + POOL_LEN:at + POOL_LEN + T]
        rstd = W[:, at + POOL_LEN + T:at + POOL_LEN + 2 * T]
        assert at + POOL_LEN + 2 * T <= MOE_UNROLL * CHUNK
        f13 = [W[:, s * 2048:(s + 1) * 2048].rearrange("p (m k f) -> p m k f", m=2, k=KD) for s in range(2)]
        f2 = W[:, 4096:6144].rearrange("p (s d) -> p s d", s=2)
        fsil = W[:, 6144:7168].rearrange("p (s t) -> p s t", s=2)
        fact = W[:, 7168:8192].rearrange("p (s t) -> p s t", s=2)
        chunk = [W[:, u * CHUNK:(u + 1) * CHUNK] for u in range(MOE_UNROLL)]

        B_LEN = 17408
        B = sb("B", [P, B_LEN])
        place = [0]

        def take(n):
            a = place[0]
            place[0] += n
            assert place[0] <= B_LEN, place[0]
            return B[:, a:a + n]

        merged = B[:, 0:KD * T].rearrange("p (k t) -> p k t", k=KD)
        hsq = B[:, 0:5 * T].rearrange("p (n t) -> p n t", n=5)
        Yf = B[:, 0:4 * T].rearrange("p (b t) -> p b t", b=4)
        Zp = B[:, 4 * T:4 * T + 4 * LAT].rearrange("p (b t) -> p b t", b=4)
        pT = take(KD * T).rearrange("p (b c j q) -> p b c j q", b=2, c=4, j=4)
        qk = take(5 * T).rearrange("p (n t) -> p n t", n=5)
        kdup = take(2 * T).rearrange("p (g t) -> p g t", g=2)
        vtok = take(4 * P).rearrange("p (c d) -> p c d", c=4)
        sq = take(2 * T).rearrange("p (b t) -> p b t", b=2)
        prob = take(3 * T).rearrange("p (b t) -> p b t", b=3)
        ypad = take(2 * 2 * PADT).rearrange("p (c s t) -> p c s t", c=2, s=2)
        conv = take(2 * T).rearrange("p (c t) -> p c t", c=2)
        fT = take(2 * T).rearrange("p (c t) -> p c t", c=2)
        plT = take(2 * T).rearrange("p (c t) -> p c t", c=2)
        attnT_flat = take(4 * T)
        attnT = attnT_flat.rearrange("p (c t) -> p c t", c=4)
        Xf = attnT_flat[:, 0:2 * T].rearrange("p (b c) -> p b c", c=256)
        Xp = attnT_flat[:, 2 * T:4 * T].rearrange("p (b c) -> p b c", c=256)
        mrow = prob[0:2, :, :]
        csq = prob[:, 0:2, :]
        place[0] = 0
        hg = take(KD * E * SLOTS).rearrange("p (k n) -> p k n", k=KD)
        Pm = take(2 * E * SLOTS).rearrange("p (t e s) -> p t e s", t=2, e=E)
        Pw = take(2 * E * SLOTS).rearrange("p (t e s) -> p t e s", t=2, e=E)
        PwT = take(E * LAT)
        htok = take(2 * D).rearrange("p (t d) -> p t d", t=2)
        ysum = take(D)
        msil = hT[:, 0, :].rearrange("p (b s) -> p b s", b=4)
        mact = hT[:, 1, :].rearrange("p (b s) -> p b s", b=4)

        banks = [ctx.enter_context(nc.psum_tensor(f"bank{b}", [P, 512], F32)) for b in range(8)]

        def C(name):
            a, b = CONST[name]
            return const[:, a:b]

        def V(layer, name):
            a, b = COLS[name]
            return vec[:, layer, a:b]

        seq = C("seq").rearrange("p (c t) -> p c t", c=2)

        use = {}
        for layer in range(DEPTH):
            for name in psum_order(layer):
                use[layer, name] = (len(use) % 8, len(use) // 8)
        uses_to = [len(psum_order(0)), len(use)]

        def filled(eng, layer, name):
            b, k = use[layer, name]
            eng.wait_ge(S(f"bank_full{b}"), k + 1)
            return banks[b]

        def free(layer, name):
            return S(f"bank_free{use[layer, name][0]}")

        def read(eng, layer, name):
            eng.wait_ge(free(layer, name), use[layer, name][1] + 1)

        class Next:

            def __init__(self, eng):
                self.eng, self.seen = eng, {}

            def __call__(self, name, n=1):
                self.seen[name] = self.seen.get(name, 0) + n
                self.eng.wait_ge(S(name), self.seen[name])

        def block_at(layer, idx):
            n = layer * (MOD_BLOCKS + N_BLOCKS) + MOD_BLOCKS + idx
            return n % RING, n // RING

        def mod_slot(layer, u):
            n = layer * (MOD_BLOCKS + N_BLOCKS) + u
            return n % RING, n // RING

        blk = ctx.enter_context(nc.Block())

        @blk.sync
        def _(sp):
            sp.dma_start(cond[:, :], cond_in).then_inc(S("cond_in"), 16)
            sp.dma_start(const[:, :], consts_in).then_inc(S("const_in"), 16)
            for layer in range(DEPTH):
                if layer:
                    sp.wait_ge(S("ffn_y_free"), 1 + KD * F_TILES // 2)

                def mod_load(i, u):
                    s, _ = mod_slot(layer, u)
                    sp.dma_start(slots[s][:, 0:KD * 512], mod_in[layer, i * RING + u]).then_inc(S(f"block_in{s}"), 16)

                for u in range(RING):
                    mod_load(0, u)
                if layer == 0:
                    sp.dma_start(vec[:, :, :], vec_in).then_inc(S("vec_in"), 16)
                    sp.dma_start(xT[:, :, :], xT_in).then_inc(S("x_in"), 16)
                    sp.dma_start(router[:, :, :], router_in).then_inc(S("router_in"), 16)
                sp.dma_start(poolm, pool_in.rearrange("p (c a t) -> p c a t", c=2, a=2)).then_inc(S("poolm_in"), 16)
                with sp.Fori(1, MOD_BLOCKS // RING) as i:
                    for u in range(RING):
                        sp.wait_ge(S("mod_row_full"), i * RING + (layer * MOD_BLOCKS + u + 1 - RING))
                        mod_load(i, u)
                for idx in range(N_BLOCKS):
                    s, _ = block_at(layer, idx)
                    n = BLOCK_LEN[idx]
                    if idx < RING:
                        sp.wait_ge(S("mod_row_full"), (layer + 1) * MOD_BLOCKS - RING + idx + 1)
                    else:
                        filled(sp, layer, last_use(layer, idx - RING))
                    sp.dma_start(slots[s][:, 0:n], attn_in[layer, idx, :, 0:n]).then_inc(S(f"block_in{s}"), 16)
                filled(sp, layer, last_use(layer, N_BLOCKS - 1))
                if layer == 0:
                    for s in range(2):
                        sp.dma_start(f13[s], ffn13_in[0, s].rearrange("p (m k f) -> p m k f", m=2, k=KD)) \
                            .then_inc(S(f"ffn13_in{s}"), 16)
                    sp.dma_start(f2, ffn2_in[0].rearrange("p (s d) -> p s d", s=2)).then_inc(S("ffn2_in"), 16)
                    with sp.Fori(1, F_TILES // 2) as i:
                        for s in range(2):
                            sp.wait_ge(S("ffn_up3_full"), 2 * i + (s - 1))
                            sp.dma_start(f13[s], ffn13_in[i, s].rearrange("p (m k f) -> p m k f", m=2, k=KD)) \
                                .then_inc(S(f"ffn13_in{s}"), 16)
                        sp.wait_ge(S("ffn_y_full"), i * KD)
                        sp.dma_start(f2, ffn2_in[i].rearrange("p (s d) -> p s d", s=2)).then_inc(S("ffn2_in"), 16)
            sp.wait_ge(S("h_ready"), N_SHIFTS)

            for u in range(MOE_UNROLL):
                sp.dma_start(chunk[u], moe_in[0, u]).then_inc(S(f"chunk_in{u}"), 16)
            with sp.Fori(1, E * MOE_TURNS) as it:
                for u in range(MOE_UNROLL):
                    sp.wait_ge(S("moe_down_full"), it * MOE_UNROLL + (u + 1 - MOE_UNROLL))
                    sp.dma_start(chunk[u], moe_in[it, u]).then_inc(S(f"chunk_in{u}"), 16)
            sp.wait_ge(S("over_ready"), 1)
            over = sp.value_load(over_i[0:1, 0:1], min_val=0, max_val=LAT)
            sp.wait_ge(S("scatter_free"), 1 + 4 * E)
            with sp.If(over > SLOTS):
                with sp.Fori(0, E * MOE_TURNS) as it:
                    for u in range(MOE_UNROLL):
                        sp.wait_ge(S("moe_down_full"), it * MOE_UNROLL + ((E * MOE_TURNS - 1) * MOE_UNROLL + u + 1))
                        sp.dma_start(chunk[u], moe_in[it, u]).then_inc(S(f"chunk_in{u}"), 16)
                sp.wait_ge(S("scatter_free"), 1 + 8 * E)
            sp.dma_start(out, xT[:, :, 0:LAT]).then_inc(S("out_done"), 16)
            sp.wait_ge(S("out_done"), 16)

        @blk.tensor
        def _(pe):
            nxt = Next(pe)
            mm = pe.matmul

            def opened(layer, name):
                b, k = use[layer, name]
                if k:
                    pe.wait_ge(S(f"bank_free{b}"), k)
                return banks[b]

            def done(layer, name, ins):
                ins.then_inc(S(f"bank_full{use[layer, name][0]}"), 1)

            def block_ready(layer, idx, width=512):
                s, k = block_at(layer, idx)
                pe.wait_ge(S(f"block_in{s}"), 16 * (k + 1))
                return slots[s][:, 0:KD * width].rearrange("p (k n) -> p k n", k=KD)

            def modulation(layer):
                with pe.Fori(0, MOD_BLOCKS // RING) as i:
                    def row(u):
                        s, use0 = mod_slot(layer, u)
                        pe.wait_ge(S(f"block_in{s}"), i * 16 + 16 * (use0 + 1))
                        w = slots[s][:, 0:KD * 512].rearrange("p (k n) -> p k n", k=KD)
                        for k in range(KD):
                            last = mm(banks[u][0:2, :], cs[:, 2 * k:2 * k + 2], w[:, k, :], start=k == 0, stop=k == KD - 1)
                        last.then_inc(S("mod_row_full"), 1)

                    def columns(u):
                        pe.wait_ge(S("mod_row_copied"), i * RING + (layer * MOD_BLOCKS + u + 1))
                        for q in range(4):
                            last = mm(banks[3 + u][:, 2 * q:2 * q + 2], mrow[:, u, q * P:(q + 1) * P],
                                      C("ident")[0:2, 0:2], start=True, stop=True)
                        last.then_inc(S("mod_cols_full"), 1)

                    pe.wait_ge(S("mod_cols_read"), i * RING + (layer * MOD_BLOCKS + 1))
                    row(0)
                    row(1)
                    columns(0)
                    row(2)
                    columns(1)
                    columns(2)
                pe.wait_ge(S("mod_cols_read"), (layer + 1) * MOD_BLOCKS + 1)

            def sum_squares(layer, name, n):
                b = opened(layer, name)
                for k in range(KD):
                    nxt("square_ready")
                    last = mm(b[:, 0:n], C("ones"), sq[:, k % 2, 0:n], start=k == 0, stop=k == KD - 1)
                    if k < KD - 1:
                        last.then_inc(S("square_used"), 1)
                done(layer, name, last)

            def attention(layer):
                units = attention_units(layer)
                read(pe, layer, "v")
                read(pe, layer, "dup1")

                def scores(u):
                    s, g, qt, j = units[u]
                    h = 4 * g + j
                    half = slice(64 * (h % 2), 64 * (h % 2) + 64)
                    a, z = (0, T) if s == 0 else (LAT, T)
                    q0 = s * LAT + qt * P
                    b = opened(layer, f"S{u}")
                    done(layer, f"S{u}", mm(b[:, 0:z - a], qk[half, 1 + h // 2, q0:q0 + P], kdup[half, g, a:z],
                                            start=True, stop=True))

                def turned(u):
                    s = units[u][0]
                    nxt("prob_ready")
                    b = opened(layer, f"T{u}")
                    for c in range(4 - 2 * s):
                        last = pe.transpose(b[:, c * P:(c + 1) * P], prob[:, u % 3, c * P:(c + 1) * P], C("ident"))
                    done(layer, f"T{u}", last)

                def values(v):
                    s, g, qt, _ = units[4 * v]
                    for u in range(4 * v, 4 * v + 4):
                        read(pe, layer, f"T{u}")
                    b = opened(layer, f"V{v}")
                    n = 4 - 2 * s
                    for half in range(2):
                        for c in range(n):
                            last = mm(b[64 * half:64 * half + 64, 0:256], vtok[:, 2 * s + c, 64 * g:64 * g + 64],
                                      pT[:, v % 2, c, half::2, :], start=c == 0, stop=c == n - 1)
                    done(layer, f"V{v}", last)

                for u in range(len(units) + LAG + 1):
                    if u < len(units):
                        scores(u)
                    if LAG <= u < len(units) + LAG:
                        turned(u - LAG)
                    if u > LAG and (u - LAG - 1) % 4 == 3:
                        values((u - LAG - 1) // 4)

            def attention_half(layer):
                N = T if layer == 0 else LAT
                streams = range(2 - layer)
                last_stream = 1 - layer
                sum_squares(layer, "norm1", T)
                nxt("h_ready", 2 * KD)

                def channel_major(name, w, col, n=N):
                    b = opened(layer, name)
                    for k in range(KD):
                        last = mm(b[:, 0:n], w[:, k, col:col + P], hT[:, k, 0:n], start=k == 0, stop=k == KD - 1)
                    done(layer, name, last)

                def token_major(prefix, w, col):
                    for s in streams:
                        b = opened(layer, f"{prefix}{s}")
                        for c in range(2):
                            for k in range(KD):
                                last = mm(b[:, c * 256:(c + 1) * 256], hT[:, k, s * LAT + c * P:s * LAT + (c + 1) * P],
                                          w[:, k, col:col + 256], start=k == 0, stop=k == KD - 1)
                        done(layer, f"{prefix}{s}", last)

                w = block_ready(layer, BLOCK_KV, 256)
                channel_major("k", w, 0, T)
                b = opened(layer, "v")
                for c in range(4):
                    for k in range(KD):
                        last = mm(b[:, c * P:(c + 1) * P], hT[:, k, c * P:(c + 1) * P], w[:, k, P:2 * P],
                                  start=k == 0, stop=k == KD - 1)
                done(layer, "v", last)
                w = block_ready(layer, BLOCK_Q)
                for t in range(4):
                    channel_major(f"q{t}", w, t * P)
                w = block_ready(layer, BLOCK_FC)
                token_major("F", w, 0)
                channel_major("ca0", w, 256)
                channel_major("ca1", w, 384)
                for t in range(5):
                    n = T if t == 0 else N
                    nxt("head_square_ready")
                    b = opened(layer, f"heads{t}")
                    done(layer, f"heads{t}", mm(b[:, 0:n], C("heads"), hsq[:, t, 0:n], start=True, stop=True))
                w = block_ready(layer, BLOCK_GP)
                channel_major("cg0", w, 0)
                channel_major("cg1", w, P)
                token_major("P", w, 256)
                for t in range(5):
                    nxt("head_normed")
                    b = opened(layer, f"rot{t}")
                    done(layer, f"rot{t}", mm(b[:, 0:LAT], C("rot"), qk[:, t, 0:LAT], start=True, stop=True))
                read(pe, layer, f"F{last_stream}")
                for s in streams:
                    for c in range(2):
                        b = opened(layer, f"Y{s}{c}")
                        for t in range(2):
                            last = mm(b[:, :], Xf[:, 2 * s + t, c * P:(c + 1) * P], seq[:, t, :], start=t == 0, stop=t == 1)
                        done(layer, f"Y{s}{c}", last)
                read(pe, layer, f"P{last_stream}")
                pe.wait_ge(S("poolm_in"), 16 * (layer + 1))
                for s in streams:
                    for c in range(2):
                        b = opened(layer, f"Z{s}{c}")
                        for t in range(2):
                            last = mm(b[:, :], Xp[:, 2 * s + t, c * P:(c + 1) * P], poolm[:, c, t, :], start=t == 0, stop=t == 1)
                        done(layer, f"Z{s}{c}", last)
                for s in streams:
                    for c in range(2):
                        read(pe, layer, f"Y{s}{c}")
                        b = opened(layer, f"f{s}{c}")
                        mm(b[:, 0:LAT], C("chan_cos"), Yf[:, 2 * s + c, 0:LAT], start=True, stop=False)
                        done(layer, f"f{s}{c}", mm(b[:, 0:LAT], C("chan_sin"), Yf[:, 2 * s + c, LAT:2 * LAT],
                                                   start=False, stop=True))
                for s in streams:
                    for c in range(2):
                        read(pe, layer, f"Z{s}{c}")
                        b = opened(layer, f"p{s}{c}")
                        a = c * P
                        done(layer, f"p{s}{c}", mm(b[:, 0:LAT], V(layer, "pool_w")[:, a:a + P], Zp[:, 2 * s + c, :],
                                                   start=True, stop=True))
                nxt("roped")
                for g in range(NKV):
                    b = opened(layer, f"dup{g}")
                    done(layer, f"dup{g}", mm(b[:, :], C(f"dup{g}"), qk[:, 0, :], start=True, stop=True))
                attention(layer)

                for bi, i in enumerate(BRANCH_ORDER):
                    if i == 1:
                        b = opened(layer, "convnorm")
                        for c in range(2):
                            nxt("conv_square_ready")
                            last = mm(b[:, 0:N], C("ones"), csq[:, c, 0:N], start=c == 0, stop=c == 1)
                        done(layer, "convnorm", last)
                    src = (fT, conv, plT, attnT)[i]
                    for j in range(KD):
                        hf, jj = divmod(j, 4)
                        w = block_ready(layer, BLOCK_BRANCH + 2 * bi + hf)
                        s, _ = block_at(layer, BLOCK_BRANCH + 2 * bi + hf)
                        wb = slots[s][:, KD * 512:(KD + BRANCH_K[i]) * 512].rearrange("p (k n) -> p k n", n=512)
                        channel_major(f"gate{i}{j}", w, jj * P)
                        if j == 0:
                            if i == 0:
                                read(pe, layer, f"f{last_stream}1")
                            elif i == 2:
                                read(pe, layer, f"p{last_stream}1")
                            elif i == 3:
                                read(pe, layer, f"V{len(attention_units(layer)) // 4 - 1}")
                            else:
                                nxt("conv_ready", 2)
                        b = opened(layer, f"branch{i}{j}")
                        for k in range(BRANCH_K[i]):
                            last = mm(b[:, 0:N], wb[:, k, jj * P:(jj + 1) * P], src[:, k, 0:N],
                                      start=k == 0, stop=k == BRANCH_K[i] - 1)
                        done(layer, f"branch{i}{j}", last)
                nxt("merged_ready", KD)
                for j in range(KD):
                    hf, jj = divmod(j, 4)
                    w = block_ready(layer, BLOCK_OUT + hf)
                    b = opened(layer, f"out{j}")
                    for k in range(KD):
                        last = mm(b[:, 0:N], w[:, k, jj * P:(jj + 1) * P], merged[:, k, 0:N], start=k == 0, stop=k == KD - 1)
                    done(layer, f"out{j}", last)
                sum_squares(layer, "norm2", N)
                nxt("h_ready", KD * (2 - layer))
                for b in range(8):
                    pe.wait_ge(S(f"bank_free{b}"), len(range(b, uses_to[layer], 8)))

            pe.wait_ge(S("const_in"), 16)
            pe.wait_ge(S("cs_ready"), 1)
            modulation(0)
            pe.wait_ge(S("vec_in"), 16)
            attention_half(0)

            with pe.Fori(0, F_TILES // 2) as i:
                for s in range(2):
                    pe.wait_ge(S(f"ffn13_in{s}"), i * 16 + 16)
                    for m in range(2):
                        for k in range(KD):
                            last = mm(banks[2 * s + m][:, :], f13[s][:, m, k, :], hT[:, k, :], start=k == 0, stop=k == KD - 1)
                        last.then_inc(S(("ffn_up1_full", "ffn_up3_full")[m]), 1)
                pe.wait_ge(S("ffn2_in"), i * 16 + 16)
                pe.wait_ge(S("ffn_act_ready"), i * 2 + 2)
                pe.wait_ge(S("ffn_y_free"), i * KD + 1)
                for d in range(KD):
                    if d >= 4:
                        pe.wait_ge(S("ffn_y_free"), i * KD + (d - 2))
                    for s in range(2):
                        last = mm(banks[4 + d % 4][:, :], f2[:, s, d * P:(d + 1) * P], fact[:, s, :], start=s == 0, stop=s == 1)
                    last.then_inc(S("ffn_y_full"), 1)
            pe.wait_ge(S("ffn_y_free"), 1 + KD * F_TILES // 2)

            modulation(1)
            attention_half(1)

            pe.wait_ge(S("router_in"), 16)
            for t in range(2):
                for k in range(KD):
                    last = mm(banks[0][:, t * E:(t + 1) * E], hT[:, k, t * P:(t + 1) * P], router[:, k, :],
                              start=k == 0, stop=k == KD - 1)
            last.then_inc(S("logits_full"), 1)
            for t in range(2):
                for hf in range(2):
                    for kk in range(4):
                        last = pe.transpose(banks[1 + 2 * t + hf][:, kk * P:(kk + 1) * P],
                                            hT[:, 4 * hf + kk, t * P:(t + 1) * P], C("ident"))
                    last.then_inc(S("htok_full"), 1)
            pe.wait_ge(S("mask_ready"), 1)
            m = R[:, MASK]
            mm(banks[5][:, 0:E], C("below"), m[:, 0, :], start=True, stop=True)
            mm(banks[5][:, E:2 * E], C("ones"), m[:, 0, :], start=True, stop=False)
            mm(banks[5][:, E:2 * E], C("below"), m[:, 1, :], start=False, stop=True)
            mm(banks[5][:, 2 * E:3 * E], C("ones"), m[:, 0, :], start=True, stop=False)
            mm(banks[5][:, 2 * E:3 * E], C("ones"), m[:, 1, :], start=False, stop=True).then_inc(S("rank_full"), 1)

            def experts(n):
                turn0 = n * E * MOE_TURNS
                pe.wait_ge(S("select_ready"), n + 1)
                if n == 0:
                    pe.wait_ge(S("htok_ready"), 4)
                for r in range(2 * KD + 4):
                    if r >= 6:
                        pe.wait_ge(S("gather_read"), n * 20 + r - 5)
                    if r < 2 * KD:
                        k, hf = divmod(r, 2)
                        for t in range(2):
                            last = mm(banks[r % 6][:, :], htok[:, t, k * P:(k + 1) * P], Pm[:, t, 4 * hf:4 * hf + 4, :],
                                      start=t == 0, stop=t == 1)
                    else:
                        for i in range(4):
                            e, t = divmod(4 * (r - 2 * KD) + i, 2)
                            last = pe.transpose(banks[r % 6][:, i * P:(i + 1) * P], Pw[:, t, e, :], C("ident"))
                    last.then_inc(S("gather_full"), 1)
                pe.wait_ge(S("gather_read"), n * 20 + 20)

                with pe.Fori(0, E) as e:
                    def up(u, turn):
                        pe.wait_ge(S(f"chunk_in{u}"), turn * 16 + 16)
                        for m in range(2):
                            w = chunk[u][:, m * D:(m + 1) * D].rearrange("p (k f) -> p k f", k=KD)
                            for k in range(KD):
                                last = mm(banks[u % 4][:, m * SLOTS:(m + 1) * SLOTS], w[:, k, :],
                                          hg[:, k, bass.ds(e * SLOTS, SLOTS)], start=k == 0, stop=k == KD - 1)
                        last.then_inc(S("moe_up_full"), 1)

                    def down(u, turn):
                        pe.wait_ge(S("moe_act_ready"), turn * MOE_UNROLL + (u + 1))
                        if u == 0:
                            pe.wait_ge(S("moe_sums_read"), turn + 1)
                        for hf in range(2):
                            a = 2 * D + hf * 512
                            last = mm(banks[4 + hf][:, :], mact[:, u % 4, :], chunk[u][:, a:a + 512],
                                      start=u == 0, stop=u == MOE_UNROLL - 1, skip_group_check=True)
                        last.then_inc(S("moe_down_full"), 1)

                    up(0, e * MOE_TURNS + turn0)
                    with pe.Fori(0, MOE_TURNS - 1) as q:
                        turn = e * MOE_TURNS + q + turn0
                        for u in range(MOE_UNROLL - 1):
                            up(u + 1, turn)
                            down(u, turn)
                        up(0, turn + 1)
                        down(MOE_UNROLL - 1, turn)
                    turn = e * MOE_TURNS + (turn0 + MOE_TURNS - 1)
                    for u in range(MOE_UNROLL - 1):
                        up(u + 1, turn)
                        down(u, turn)
                    down(MOE_UNROLL - 1, turn)
                    pe.wait_ge(S("moe_sums_read"), turn + 2)
                    for q in range(4):
                        pe.wait_ge(S("scatter_free"), e * 4 + (n * 4 * E + 1 + max(0, q - 1)))
                        for i in range(2):
                            k = 2 * q + i
                            last = mm(banks[6 + q % 2][:, i * LAT:(i + 1) * LAT], ysum[:, k * P:(k + 1) * P],
                                      PwT[:, bass.ds(e * LAT, LAT)], start=True, stop=True)
                        last.then_inc(S("scatter_full"), 1)

            experts(0)
            pe.wait_ge(S("over_ready"), 1)
            over = pe.value_load(over_i[0:1, 0:1], min_val=0, max_val=LAT)
            with pe.If(over > SLOTS):
                experts(1)

        @blk.scalar
        def _(act):
            nxt = Next(act)
            fn = nc.scalar.activation
            act.wait_ge(S("cond_in"), 16)
            fn(cs[:, :], cond[:, :], ACT.Silu).then_inc(S("cs_ready"), 1)
            act.wait_ge(S("const_in"), 16)

            def modulation(layer):
                with act.Fori(0, MOD_BLOCKS // RING) as i:
                    for u in range(RING):
                        act.wait_ge(S("mod_row_full"), i * RING + (layer * MOD_BLOCKS + u + 1))
                        fn(mrow[:, u, :], banks[u][0:2, :], ACT.Copy).then_inc(S("mod_row_copied"), 1)

            def norm(layer, name, n):
                for k in range(KD):
                    if name == "norm2":
                        read(act, layer, f"out{k}")
                    if k >= 2:
                        nxt("square_used")
                    fn(sq[:, k % 2, 0:n], xT[:, k, 0:n], ACT.Square).then_inc(S("square_ready"), 1)
                nxt("square_used")
                b = filled(act, layer, name)
                fn(root[:, 0:n], b[:, 0:n], ACT.Sqrt, bias=C("eps"), scale=1.0 / D).then_inc(free(layer, name), 1)
                shift = 0 if name == "norm1" else 3 * KD
                for s in range(n // LAT):
                    for k in range(KD):
                        nxt("h_scaled")
                        fn(hT[:, k, s * LAT:(s + 1) * LAT], hT[:, k, s * LAT:(s + 1) * LAT], ACT.Identity,
                           bias=modT[:, shift + k, s:s + 1]).then_inc(S("h_ready"), 1)

            def attention_half(layer):
                N = T if layer == 0 else LAT
                norm(layer, "norm1", T)
                for t in range(5):
                    n = T if t == 0 else N
                    name = "k" if t == 0 else f"q{t - 1}"
                    b = filled(act, layer, name)
                    fn(hsq[:, t, 0:n], b[:, 0:n], ACT.Square).then_inc(S("head_square_ready"), 1)
                    fn(qk[:, t, 0:n], b[:, 0:n], ACT.Copy).then_inc(free(layer, name), 1)
                for t in range(5):
                    n = T if t == 0 else N
                    b = filled(act, layer, f"heads{t}")
                    fn(hsq[:, t, 0:n], b[:, 0:n], ACT.Sqrt, bias=C("eps"), scale=1.0 / HD) \
                        .then_inc(free(layer, f"heads{t}"), 1)
                for c in range(2):
                    b = filled(act, layer, f"cg{c}")
                    fn(sg[:, c, 0:N], b[:, 0:N], ACT.Sigmoid).then_inc(free(layer, f"cg{c}"), 1)

                units = attention_units(layer)

                def keep_turned(u):
                    s, g, qt, j = units[u]
                    n = 4 - 2 * s
                    v = u // 4
                    if j == 0 and v >= 2:
                        filled(act, layer, f"V{v - 2}")
                    b = filled(act, layer, f"T{u}")
                    fn(pT[:, v % 2, 0:n, j, :], b[:, 0:n * P].rearrange("p (c q) -> p c q", q=P), ACT.Copy) \
                        .then_inc(free(layer, f"T{u}"), 1)

                for u in range(len(units) + LAG):
                    if u >= LAG:
                        keep_turned(u - LAG)
                    if u < len(units):
                        n = T if units[u][0] == 0 else CTX
                        nxt("negmax_ready")
                        b = filled(act, layer, f"S{u}")
                        fn(prob[:, u % 3, 0:n], b[:, 0:n], ACT.Exp, bias=stat[:, u % 4, 0:1], scale=HD ** -0.5,
                           accum_out=stat[:, u % 4, 1:2]).then_inc(free(layer, f"S{u}"), 1)

                step = 0
                for i in BRANCH_ORDER:
                    if i == 1:
                        act.wait_ge(S("conv_summed"), layer + 1)
                        for c in range(2):
                            fn(csq[:, c, 0:N], conv[:, c, 0:N], ACT.Square).then_inc(S("conv_square_ready"), 1)
                        b = filled(act, layer, "convnorm")
                        fn(root[:, 0:N], b[:, 0:N], ACT.Sqrt, bias=C("eps"), scale=1.0 / 256) \
                            .then_inc(free(layer, "convnorm"), 1)
                        for c in range(2):
                            nxt("conv_normed")
                            fn(conv[:, c, 0:N], conv[:, c, 0:N], ACT.Silu).then_inc(S("conv_ready"), 1)
                    for j in range(KD):
                        if step == 0:
                            act.wait_ge(S("conv_gated"), 2 * layer + 2)
                        if step >= 2:
                            pi, pj = BRANCH_ORDER[(step - 2) // KD], (step - 2) % KD
                            read(act, layer, f"branch{pi}{pj}")
                        b = filled(act, layer, f"gate{i}{j}")
                        fn(sg[:, step % 2, 0:N], b[:, 0:N], ACT.Sigmoid).then_inc(free(layer, f"gate{i}{j}"), 1)
                        step += 1
                norm(layer, "norm2", N)

            modulation(0)
            act.wait_ge(S("x_in"), 16)
            attention_half(0)
            with act.Fori(0, F_TILES // 2) as i:
                for s in range(2):
                    act.wait_ge(S("ffn_up1_full"), i * 2 + (s + 1))
                    fn(fsil[:, s, :], banks[2 * s][:, :], ACT.Silu).then_inc(S("ffn_silu_ready"), 1)
            modulation(1)
            act.wait_ge(S("ffn_y_free"), 1 + KD * F_TILES // 2)
            attention_half(1)

            for r in range(4):
                act.wait_ge(S("htok_full"), r + 1)
                t, hf = divmod(r, 2)
                fn(htok[:, t, hf * 512:(hf + 1) * 512], banks[1 + r][:, :], ACT.Copy).then_inc(S("htok_ready"), 1)
            act.wait_ge(S("gap_ready"), 1)
            fn(R[:, ODDS, 0, 0:2], R[:, GAP, 0, 0:2], ACT.Exp).then_inc(S("odds_ready"), 1)

            def experts(n):
                for r in range(2 * KD + 4):
                    act.wait_ge(S("gather_full"), n * 20 + r + 1)
                    if r < 2 * KD:
                        k, hf = divmod(r, 2)
                        dst = hg[:, k, hf * 512:(hf + 1) * 512]
                    else:
                        dst = PwT[:, (r - 2 * KD) * 512:(r - 2 * KD + 1) * 512]
                    fn(dst, banks[r % 6][:, :], ACT.Copy).then_inc(S("gather_read"), 1)
                with act.Fori(0, E * MOE_TURNS) as it:
                    for u in range(MOE_UNROLL):
                        act.wait_ge(S("moe_up_full"), it * MOE_UNROLL + (n * E * FE_TILES + u + 1))
                        fn(msil[:, u % 4, :], banks[u % 4][:, 0:SLOTS], ACT.Silu).then_inc(S("moe_silu_ready"), 1)

            experts(0)
            act.wait_ge(S("over_ready"), 1)
            over = act.value_load(over_i[0:1, 0:1], min_val=0, max_val=LAT)
            with act.If(over > SLOTS):
                experts(1)

        @blk.vector
        def _(dve):
            nxt = Next(dve)
            own = [0]
            tt, ts, stt = dve.tensor_tensor, dve.tensor_scalar, dve.scalar_tensor_tensor

            def step(ins, lag=0):
                own[0] += 1
                ins.then_inc(S("dve_own"), 1)
                if own[0] > lag:
                    dve.wait_ge(S("dve_own"), own[0] - lag)

            for name in ("mod_cols_read", "ffn_y_free", "moe_sums_read", "scatter_free"):
                dve.sem_inc(S(name), 1)
            step(dve.memset(ypad[:, :, :, :], 0.0))

            def modulation(layer):
                with dve.Fori(0, MOD_BLOCKS // RING) as i:
                    for u in range(RING):
                        dve.wait_ge(S("mod_cols_full"), i * RING + (layer * MOD_BLOCKS + u + 1))
                        a = i * 12 + 4 * u
                        bias = vec[:, layer, bass.ds(a, 4)].unsqueeze(2).broadcast_to([P, 4, 2])
                        tt(modT[:, bass.ds(a, 4), :], banks[3 + u][:, 0:8].rearrange("p (q v) -> p q v", v=2), bias, ALU.add) \
                            .then_inc(S("mod_cols_read"), 1)
                dve.wait_ge(S("mod_cols_read"), (layer + 1) * MOD_BLOCKS + 1)
                for n, name in enumerate(("norm1", "norm2")):
                    gain = V(layer, name).unsqueeze(2).broadcast_to([P, KD, 2])
                    a = (1 + 3 * n) * KD
                    step(stt(out=scale[:, n], in0=modT[:, a:a + KD, :], scalar=1.0, in1=gain, op0=ALU.add, op1=ALU.mult))

            def norm(layer, name, n):
                read(dve, layer, name)
                step(dve.reciprocal(rstd[:, 0:n], root[:, 0:n]))
                for s in range(n // LAT):
                    for k in range(KD):
                        stt(out=hT[:, k, s * LAT:(s + 1) * LAT], in0=xT[:, k, s * LAT:(s + 1) * LAT],
                            scalar=scale[:, int(name == "norm2"), k, s:s + 1], in1=rstd[:, s * LAT:(s + 1) * LAT],
                            op0=ALU.mult, op1=ALU.mult).then_inc(S("h_scaled"), 1)

            def attention_half(layer):
                N = T if layer == 0 else LAT
                ns = 2 - layer
                units = attention_units(layer)
                norm(layer, "norm1", T)
                b = filled(dve, layer, "v")
                dve.tensor_copy(vtok, b[:, :].rearrange("p (c d) -> p c d", c=4)).then_inc(free(layer, "v"), 1)
                for s in range(ns):
                    b = filled(dve, layer, f"F{s}")
                    dve.tensor_copy(Xf[:, 2 * s:2 * s + 2, :], b[:, :].rearrange("p (c d) -> p c d", c=2)) \
                        .then_inc(free(layer, f"F{s}"), 1)
                for c in range(2):
                    b = filled(dve, layer, f"ca{c}")
                    dve.tensor_copy(ypad[:, c, 0:ns, HALO:HALO + LAT], b[:, 0:N].rearrange("p (s t) -> p s t", t=LAT)) \
                        .then_inc(free(layer, f"ca{c}"), 1)
                for t in range(5):
                    n = T if t == 0 else N
                    read(dve, layer, f"heads{t}")
                    step(dve.reciprocal(hsq[:, t, 0:n], hsq[:, t, 0:n]))
                    stt(out=qk[:, t, 0:n], in0=qk[:, t, 0:n], scalar=V(layer, "k_g" if t == 0 else "q_g"),
                        in1=hsq[:, t, 0:n], op0=ALU.mult, op1=ALU.mult).then_inc(S("head_normed"), 1)
                for c in range(2):
                    read(dve, layer, f"ca{c}")
                    read(dve, layer, f"cg{c}")
                    y = ypad[:, c, 0:ns, HALO:HALO + LAT]
                    tt(y, y, sg[:, c, 0:N].rearrange("p (s t) -> p s t", t=LAT), ALU.mult).then_inc(S("conv_gated"), 1)
                for s in range(ns):
                    b = filled(dve, layer, f"P{s}")
                    dve.tensor_copy(Xp[:, 2 * s:2 * s + 2, :], b[:, :].rearrange("p (c d) -> p c d", c=2)) \
                        .then_inc(free(layer, f"P{s}"), 1)
                dve.wait_ge(S("head_normed"), 5 * layer + 5)
                cos = C("cos").unsqueeze(1).broadcast_to([P, 5, LAT])
                step(tt(hsq[:, :, 0:LAT], qk[:, :, 0:LAT], cos, ALU.mult))
                for t in range(5):
                    b = filled(dve, layer, f"rot{t}")
                    tt(hsq[:, t, LAT:T], b[:, 0:LAT], C("sin"), ALU.mult).then_inc(free(layer, f"rot{t}"), 1)
                for t in range(5):
                    read(dve, layer, f"rot{t}")
                tt(qk[:, :, 0:LAT], hsq[:, :, 0:LAT], hsq[:, :, LAT:T], ALU.add).then_inc(S("roped"), 1)
                dve.wait_ge(S("roped"), layer + 1)
                for s in range(ns):
                    for c in range(2):
                        b = filled(dve, layer, f"Y{s}{c}")
                        dve.tensor_copy(Yf[:, 2 * s + c, :], b[:, :]).then_inc(free(layer, f"Y{s}{c}"), 1)
                for s in range(ns):
                    for c in range(2):
                        b = filled(dve, layer, f"Z{s}{c}")
                        dve.tensor_copy(Zp[0:64, 2 * s + c, :], b[0:64, 0:LAT])
                        dve.tensor_copy(Zp[64:P, 2 * s + c, :], b[64:P, LAT:2 * LAT]).then_inc(free(layer, f"Z{s}{c}"), 1)
                for s in range(ns):
                    for c in range(2):
                        b = filled(dve, layer, f"f{s}{c}")
                        dve.tensor_copy(fT[:, c, s * LAT:(s + 1) * LAT], b[:, 0:LAT]).then_inc(free(layer, f"f{s}{c}"), 1)
                for s in range(ns):
                    for c in range(2):
                        b = filled(dve, layer, f"p{s}{c}")
                        ts(plT[:, c, s * LAT:(s + 1) * LAT], b[:, 0:LAT], V(layer, "pool_scale")[:, c:c + 1], None, ALU.mult) \
                            .then_inc(free(layer, f"p{s}{c}"), 1)
                for g in range(NKV):
                    b = filled(dve, layer, f"dup{g}")
                    dve.tensor_copy(kdup[:, g, :], b[:, :]).then_inc(free(layer, f"dup{g}"), 1)

                def maximum(u):
                    n = T if units[u][0] == 0 else CTX
                    b = filled(dve, layer, f"S{u}")
                    step(dve.tensor_reduce(stat[:, u % 4, 3:4], b[:, 0:n], AX, ALU.max))
                    ts(stat[:, u % 4, 0:1], stat[:, u % 4, 3:4], -HD ** -0.5, None, ALU.mult).then_inc(S("negmax_ready"), 1)

                def normalise(u):
                    n = T if units[u][0] == 0 else CTX
                    read(dve, layer, f"S{u}")
                    step(dve.reciprocal(stat[:, u % 4, 2:3], stat[:, u % 4, 1:2]))
                    ts(prob[:, u % 3, 0:n], prob[:, u % 3, 0:n], stat[:, u % 4, 2:3], None, ALU.mult) \
                        .then_inc(S("prob_ready"), 1)

                def keep_values(v):
                    s, g, qt, _ = units[4 * v]
                    b = filled(dve, layer, f"V{v}")
                    q0 = s * LAT + qt * P
                    dve.tensor_copy(attnT[:, 2 * g:2 * g + 2, q0:q0 + P], b[:, 0:256].rearrange("p (c q) -> p c q", q=P)) \
                        .then_inc(free(layer, f"V{v}"), 1)

                for u in range(len(units) + LAG + 2):
                    if u < len(units):
                        maximum(u)
                    if 1 <= u <= len(units):
                        normalise(u - 1)
                    if u > LAG + 1 and (u - LAG - 2) % 4 == 3:
                        keep_values((u - LAG - 2) // 4)

                dve.wait_ge(S("conv_gated"), 2 * layer + 2)

                def tap(k, c):
                    src = ypad[:, c, 0:ns, k:k + LAT]
                    dst = conv[:, c, 0:N].rearrange("p (s t) -> p s t", t=LAT)
                    w = V(layer, "taps")[:, c * CONV_K + k:c * CONV_K + k + 1]
                    if k == 0:
                        step(ts(dst, src, w, V(layer, "conv_b")[:, c:c + 1], ALU.mult, ALU.add), lag=1)
                    else:
                        step(stt(out=dst, in0=src, scalar=w, in1=dst, op0=ALU.mult, op1=ALU.add), lag=1)

                taps = [(k, c) for k in range(CONV_K) for c in range(2)]
                for bi, i in enumerate(BRANCH_ORDER):
                    if i == 1:
                        read(dve, layer, "convnorm")
                        step(dve.reciprocal(rstd[:, 0:N], root[:, 0:N]))
                        for c in range(2):
                            stt(out=conv[:, c, 0:N], in0=conv[:, c, 0:N], scalar=V(layer, "conv_g")[:, c:c + 1],
                                in1=rstd[:, 0:N], op0=ALU.mult, op1=ALU.mult).then_inc(S("conv_normed"), 1)
                    for j in range(KD):
                        n = KD * bi + j
                        read(dve, layer, f"gate{i}{j}")
                        b = filled(dve, layer, f"branch{i}{j}")
                        if bi == 0:
                            tt(merged[:, j, 0:N], sg[:, n % 2, 0:N], b[:, 0:N], ALU.mult).then_inc(free(layer, f"branch{i}{j}"), 1)
                        else:
                            tt(sq[:, n % 2, 0:N], sg[:, n % 2, 0:N], b[:, 0:N], ALU.mult).then_inc(free(layer, f"branch{i}{j}"), 1)
                            read(dve, layer, f"branch{i}{j}")
                            add = tt(merged[:, j, 0:N], merged[:, j, 0:N], sq[:, n % 2, 0:N], ALU.add)
                            if bi == 3:
                                add.then_inc(S("merged_ready"), 1)
                            else:
                                step(add)
                        if taps:
                            for k, c in taps[:4]:
                                tap(k, c)
                            taps = taps[4:]
                            if not taps:
                                dve.wait_ge(S("dve_own"), own[0])
                                dve.sem_inc(S("conv_summed"), 1)
                for j in range(KD):
                    b = filled(dve, layer, f"out{j}")
                    for s in range(ns):
                        x = xT[:, j, s * LAT:(s + 1) * LAT]
                        last = stt(out=x, in0=b[:, s * LAT:(s + 1) * LAT], scalar=modT[:, 2 * KD + j, s:s + 1], in1=x,
                                   op0=ALU.mult, op1=ALU.add)
                    last.then_inc(free(layer, f"out{j}"), 1)
                norm(layer, "norm2", N)

            dve.wait_ge(S("vec_in"), 16)
            dve.wait_ge(S("const_in"), 16)
            modulation(0)
            dve.wait_ge(S("x_in"), 16)
            attention_half(0)
            with dve.Fori(0, F_TILES // 2) as i:
                for s in range(2):
                    dve.wait_ge(S("ffn_silu_ready"), i * 2 + (s + 1))
                    dve.wait_ge(S("ffn_up3_full"), i * 2 + (s + 1))
                    tt(fact[:, s, :], fsil[:, s, :], banks[2 * s + 1][:, :], ALU.mult).then_inc(S("ffn_act_ready"), 1)
                dve.wait_ge(S("ffn_y_free"), i * KD + 1)
                for d in range(KD):
                    dve.wait_ge(S("ffn_y_full"), i * KD + (d + 1))
                    for s in range(2):
                        x = xT[:, d, s * LAT:(s + 1) * LAT]
                        last = stt(out=x, in0=banks[4 + d % 4][:, s * LAT:(s + 1) * LAT], scalar=modT[:, 5 * KD + d, s:s + 1],
                                   in1=x, op0=ALU.mult, op1=ALU.add)
                    last.then_inc(S("ffn_y_free"), 1)
            dve.wait_ge(S("ffn_y_free"), 1 + KD * F_TILES // 2)
            modulation(1)
            attention_half(1)

            dve.wait_ge(S("logits_full"), 1)
            step(dve.tensor_copy(R[:, LOGITS], banks[0][:, 0:2 * E].rearrange("p (t e) -> p t e", t=2)))
            iota8 = C("iota8")
            top = R[:, TOP, 0]

            def choose(src, one, at):
                for t in range(2):
                    step(dve.tensor_reduce(top[:, at + t:at + t + 1], R[:, src, t], AX, ALU.max))
                    step(stt(out=R[:, EQUAL, t], in0=R[:, src, t], scalar=top[:, at + t:at + t + 1], in1=iota8,
                             op0=ALU.is_equal, op1=ALU.mult))
                    step(dve.tensor_reduce(top[:, 6 + t:7 + t], R[:, EQUAL, t], AX, ALU.max))
                    step(ts(R[:, one, t], R[:, EQUAL, t], top[:, 6 + t:7 + t], None, ALU.is_equal))

            choose(LOGITS, FIRST, 0)
            step(stt(out=R[:, REST], in0=R[:, FIRST], scalar=-3.0e38, in1=R[:, LOGITS], op0=ALU.mult, op1=ALU.add))
            choose(REST, SECOND, 2)
            tt(R[:, MASK], R[:, FIRST], R[:, SECOND], ALU.add).then_inc(S("mask_ready"), 1)
            dve.wait_ge(S("mask_ready"), 1)
            tt(R[:, GAP, 0, 0:2], top[:, 2:4], top[:, 0:2], ALU.subtract).then_inc(S("gap_ready"), 1)
            dve.wait_ge(S("odds_ready"), 1)
            odds, w = R[:, ODDS, 0, 0:2], R[:, WEIGHT, 0]
            step(ts(R[:, GAP, 0, 2:4], odds, 1.0, None, ALU.add))
            step(dve.reciprocal(w[:, 0:2], R[:, GAP, 0, 2:4]))
            step(tt(w[:, 2:4], w[:, 0:2], odds, ALU.mult))
            for t in range(2):
                step(ts(R[:, FIRST, t], R[:, FIRST, t], w[:, t:t + 1], None, ALU.mult))
                step(stt(out=R[:, COMB, t], in0=R[:, SECOND, t], scalar=w[:, 2 + t:3 + t], in1=R[:, FIRST, t],
                         op0=ALU.mult, op1=ALU.add))
            dve.wait_ge(S("rank_full"), 1)
            step(ts(R[:, EQUAL], R[:, MASK], -1.0, 1000.0, ALU.add, ALU.mult))
            step(tt(R[:, RANK], banks[5][:, 0:2 * E].rearrange("p (t e) -> p t e", t=2), R[:, MASK], ALU.mult))
            step(tt(R[:, RANK], R[:, RANK], R[:, EQUAL], ALU.add))
            step(dve.tensor_reduce(over_f[:, :], banks[5][:, 2 * E:3 * E], AX, ALU.max))
            dve.tensor_copy(over_i[:, :], over_f[0:1, :]).then_inc(S("over_ready"), 1)

            def experts(n):
                turn0 = n * E * MOE_TURNS
                if n:
                    step(ts(R[:, RANK], R[:, RANK], -float(SLOTS), None, ALU.add))
                for t in range(2):
                    for e in range(E):
                        rank = R[:, RANK, t, e:e + 1]
                        ts(Pm[:, t, e, :], C("iota"), rank, None, ALU.is_equal)
                        last = ts(Pw[:, t, e, :], C("iota"), rank, R[:, COMB, t, e:e + 1], ALU.is_equal, ALU.mult)
                last.then_inc(S("select_ready"), 1)
                dve.wait_ge(S("select_ready"), n + 1)
                with dve.Fori(0, E) as e:
                    def product(u, turn):
                        dve.wait_ge(S("moe_silu_ready"), turn * MOE_UNROLL + (u + 1))
                        tt(mact[:, u % 4, :], msil[:, u % 4, :], banks[u % 4][:, SLOTS:2 * SLOTS], ALU.mult) \
                            .then_inc(S("moe_act_ready"), 1)

                    def sums(turn, first):
                        dve.wait_ge(S("moe_down_full"), turn * MOE_UNROLL + MOE_UNROLL)
                        if not first:
                            dve.wait_ge(S("moe_sums_read"), turn + 1)
                        for hf in range(2):
                            y = ysum[:, hf * 512:(hf + 1) * 512]
                            if first:
                                last = dve.tensor_copy(y, banks[4 + hf][:, :])
                            else:
                                last = tt(y, y, banks[4 + hf][:, :], ALU.add)
                        last.then_inc(S("moe_sums_read"), 1)

                    turn = e * MOE_TURNS + turn0
                    for u in range(MOE_UNROLL):
                        product(u, turn)
                    product(0, turn + 1)
                    sums(turn, True)
                    with dve.Fori(1, MOE_TURNS - 1) as q:
                        turn = e * MOE_TURNS + q + turn0
                        for u in range(1, MOE_UNROLL):
                            product(u, turn)
                        product(0, turn + 1)
                        sums(turn, False)
                    turn = e * MOE_TURNS + (turn0 + MOE_TURNS - 1)
                    for u in range(1, MOE_UNROLL):
                        product(u, turn)
                    sums(turn, False)
                    dve.wait_ge(S("scatter_free"), e * 4 + (n * 4 * E + 1))
                    for q in range(4):
                        dve.wait_ge(S("scatter_full"), e * 4 + (n * 4 * E + q + 1))
                        for i in range(2):
                            k = 2 * q + i
                            x = xT[:, k, 0:LAT]
                            last = stt(out=x, in0=banks[6 + q % 2][:, i * LAT:(i + 1) * LAT],
                                       scalar=modT[:, 5 * KD + k, 0:1], in1=x, op0=ALU.mult, op1=ALU.add)
                        last.then_inc(S("scatter_free"), 1)

            experts(0)
            dve.wait_ge(S("over_ready"), 1)
            over = dve.value_load(over_i[0:1, 0:1], min_val=0, max_val=LAT)
            with dve.If(over > SLOTS):
                experts(1)


def constants():
    c = np.zeros((P, CONST_LEN), np.float64)

    def put(name, a):
        c[:a.shape[0], CONST[name][0]:CONST[name][1]] = a

    i = np.arange(P)
    put("ident", np.eye(P))
    put("ones", np.ones((P, P)))
    put("heads", (i[:, None] // HD == i[None, :] // HD).astype(float))
    rot = np.zeros((P, P))
    for out_c in range(P):
        rot[out_c + 16 if out_c % 32 < 16 else out_c - 16, out_c] = -1.0 if out_c % 32 < 16 else 1.0
    put("rot", rot)
    for g in range(NKV):
        d = np.zeros((P, P))
        d[HD * g + i % HD, i] = 1.0
        put(f"dup{g}", d)
    ch = np.outer(np.arange(64), np.arange(64)) * (2 * np.pi / 64)
    eye2 = np.eye(2)
    norm = 1.0 / np.sqrt(64.0 * LAT)
    put("chan_cos", np.kron(eye2, np.cos(ch)) * norm)
    put("chan_sin", -np.kron(eye2, np.sin(ch)) * norm)
    put("below", (i[:, None] < i[None, :]).astype(float))
    put("iota", np.tile(i[None, :], (P, 1)))
    put("iota8", np.tile(E - np.arange(E)[None, :], (P, 1)))
    put("eps", np.full((P, 1), EPS))
    t = np.outer(np.arange(LAT), np.arange(LAT)) % LAT * (2 * np.pi / LAT)
    s = np.concatenate([np.cos(t), np.sin(t)], axis=1).reshape(2, P, 512)
    put("seq", s.transpose(1, 0, 2).reshape(P, 1024))
    n_freq = HD // 4
    freqs = (10000.0 ** (-np.arange(n_freq) / n_freq)).astype(np.float32)
    tok = np.arange(LAT)
    where = np.where((i % HD < 32)[:, None], (tok // GRID_W)[None, :], (tok % GRID_W)[None, :])
    angle = where.astype(np.float32) * freqs[i % 16][:, None]
    put("cos", np.cos(angle.astype(np.float64)))
    put("sin", np.sin(angle.astype(np.float64)))
    m = np.zeros((2, 2, P, 2, LAT))
    for g, w in enumerate(WINDOWS):
        full = np.zeros((LAT, LAT))
        for o in range(LAT):
            lo, hi = max(o - w // 2, 0), min(o + w // 2, LAT)
            full[lo:hi, o] = 1.0 / (hi - lo)
            full[o, o] -= 1.0
        m[g // 2, :, :, g % 2, :] = full.reshape(2, P, LAT)
    pool = m.transpose(2, 0, 1, 3, 4).reshape(P, POOL_LEN)
    return c.astype(np.float32), pool.astype(np.float32)


def tiled(w, width):
    k, n = w.shape
    return w.reshape(k // P, P, n // width, width).transpose(2, 1, 0, 3).reshape(n // width, P, k // P * width)


def columns(v):
    return np.ascontiguousarray(v.reshape(-1, P).T)


def layout(a):
    a = {k: np.asarray(v) for k, v in a.items()}
    x = np.concatenate([a["x"][0], a["ctx"][0]], axis=0)
    vec = np.zeros((P, DEPTH, VEC_LEN), np.float32)
    attn = np.zeros((DEPTH, N_BLOCKS, P, SLOT_LEN), np.float32)
    for l in range(DEPTH):
        def put(name, v):
            vec[:, l, COLS[name][0]:COLS[name][1]] = v

        put("b_mod", columns(a["b_mod"][l]))
        put("norm1", columns(a["norm1_g"][l]))
        put("norm2", columns(a["norm2_g"][l]))
        put("conv_b", columns(a["conv_b"][l]))
        put("conv_g", columns(a["conv_norm_g"][l]))
        put("pool_scale", columns(a["pool_scale"][l]))
        put("q_g", np.tile(a["q_norm_g"][l], 2)[:, None])
        put("k_g", np.tile(a["k_norm_g"][l], 2)[:, None])
        put("taps", a["conv_dw"][l].T.reshape(2, P, CONV_K).transpose(1, 0, 2).reshape(P, -1))
        pw = np.zeros((P, 2, P), np.float32)
        for g in range(4):
            h = 64 * (g % 2)
            pw[h:h + 64, g // 2, h:h + 64] = a["pool_w"][l, g]
        put("pool_w", pw.reshape(P, -1))
        w = a["w_in"][l]
        off_q = 1024
        off_k, off_g = off_q + 512, off_q + 768
        attn[l, BLOCK_KV, :, 0:KD * 256] = tiled(w[:, off_k:off_g], 256)[0]
        attn[l, BLOCK_Q, :, 0:KD * 512] = tiled(w[:, off_q:off_k], 512)[0]
        attn[l, BLOCK_FC, :, 0:KD * 512] = tiled(w[:, 0:512], 512)[0]
        attn[l, BLOCK_GP, :, 0:KD * 512] = tiled(w[:, 512:1024], 512)[0]
        branch = [a["w_br_fourier"][l], a["w_br_conv"][l], a["w_br_pool"][l], a["w_br_attn"][l]]
        for b, i in enumerate(BRANCH_ORDER):
            gate = tiled(w[:, off_g + i * D:off_g + (i + 1) * D], 512)
            br = tiled(branch[i], 512)
            for hf in range(2):
                attn[l, BLOCK_BRANCH + 2 * b + hf, :, 0:KD * 512] = gate[hf]
                attn[l, BLOCK_BRANCH + 2 * b + hf, :, KD * 512:(KD + BRANCH_K[i]) * 512] = br[hf]
        attn[l, BLOCK_OUT:, :, 0:KD * 512] = tiled(a["w_out"][l], 512)
    consts, pool = constants()
    cond = np.stack([a["c"][0].reshape(KD, P), a["c_ctx"].reshape(KD, P)], axis=2)
    f1, f3, f2 = a["ffn_w1"][0], a["ffn_w3"][0], a["ffn_w2"][0]
    turns = F_TILES // 2
    ffn13 = np.stack([tiled(f1, P), tiled(f3, P)], axis=2).reshape(turns, 2, P, 2 * D)
    ffn2 = f2.reshape(turns, 2, P, D).transpose(0, 2, 1, 3).reshape(turns, P, 2 * D)
    moe = np.empty((E, FE_TILES, P, CHUNK), np.float32)
    for e in range(E):
        moe[e, :, :, 0:D] = tiled(a["moe_w1"][0, e], P)
        moe[e, :, :, D:2 * D] = tiled(a["moe_w3"][0, e], P)
        moe[e, :, :, 2 * D:] = a["moe_w2"][0, e].reshape(FE_TILES, P, D)
    return {
        "xT": np.ascontiguousarray(x.T.reshape(KD, P, T).transpose(1, 0, 2)),
        "consts": consts,
        "pool_windows": pool,
        "vectors": vec,
        "cond": np.ascontiguousarray(cond.transpose(1, 0, 2).reshape(P, 2 * KD)),
        "router": np.ascontiguousarray(a["moe_router"][0].reshape(KD, P, E).transpose(1, 0, 2)),
        "w_mod_blocks": np.stack([tiled(a["w_mod"][l], 512) for l in range(DEPTH)]),
        "attn_blocks": attn,
        "ffn13": ffn13,
        "ffn2": np.ascontiguousarray(ffn2),
        "moe": moe.reshape(E * MOE_TURNS, MOE_UNROLL, P, CHUNK),
    }


def kernel(**inputs):
    import concourse.bacc as bacc
    from concourse.bass_utils import run_bass_kernel_spmd

    arrays = layout(inputs)
    nc = bacc.Bacc("TRN2", target_bir_lowering=False, num_devices=1)
    args = [nc.dram_tensor(f"in_{name}", v.shape, mybir.dt.from_np(v.dtype), kind="ExternalInput").ap() for name, v in arrays.items()]
    out = nc.dram_tensor("outT", (P, KD, LAT), F32, kind="ExternalOutput").ap()
    build(nc, *args, out)
    got = run_bass_kernel_spmd(nc, [{f"in_{k}": v for k, v in arrays.items()}], core_ids=[0]).results[0]["outT"]
    return np.ascontiguousarray(got.transpose(2, 1, 0).reshape(1, LAT, D))
```

```python
from contextlib import ExitStack

import numpy as np

import concourse.bass as bass
from concourse import mybir

F32 = mybir.dt.float32
F32R = mybir.dt.float32r
I32 = mybir.dt.int32
ALU = mybir.AluOpType
ACT = mybir.ActivationFunctionType
AX = mybir.AxisListType.X

P = 128
DEPTH, D, LAT, CTX = 2, 1024, 256, 256
T = LAT + CTX
KD = D // P
GRID_W = 64
EPS = 1e-6
HD = 64
NH, NKV = 8, 2
CONV_K = 31
HALO = CONV_K // 2
PADT = LAT + 2 * HALO
WINDOWS = (2, 4, 8, 16)
F_TILES = 2816 // P
E, FE_TILES = 8, 3584 // P
SLOTS = P

BLOCK_KV, BLOCK_Q, BLOCK_FC, BLOCK_GP = range(4)
BRANCH_ORDER = (0, 2, 3, 1)
BRANCH_K = (2, 2, 2, 4)
BLOCK_BRANCH, BLOCK_OUT = 4, 12
N_BLOCKS = 14
BLOCK_LEN = [KD * 256] + [KD * 512] * 3 + [(KD + BRANCH_K[i]) * 512 for i in BRANCH_ORDER for _ in range(2)] \
    + [KD * 512] * 2
SLOT_LEN = max(BLOCK_LEN)
RING = 2
MOD_UNROLL = 4
TILE_RING = 3
MOD_BLOCKS = 6 * D // 512
MOE_UNROLL = 4
MOE_TURNS = FE_TILES // MOE_UNROLL
CHUNK = 3 * D
BEFORE = {"mod_cols_read": 1, "ffn_y_free": 1, "scatter_free": 1, "moe_up_full": 2, "moe_down_full": 4,
          "moe_split": 4, "sums_read": 1}

COLS = {}
_at = 0
for _name, _n in (("b_mod", 48), ("norm1", 8), ("norm2", 8), ("conv_b", 2), ("conv_g", 2), ("pool_scale", 2),
                  ("q_g", 1), ("k_g", 1), ("taps", 2 * CONV_K), ("pool_w", 2 * P)):
    COLS[_name] = (_at, _at + _n)
    _at += _n
VEC_LEN = _at
CONST = {}
_at = 0
for _name, _n in (("ident", P), ("ones", P), ("heads", P), ("rot", P), ("dup0", P), ("dup1", P), ("chan_cos", P),
                  ("chan_sin", P), ("below", P), ("iota", P), ("iota8", 8), ("eps", 1), ("seq", 2 * 512),
                  ("cos", LAT), ("sin", LAT)):
    CONST[_name] = (_at, _at + _n)
    _at += _n
CONST_LEN = _at
POOL_LEN = 2 * 2 * 512
LOGITS, EQUAL, FIRST, REST, SECOND, MASK, COMB, RANK, TOP, GAP, ODDS, WEIGHT = range(12)


LAG = 3


def attention_units(layer):
    return [(s, g, qt, j) for s in range(2 - layer) for g in range(NKV) for qt in range(2) for j in range(4)]


def psum_order(layer):
    streams = range(2 - layer)
    order = ["norm1", "k", "v"] + [f"q{t}" for t in range(4)]
    order += ["F0", "F1", "ca0", "ca1"]
    order += [f"heads{t}" for t in range(5)]
    order += ["cg0", "cg1", "P0", "P1", "vtok"]
    order += [f"rot{t}" for t in range(5)]
    order += [f"Y{s}{c}" for s in streams for c in range(2)] + [f"Z{s}{c}" for s in streams for c in range(2)]
    order += [f"f{s}{c}" for s in streams for c in range(2)] + [f"p{s}{c}" for s in streams for c in range(2)]
    order += ["dup0", "dup1"]
    n = len(attention_units(layer))
    for u in range(n + LAG + 1):
        if u < n:
            order.append(f"S{u}")
        if LAG <= u < n + LAG:
            order.append(f"T{u - LAG}")
        if u > LAG and (u - LAG - 1) % 4 == 3:
            order.append(f"V{(u - LAG - 1) // 4}")
    for i in BRANCH_ORDER:
        if i == 1:
            order.append("convnorm")
        for j in range(KD):
            order += [f"gate{i}{j}", f"branch{i}{j}"]
    return order + [f"out{j}" for j in range(KD)] + ["norm2"]


TILES = [("k", BLOCK_KV, 0), ("v", BLOCK_KV, 1)] + [(f"q{t}", BLOCK_Q, t) for t in range(4)] \
    + [("F0", BLOCK_FC, 0), ("F1", BLOCK_FC, 1), ("ca0", BLOCK_FC, 2), ("ca1", BLOCK_FC, 3)] \
    + [("cg0", BLOCK_GP, 0), ("cg1", BLOCK_GP, 1), ("P0", BLOCK_GP, 2), ("P1", BLOCK_GP, 3)] \
    + [(f"gate{i}{j}", BLOCK_BRANCH + 2 * b + j // 4, j % 4) for b, i in enumerate(BRANCH_ORDER) for j in range(KD)]
TILE_NO = {name: n for n, (name, _, _) in enumerate(TILES)}


def build(nc, xT_in, consts_in, pool_in, vec_in, cond_in, router_in, mod_in, attn_in, ffn13_in, ffn2_in, moe_in, out):
    with ExitStack() as ctx:
        def sb(name, shape, dt=F32):
            return ctx.enter_context(nc.sbuf_tensor(name, shape, dt))

        sems = {}

        def S(name):
            if name not in sems:
                sems[name] = ctx.enter_context(nc.semaphore(name))
            return sems[name]

        base = (nc.sbuf_base + 63) // 64 * 64
        room = (nc.sbuf_usable_end - base) // 4
        sb("arena", [P, room - 32])
        top = [0]

        def at(name, shape, off=None, dt=F32, parts=P):
            n = int(np.prod(shape))
            if off is None:
                off = top[0]
                top[0] += (n + 7) // 8 * 8
            assert off + n <= room - 32, (name, off + n, room)
            return nc.alloc_sbuf_tensor_at(name, [parts, *shape], dt, offset=base + 4 * off)

        xT = at("xT", [KD, T])
        const = at("const", [CONST_LEN])
        vec = at("vec", [DEPTH, VEC_LEN])
        cond = at("cond", [2 * KD])
        cs = at("cs", [2 * KD])
        router = at("router", [KD, E])
        modT = at("modT", [48, 2])
        scale = at("scale", [2, KD, 2])
        stat = at("stat", [4, 4])
        R = at("R", [16, 2, E])
        over_f = at("over_f", [1])
        over_i = at("over_i", [1], dt=I32, parts=1)
        sg = at("sg", [2, T])
        W = at("W", [MOE_UNROLL * CHUNK])
        slots = [W[:, s * SLOT_LEN:(s + 1) * SLOT_LEN] for s in range(RING)]
        poolm = slots[BLOCK_GP % RING][:, KD * 512:KD * 512 + POOL_LEN].rearrange("p (c a t) -> p c a t", c=2, a=2)
        f13 = [W[:, s * 2048:(s + 1) * 2048].rearrange("p (m k f) -> p m k f", m=2, k=KD) for s in range(2)]
        f2 = W[:, 4096:6144].rearrange("p (s d) -> p s d", s=2)
        chunk = [W[:, u * CHUNK:(u + 1) * CHUNK] for u in range(MOE_UNROLL)]
        root = at("root", [T])
        rstd = at("rstd", [T])

        shared = top[0]
        hh = at("h_high", [KD, T], dt=F32R)
        hl = at("h_low", [KD, T], dt=F32R)
        after_h = top[0]
        wh = at("tile_high", [TILE_RING, KD, P], dt=F32R)
        wl = at("tile_low", [TILE_RING, KD, P], dt=F32R)
        region = top[0]
        merged = at("merged", [KD, T])
        hsq = at("hsq", [5, T], region)
        Yf = at("Yf", [4, 2, 2 * P], region)
        Zp = at("Zp", [4, 2, P], region + 4 * T)
        pT = at("pT", [2, 4, 4, P], region)
        qk = at("qk", [5, T])
        csq = qk[:, 0:2, :]
        kdup_at = top[0]
        kdup = at("kdup", [NKV, T])
        conv = at("conv", [2, T], kdup_at)
        vtok = at("vtok", [4, P])
        prob_at = top[0]
        prob = at("prob", [3, T])
        sq = at("sq", [2, T], prob_at)
        vch = at("vch", [T], prob_at)
        ypad = at("ypad", [2, 2, PADT])
        fT = at("fT", [2, T])
        plT = at("plT", [2, T])
        attnT_at = top[0]
        attnT = at("attnT", [4, T])
        Xf = at("Xf", [2, T], attnT_at)
        Xp = at("Xp", [2, T], attnT_at + 2 * T)
        ht = at("ht", [4, LAT], attnT_at)
        mrow = at("mrow", [MOD_UNROLL, 512], attnT_at, parts=2)
        top[0] = after_h
        f13h = at("f13_high", [2, 2, KD, P], dt=F32R)
        f13l = at("f13_low", [2, 2, KD, P], dt=F32R)
        f2h = at("f2_high", [2, D], dt=F32R)
        f2l = at("f2_low", [2, D], dt=F32R)
        fsil = at("fsil", [2, T])
        fprod = at("fprod", [2, T])
        fah = at("fact_high", [2, T], dt=F32R)
        fal = at("fact_low", [2, T], dt=F32R)
        top[0] = shared
        Pm = at("Pm", [2, (E + 1) * SLOTS])
        PwT = at("PwT", [E * LAT])
        htok = at("htok", [2, D])
        ysum = at("ysum", [D])
        hgh = at("gathered_high", [KD, SLOTS], dt=F32R)
        hgl = at("gathered_low", [KD, SLOTS], dt=F32R)
        msil = at("msil", [2, SLOTS])
        mprod = at("mprod", [2, P])
        mah = at("mact_high", [2, SLOTS], dt=F32R)
        mal = at("mact_low", [2, SLOTS], dt=F32R)
        split_at = top[0]
        m13h = at("m13_high", [2, KD, 2 * P], dt=F32R)
        m13l = at("m13_low", [2, KD, 2 * P], dt=F32R)
        m2h = at("m2_high", [4, D], dt=F32R)
        m2l = at("m2_low", [4, D], dt=F32R)
        top[0] = split_at
        Pw = at("Pw", [2, E, SLOTS])
        hT = at("hT", [KD, LAT])

        banks = [ctx.enter_context(nc.psum_tensor(f"bank{b}", [P, 512], F32)) for b in range(8)]

        def C(name):
            a, b = CONST[name]
            return const[:, a:b]

        def V(layer, name):
            a, b = COLS[name]
            return vec[:, layer, a:b]

        seq = C("seq").rearrange("p (c t) -> p c t", c=2)

        use = {}
        for layer in range(DEPTH):
            for name in psum_order(layer):
                use[layer, name] = (len(use) % 8, len(use) // 8)
        uses_to = [len(psum_order(0)), len(use)]

        def filled(eng, layer, name):
            b, k = use[layer, name]
            eng.wait_ge(S(f"bank_full{b}"), k + 1)
            return banks[b]

        def free(layer, name):
            return S(f"bank_free{use[layer, name][0]}")

        def read(eng, layer, name):
            eng.wait_ge(free(layer, name), use[layer, name][1] + 1)

        class Next:

            def __init__(self, eng):
                self.eng, self.seen = eng, {}

            def __call__(self, name, n=1):
                self.seen[name] = self.seen.get(name, 0) + n
                self.eng.wait_ge(S(name), self.seen[name])

        def block_at(layer, idx):
            n = layer * (MOD_BLOCKS + N_BLOCKS) + MOD_BLOCKS + idx
            return n % RING, n // RING

        def raw_tile(idx, col):
            width = 256 if idx == BLOCK_KV else 512
            w = slots[idx % RING][:, 0:KD * width].rearrange("p (k n) -> p k n", k=KD)
            return w[:, :, col * P:(col + 1) * P]

        def mod_slot(layer, u):
            n = layer * (MOD_BLOCKS + N_BLOCKS) + u
            return n % RING, n // RING

        blk = ctx.enter_context(nc.Block())

        @blk.sync
        def _(sp):
            sp.dma_start(cond[:, :], cond_in).then_inc(S("cond_in"), 16)
            sp.dma_start(const[:, :], consts_in).then_inc(S("const_in"), 16)
            for layer in range(DEPTH):
                if layer:
                    sp.wait_ge(S("ffn_low_ready"), 3 * F_TILES // 2)

                def mod_load(i, u):
                    s, _ = mod_slot(layer, u)
                    sp.dma_start(slots[s][:, 0:KD * 512], mod_in[layer, i * MOD_UNROLL + u]).then_inc(S(f"block_in{s}"), 16)

                def mod_left(i, u):
                    sp.wait_ge(S("mod_row_full"), i * MOD_UNROLL + (layer * MOD_BLOCKS + u + 1 - RING))

                for u in range(MOD_UNROLL):
                    if u >= RING:
                        mod_left(0, u)
                    mod_load(0, u)
                    if layer == 0 and u == 1:
                        sp.dma_start(xT[:, :, :], xT_in).then_inc(S("x_in"), 16)
                        sp.dma_start(vec[:, :, :], vec_in).then_inc(S("vec_in"), 16)
                        sp.dma_start(router[:, :, :], router_in).then_inc(S("router_in"), 16)
                with sp.Fori(1, MOD_BLOCKS // MOD_UNROLL) as i:
                    for u in range(MOD_UNROLL):
                        mod_left(i, u)
                        mod_load(i, u)
                for idx in range(N_BLOCKS):
                    s, _ = block_at(layer, idx)
                    n = BLOCK_LEN[idx]
                    last = idx - RING
                    if last < 0:
                        sp.wait_ge(S("mod_row_full"), (layer + 1) * MOD_BLOCKS + last + 1)
                    elif last < BLOCK_GP:
                        tiles = [t for t, (_, b, _) in enumerate(TILES) if b == last]
                        sp.wait_ge(S("tile_low_ready"), layer * len(TILES) + tiles[-1] + 1)
                    elif last == BLOCK_GP:
                        filled(sp, layer, f"p{1 - layer}1")
                    elif last < BLOCK_OUT:
                        b, hf = divmod(last - BLOCK_BRANCH, 2)
                        filled(sp, layer, f"branch{BRANCH_ORDER[b]}{4 * hf + 3}")
                    sp.dma_start(slots[s][:, 0:n], attn_in[layer, idx, :, 0:n]).then_inc(S(f"block_in{s}"), 16)
                    if idx == BLOCK_GP:
                        sp.dma_start(poolm, pool_in.rearrange("p (c a t) -> p c a t", c=2, a=2)).then_inc(S("poolm_in"), 16)
                filled(sp, layer, "out7")
                if layer == 0:
                    for s in range(2):
                        sp.dma_start(f13[s], ffn13_in[0, s].rearrange("p (m k f) -> p m k f", m=2, k=KD)) \
                            .then_inc(S(f"ffn13_in{s}"), 16)
                    sp.dma_start(f2, ffn2_in[0].rearrange("p (s d) -> p s d", s=2)).then_inc(S("ffn2_in"), 16)
                    with sp.Fori(1, F_TILES // 2) as i:
                        for s in range(2):
                            sp.wait_ge(S("ffn_low_ready"), 3 * i + (s - 2))
                            sp.dma_start(f13[s], ffn13_in[i, s].rearrange("p (m k f) -> p m k f", m=2, k=KD)) \
                                .then_inc(S(f"ffn13_in{s}"), 16)
                        sp.wait_ge(S("ffn_low_ready"), 3 * i)
                        sp.dma_start(f2, ffn2_in[i].rearrange("p (s d) -> p s d", s=2)).then_inc(S("ffn2_in"), 16)

            def chunks(n):
                with sp.Fori(0, E * MOE_TURNS) as it:
                    for u in range(MOE_UNROLL):
                        m = it * MOE_UNROLL + (n * E * FE_TILES + u + 1)
                        slot = (u + 1) % MOE_UNROLL
                        sp.wait_ge(S("moe_split"), m + 1)
                        sp.dma_start(chunk[slot], moe_in[it * MOE_UNROLL + (u + 1)]).then_inc(S(f"chunk_in{slot}"), 16)

            sp.dma_start(chunk[0], moe_in[0]).then_inc(S("chunk_in0"), 16)
            chunks(0)
            sp.wait_ge(S("over_ready"), 1)
            over = sp.value_load(over_i[0:1, 0:1], min_val=0, max_val=LAT)
            sp.wait_ge(S("scatter_free"), 1 + 4 * E)
            with sp.If(over > SLOTS):
                chunks(1)
                sp.wait_ge(S("scatter_free"), 1 + 8 * E)
            sp.dma_start(out, xT[:, :, 0:LAT]).then_inc(S("out_done"), 16)
            sp.wait_ge(S("out_done"), 16)

        @blk.tensor
        def _(pe):
            nxt = Next(pe)
            mm = pe.matmul

            def opened(layer, name):
                b, k = use[layer, name]
                if k:
                    pe.wait_ge(S(f"bank_free{b}"), k)
                return banks[b]

            def done(layer, name, ins):
                ins.then_inc(S(f"bank_full{use[layer, name][0]}"), 1)

            def block_ready(layer, idx, width=512):
                s, k = block_at(layer, idx)
                pe.wait_ge(S(f"block_in{s}"), 16 * (k + 1))
                return slots[s][:, 0:KD * width].rearrange("p (k n) -> p k n", k=KD)

            def modulation(layer):
                with pe.Fori(0, MOD_BLOCKS // MOD_UNROLL) as i:
                    def row(u):
                        s, use0 = mod_slot(layer, u)
                        pe.wait_ge(S(f"block_in{s}"), i * (16 * MOD_UNROLL // RING) + 16 * (use0 + 1))
                        w = slots[s][:, 0:KD * 512].rearrange("p (k n) -> p k n", k=KD)
                        for k in range(KD):
                            last = mm(banks[u][0:2, :], cs[:, 2 * k:2 * k + 2], w[:, k, :], start=k == 0, stop=k == KD - 1)
                        last.then_inc(S("mod_row_full"), 1)

                    def turned(u):
                        pe.wait_ge(S("mod_row_copied"), i * MOD_UNROLL + (layer * MOD_BLOCKS + u + 1))
                        for q in range(4):
                            last = mm(banks[4 + u][:, 2 * q:2 * q + 2], mrow[:, u, q * P:(q + 1) * P],
                                      C("ident")[0:2, 0:2], start=True, stop=True)
                        last.then_inc(S("mod_cols_full"), 1)

                    pe.wait_ge(S("mod_cols_read"), i * MOD_UNROLL + (layer * MOD_BLOCKS + 1))
                    for u in range(MOD_UNROLL):
                        row(u)
                        if u:
                            turned(u - 1)
                    turned(MOD_UNROLL - 1)
                pe.wait_ge(S("mod_cols_read"), (layer + 1) * MOD_BLOCKS + 1)

            def sum_squares(layer, name, n):
                b = opened(layer, name)
                for k in range(KD):
                    nxt("square_ready")
                    last = mm(b[:, 0:n], C("ones"), sq[:, k % 2, 0:n], start=k == 0, stop=k == KD - 1)
                    if k < KD - 1:
                        last.then_inc(S("square_used"), 1)
                done(layer, name, last)

            def attention(layer):
                units = attention_units(layer)
                read(pe, layer, "vtok")
                read(pe, layer, "dup1")

                def scores(u):
                    s, g, qt, j = units[u]
                    h = 4 * g + j
                    half = slice(64 * (h % 2), 64 * (h % 2) + 64)
                    a, z = (0, T) if s == 0 else (LAT, T)
                    q0 = s * LAT + qt * P
                    b = opened(layer, f"S{u}")
                    done(layer, f"S{u}", mm(b[:, 0:z - a], qk[half, 1 + h // 2, q0:q0 + P], kdup[half, g, a:z],
                                            start=True, stop=True))

                def turned(u):
                    s = units[u][0]
                    nxt("prob_ready")
                    b = opened(layer, f"T{u}")
                    for c in range(4 - 2 * s):
                        last = pe.transpose(b[:, c * P:(c + 1) * P], prob[:, u % 3, c * P:(c + 1) * P], C("ident"))
                    done(layer, f"T{u}", last)

                def values(v):
                    s, g, qt, _ = units[4 * v]
                    for u in range(4 * v, 4 * v + 4):
                        read(pe, layer, f"T{u}")
                    b = opened(layer, f"V{v}")
                    n = 4 - 2 * s
                    for half in range(2):
                        for c in range(n):
                            last = mm(b[64 * half:64 * half + 64, 0:256], vtok[:, 2 * s + c, 64 * g:64 * g + 64],
                                      pT[:, v % 2, c, half::2, :], start=c == 0, stop=c == n - 1)
                    done(layer, f"V{v}", last)

                for u in range(len(units) + LAG + 1):
                    if u < len(units):
                        scores(u)
                    if LAG <= u < len(units) + LAG:
                        turned(u - LAG)
                    if u > LAG and (u - LAG - 1) % 4 == 3:
                        values((u - LAG - 1) // 4)

            def attention_half(layer):
                N = T if layer == 0 else LAT
                streams = range(2 - layer)
                last_stream = 1 - layer
                sum_squares(layer, "norm1", T)
                nxt("h_ready", 2 * KD)

                def project(name, n=N):
                    t = layer * len(TILES) + TILE_NO[name]
                    r = t % TILE_RING
                    pe.wait_ge(S("tile_low_ready"), t + 1)
                    b = opened(layer, name)
                    for k in range(KD):
                        mm(b[:, 0:n], wh[:, r, k, :], hh[:, k, 0:n], start=k == 0, stop=False)
                        mm(b[:, 0:n], wh[:, r, k, :], hl[:, k, 0:n], start=False, stop=False)
                        last = mm(b[:, 0:n], wl[:, r, k, :], hh[:, k, 0:n], start=False, stop=k == KD - 1)
                    done(layer, name, last)

                project("k", T)
                project("v", T)
                for name in ("q0", "q1", "q2", "q3", "F0", "F1", "ca0", "ca1"):
                    project(name)
                for t in range(5):
                    n = T if t == 0 else N
                    nxt("head_square_ready")
                    b = opened(layer, f"heads{t}")
                    done(layer, f"heads{t}", mm(b[:, 0:n], C("heads"), hsq[:, t, 0:n], start=True, stop=True))
                for name in ("cg0", "cg1", "P0", "P1"):
                    project(name)
                read(pe, layer, "v")
                b = opened(layer, "vtok")
                for c in range(4):
                    last = pe.transpose(b[:, c * P:(c + 1) * P], vch[:, c * P:(c + 1) * P], C("ident"))
                done(layer, "vtok", last)
                for t in range(5):
                    nxt("head_normed")
                    b = opened(layer, f"rot{t}")
                    done(layer, f"rot{t}", mm(b[:, 0:LAT], C("rot"), qk[:, t, 0:LAT], start=True, stop=True))
                both = const[:, CONST["chan_cos"][0]:CONST["chan_sin"][1]]
                for s in streams:
                    for c in range(2):
                        read(pe, layer, f"F{c}")
                        b = opened(layer, f"Y{s}{c}")
                        for t in range(2):
                            a = s * LAT + t * P
                            last = mm(b[:, t * 256:(t + 1) * 256], Xf[:, c, a:a + P], both, start=True, stop=True)
                        done(layer, f"Y{s}{c}", last)
                for s in streams:
                    for c in range(2):
                        read(pe, layer, f"P{c}")
                        b = opened(layer, f"Z{s}{c}")
                        for t in range(2):
                            a = s * LAT + t * P
                            last = mm(b[:, t * P:(t + 1) * P], Xp[:, c, a:a + P], V(layer, "pool_w")[:, c * P:(c + 1) * P],
                                      start=True, stop=True)
                        done(layer, f"Z{s}{c}", last)
                for s in streams:
                    for c in range(2):
                        read(pe, layer, f"Y{s}{c}")
                        b = opened(layer, f"f{s}{c}")
                        for t in range(2):
                            mm(b[:, 0:LAT], Yf[:, 2 * s + c, t, 0:P], seq[:, t, 0:LAT], start=t == 0, stop=False)
                            last = mm(b[:, 0:LAT], Yf[:, 2 * s + c, t, P:2 * P], seq[:, t, LAT:2 * LAT],
                                      start=False, stop=t == 1)
                        done(layer, f"f{s}{c}", last)
                pe.wait_ge(S("poolm_in"), 16 * (layer + 1))
                for s in streams:
                    for c in range(2):
                        read(pe, layer, f"Z{s}{c}")
                        b = opened(layer, f"p{s}{c}")
                        for t in range(2):
                            last = mm(b[:, :], Zp[:, 2 * s + c, t, :], poolm[:, c, t, :], start=t == 0, stop=t == 1)
                        done(layer, f"p{s}{c}", last)
                nxt("roped")
                for g in range(NKV):
                    b = opened(layer, f"dup{g}")
                    done(layer, f"dup{g}", mm(b[:, :], C(f"dup{g}"), qk[:, 0, :], start=True, stop=True))
                attention(layer)

                for bi, i in enumerate(BRANCH_ORDER):
                    if i == 1:
                        b = opened(layer, "convnorm")
                        for c in range(2):
                            nxt("conv_square_ready")
                            last = mm(b[:, 0:N], C("ones"), csq[:, c, 0:N], start=c == 0, stop=c == 1)
                        done(layer, "convnorm", last)
                    src = (fT, conv, plT, attnT)[i]
                    for j in range(KD):
                        hf, jj = divmod(j, 4)
                        s, k = block_at(layer, BLOCK_BRANCH + 2 * bi + hf)
                        pe.wait_ge(S(f"block_in{s}"), 16 * (k + 1))
                        wb = slots[s][:, KD * 512:(KD + BRANCH_K[i]) * 512].rearrange("p (k n) -> p k n", n=512)
                        project(f"gate{i}{j}")
                        if j == 0:
                            if i == 0:
                                read(pe, layer, f"f{last_stream}1")
                            elif i == 2:
                                read(pe, layer, f"p{last_stream}1")
                            elif i == 3:
                                read(pe, layer, f"V{len(attention_units(layer)) // 4 - 1}")
                            else:
                                nxt("conv_ready", 2)
                        b = opened(layer, f"branch{i}{j}")
                        for k in range(BRANCH_K[i]):
                            last = mm(b[:, 0:N], wb[:, k, jj * P:(jj + 1) * P], src[:, k, 0:N],
                                      start=k == 0, stop=k == BRANCH_K[i] - 1)
                        done(layer, f"branch{i}{j}", last)
                nxt("merged_ready", KD)
                for j in range(KD):
                    hf, jj = divmod(j, 4)
                    w = block_ready(layer, BLOCK_OUT + hf)
                    b = opened(layer, f"out{j}")
                    for k in range(KD):
                        last = mm(b[:, 0:N], w[:, k, jj * P:(jj + 1) * P], merged[:, k, 0:N], start=k == 0, stop=k == KD - 1)
                    done(layer, f"out{j}", last)
                sum_squares(layer, "norm2", N)
                nxt("h_ready", KD * (2 - layer))
                for b in range(8):
                    pe.wait_ge(S(f"bank_free{b}"), len(range(b, uses_to[layer], 8)))

            pe.wait_ge(S("const_in"), 16)
            pe.wait_ge(S("cs_ready"), 1)
            modulation(0)
            pe.wait_ge(S("vec_in"), 16)
            attention_half(0)

            with pe.Fori(0, F_TILES // 2) as i:
                for s in range(2):
                    pe.wait_ge(S("ffn_low_ready"), 3 * i + (s + 1))
                    for m in range(2):
                        b = banks[2 * s + m]
                        for k in range(KD):
                            mm(b[:, :], f13h[:, s, m, k, :], hh[:, k, :], start=k == 0, stop=False)
                            mm(b[:, :], f13h[:, s, m, k, :], hl[:, k, :], start=False, stop=False)
                            last = mm(b[:, :], f13l[:, s, m, k, :], hh[:, k, :], start=False, stop=k == KD - 1)
                        last.then_inc(S(("ffn_up1_full", "ffn_up3_full")[m]), 1)
                pe.wait_ge(S("ffn_low_ready"), 3 * i + 3)
                pe.wait_ge(S("ffn_y_free"), i * KD + 1)
                for half in range(2):
                    for s in range(2):
                        if half == 0:
                            pe.wait_ge(S("ffn_act_ready"), i * 2 + (s + 1))
                        for d in range(4 * half, 4 * half + 4):
                            if half and s == 0:
                                pe.wait_ge(S("ffn_y_free"), i * KD + (d - 2))
                            w = slice(d * P, (d + 1) * P)
                            b = banks[4 + d % 4]
                            mm(b[:, :], f2h[:, s, w], fah[:, s, :], start=s == 0, stop=False)
                            mm(b[:, :], f2h[:, s, w], fal[:, s, :], start=False, stop=False)
                            last = mm(b[:, :], f2l[:, s, w], fah[:, s, :], start=False, stop=s == 1)
                            if s:
                                last.then_inc(S("ffn_y_full"), 1)
            pe.wait_ge(S("ffn_y_free"), 1 + KD * F_TILES // 2)

            modulation(1)
            attention_half(1)

            pe.wait_ge(S("router_in"), 16)
            for t in range(2):
                for k in range(KD):
                    last = mm(banks[0][:, t * E:(t + 1) * E], hT[:, k, t * P:(t + 1) * P], router[:, k, :],
                              start=k == 0, stop=k == KD - 1)
            last.then_inc(S("logits_full"), 1)
            for t in range(2):
                for hf in range(2):
                    for kk in range(4):
                        last = pe.transpose(banks[1 + 2 * t + hf][:, kk * P:(kk + 1) * P],
                                            hT[:, 4 * hf + kk, t * P:(t + 1) * P], C("ident"))
                    last.then_inc(S("htok_full"), 1)
            pe.wait_ge(S("mask_ready"), 1)
            m = R[:, MASK]
            mm(banks[5][:, 0:E], C("below"), m[:, 0, :], start=True, stop=True)
            mm(banks[5][:, E:2 * E], C("ones"), m[:, 0, :], start=True, stop=False)
            mm(banks[5][:, E:2 * E], C("below"), m[:, 1, :], start=False, stop=True)
            mm(banks[5][:, 2 * E:3 * E], C("ones"), m[:, 0, :], start=True, stop=False)
            mm(banks[5][:, 2 * E:3 * E], C("ones"), m[:, 1, :], start=False, stop=True).then_inc(S("rank_full"), 1)

            def gather(col):
                for hf in range(2):
                    for kk in range(4):
                        k = 4 * hf + kk
                        for t in range(2):
                            last = mm(banks[6 + hf][:, kk * P:(kk + 1) * P], htok[:, t, k * P:(k + 1) * P],
                                      Pm[:, t, bass.ds(col, SLOTS)], start=t == 0, stop=t == 1)
                    last.then_inc(S("gather_full"), 1)

            def experts(n):
                pe.wait_ge(S("select_ready"), n + 1)
                if n == 0:
                    pe.wait_ge(S("htok_ready"), 4)
                for r in range(4):
                    for i in range(4):
                        e, t = divmod(4 * r + i, 2)
                        last = pe.transpose(banks[r][:, i * P:(i + 1) * P], Pw[:, t, e, :], C("ident"))
                    last.then_inc(S("turned_full"), 1)
                gather(0)
                pe.wait_ge(S("turned_read"), 4 * n + 4)

                with pe.Fori(0, E) as e:
                    m0 = e * FE_TILES + n * E * FE_TILES

                    def up(m, u):
                        pe.wait_ge(S("moe_up_low"), m + 1)
                        b = banks[u % 2]
                        for k in range(KD):
                            mm(b[:, 0:256], hgh[:, k, :], m13h[:, u % 2, k, :], start=k == 0, stop=False)
                            mm(b[:, 0:256], hgl[:, k, :], m13h[:, u % 2, k, :], start=False, stop=False)
                            last = mm(b[:, 0:256], hgh[:, k, :], m13l[:, u % 2, k, :], start=False, stop=k == KD - 1)
                        last.then_inc(S("moe_up_full"), 1)

                    def turned(m, u):
                        pe.wait_ge(S("moe_product"), m + 1)
                        pe.transpose(banks[2 + u % 2][:, 0:SLOTS], mprod[:, u % 2, :], C("ident")).then_inc(S("moe_turned"), 1)

                    def down(m, u, start=False, stop=False):
                        pe.wait_ge(S("moe_act_low"), m + 1)
                        for hf in range(2):
                            b = banks[4 + hf]
                            w = slice(hf * 512, (hf + 1) * 512)
                            mm(b[:, :], mah[:, u % 2, :], m2h[:, u, w], start=start, stop=False, skip_group_check=True)
                            mm(b[:, :], mal[:, u % 2, :], m2h[:, u, w], start=False, stop=False, skip_group_check=True)
                            last = mm(b[:, :], mah[:, u % 2, :], m2l[:, u, w], start=False, stop=stop, skip_group_check=True)
                        last.then_inc(S("moe_down_full"), 1)

                    pe.wait_ge(S("gathered_low"), e * 2 + (n * 2 * (E + 1) + 2))
                    up(m0, 0)
                    up(m0 + 1, 1)
                    turned(m0, 0)
                    up(m0 + 2, 2)
                    turned(m0 + 1, 1)
                    pe.wait_ge(S("sums_read"), e + (n * E + 1))
                    down(m0, 0, start=True)
                    up(m0 + 3, 3)
                    turned(m0 + 2, 2)
                    down(m0 + 1, 1)
                    with pe.Fori(1, MOE_TURNS) as q:
                        m = m0 + q * MOE_UNROLL
                        for u in range(MOE_UNROLL):
                            up(m + u, u)
                            turned(m + (u - 1), (u - 1) % 4)
                            down(m + (u - 2), (u - 2) % 4)
                    m = m0 + FE_TILES
                    down(m - 2, 2)
                    pe.wait_ge(S("scatter_free"), e * 4 + (n * 4 * E + 1))
                    gather(e * SLOTS + SLOTS)
                    turned(m - 1, 3)
                    down(m - 1, 3, stop=True)
                    pe.wait_ge(S("gathered_low"), e * 2 + (n * 2 * (E + 1) + 4))
                    pe.wait_ge(S("sums_read"), e + (n * E + 2))
                    for q in range(4):
                        pe.wait_ge(S("scatter_free"), e * 4 + (n * 4 * E + 1 + max(0, q - 1)))
                        for i in range(2):
                            k = 2 * q + i
                            last = mm(banks[6 + q % 2][:, i * LAT:(i + 1) * LAT], ysum[:, k * P:(k + 1) * P],
                                      PwT[:, bass.ds(e * LAT, LAT)], start=True, stop=True)
                        last.then_inc(S("scatter_full"), 1)
                pe.wait_ge(S("scatter_free"), 4 * E * (n + 1) + 1)

            experts(0)
            pe.wait_ge(S("over_ready"), 1)
            over = pe.value_load(over_i[0:1, 0:1], min_val=0, max_val=LAT)
            with pe.If(over > SLOTS):
                experts(1)

        @blk.scalar
        def _(act):
            nxt = Next(act)
            fn = nc.scalar.activation
            act.wait_ge(S("cond_in"), 16)
            fn(cs[:, :], cond[:, :], ACT.Silu).then_inc(S("cs_ready"), 1)
            act.wait_ge(S("const_in"), 16)

            def modulation(layer):
                with act.Fori(0, MOD_BLOCKS // MOD_UNROLL) as i:
                    for u in range(MOD_UNROLL):
                        act.wait_ge(S("mod_row_full"), i * MOD_UNROLL + (layer * MOD_BLOCKS + u + 1))
                        fn(mrow[:, u, :], banks[u][0:2, :], ACT.Copy).then_inc(S("mod_row_copied"), 1)

            def norm(layer, name, n):
                for k in range(KD):
                    if name == "norm2":
                        read(act, layer, f"out{k}")
                    if k >= 2:
                        nxt("square_used")
                    fn(sq[:, k % 2, 0:n], xT[:, k, 0:n], ACT.Square).then_inc(S("square_ready"), 1)
                nxt("square_used")
                b = filled(act, layer, name)
                fn(root[:, 0:n], b[:, 0:n], ACT.Sqrt, bias=C("eps"), scale=1.0 / D).then_inc(free(layer, name), 1)
                shift = 0 if name == "norm1" else 3 * KD
                for s in range(n // LAT):
                    for k in range(KD):
                        nxt("h_scaled")
                        bias = modT[:, shift + k, s:s + 1]
                        if layer and name == "norm2":
                            fn(hT[:, k, :], hT[:, k, :], ACT.Identity, bias=bias).then_inc(S("h_ready"), 1)
                        else:
                            fn(hh[:, k, s * LAT:(s + 1) * LAT], ht[:, k % 4, :], ACT.Identity, bias=bias) \
                                .then_inc(S("h_high_ready"), 1)

            def split(layer, n):
                if n >= len(TILES):
                    return
                _, idx, col = TILES[n]
                s, use0 = block_at(layer, idx)
                act.wait_ge(S(f"block_in{s}"), 16 * (use0 + 1))
                if n >= TILE_RING:
                    filled(act, layer, TILES[n - TILE_RING][0])
                fn(wh[:, (layer * len(TILES) + n) % TILE_RING], raw_tile(idx, col), ACT.Copy).then_inc(S("tile_high_ready"), 1)

            def attention_half(layer):
                N = T if layer == 0 else LAT
                for n in range(TILE_RING):
                    split(layer, n)
                norm(layer, "norm1", T)
                for name in ("k", "v", "q0", "q1", "q2", "q3", "F0", "F1", "ca0", "ca1"):
                    if name in ("k", "q0", "q1", "q2", "q3"):
                        t = 0 if name == "k" else int(name[1]) + 1
                        n = T if t == 0 else N
                        b = filled(act, layer, name)
                        fn(hsq[:, t, 0:n], b[:, 0:n], ACT.Square).then_inc(S("head_square_ready"), 1)
                        fn(qk[:, t, 0:n], b[:, 0:n], ACT.Copy).then_inc(free(layer, name), 1)
                    split(layer, TILE_NO[name] + TILE_RING)
                for t in range(5):
                    n = T if t == 0 else N
                    b = filled(act, layer, f"heads{t}")
                    fn(hsq[:, t, 0:n], b[:, 0:n], ACT.Sqrt, bias=C("eps"), scale=1.0 / HD) \
                        .then_inc(free(layer, f"heads{t}"), 1)
                for c in range(2):
                    b = filled(act, layer, f"cg{c}")
                    fn(sg[:, c, 0:N], b[:, 0:N], ACT.Sigmoid).then_inc(free(layer, f"cg{c}"), 1)
                    split(layer, TILE_NO[f"cg{c}"] + TILE_RING)
                for c in range(2):
                    split(layer, TILE_NO[f"P{c}"] + TILE_RING)

                units = attention_units(layer)

                def keep_turned(u):
                    s, g, qt, j = units[u]
                    n = 4 - 2 * s
                    v = u // 4
                    if j == 0 and v >= 2:
                        filled(act, layer, f"V{v - 2}")
                    b = filled(act, layer, f"T{u}")
                    fn(pT[:, v % 2, 0:n, j, :], b[:, 0:n * P].rearrange("p (c q) -> p c q", q=P), ACT.Copy) \
                        .then_inc(free(layer, f"T{u}"), 1)

                for u in range(len(units) + LAG):
                    if u >= LAG:
                        keep_turned(u - LAG)
                    if u < len(units):
                        n = T if units[u][0] == 0 else CTX
                        nxt("negmax_ready")
                        b = filled(act, layer, f"S{u}")
                        fn(prob[:, u % 3, 0:n], b[:, 0:n], ACT.Exp, bias=stat[:, u % 4, 0:1], scale=HD ** -0.5,
                           accum_out=stat[:, u % 4, 1:2]).then_inc(free(layer, f"S{u}"), 1)

                step = 0
                for i in BRANCH_ORDER:
                    if i == 1:
                        act.wait_ge(S("conv_summed"), layer + 1)
                        for c in range(2):
                            fn(csq[:, c, 0:N], conv[:, c, 0:N], ACT.Square).then_inc(S("conv_square_ready"), 1)
                        b = filled(act, layer, "convnorm")
                        fn(root[:, 0:N], b[:, 0:N], ACT.Sqrt, bias=C("eps"), scale=1.0 / 256) \
                            .then_inc(free(layer, "convnorm"), 1)
                        for c in range(2):
                            nxt("conv_normed")
                            fn(conv[:, c, 0:N], conv[:, c, 0:N], ACT.Silu).then_inc(S("conv_ready"), 1)
                    for j in range(KD):
                        if step == 0:
                            act.wait_ge(S("conv_gated"), 2 * layer + 2)
                        if step >= 2:
                            pi, pj = BRANCH_ORDER[(step - 2) // KD], (step - 2) % KD
                            read(act, layer, f"branch{pi}{pj}")
                        b = filled(act, layer, f"gate{i}{j}")
                        fn(sg[:, step % 2, 0:N], b[:, 0:N], ACT.Sigmoid).then_inc(free(layer, f"gate{i}{j}"), 1)
                        split(layer, TILE_NO[f"gate{i}{j}"] + TILE_RING)
                        step += 1
                norm(layer, "norm2", N)

            modulation(0)
            act.wait_ge(S("x_in"), 16)
            attention_half(0)

            def slice_high(s, turn):
                act.wait_ge(S(f"ffn13_in{s}"), turn * 16 + 16)
                fn(f13h[:, s], f13[s], ACT.Copy).then_inc(S("ffn_high_ready"), 1)

            def turn(i, last):
                act.wait_ge(S("ffn2_in"), i * 16 + 16)
                act.wait_ge(S("ffn_y_free"), i * KD + 1)
                fn(f2h[:, :, :], f2, ACT.Copy).then_inc(S("ffn_high_ready"), 1)
                for s in range(2):
                    act.wait_ge(S("ffn_up1_full"), i * 2 + (s + 1))
                    fn(fsil[:, s, :], banks[2 * s][:, :], ACT.Silu).then_inc(S("ffn_silu_ready"), 1)
                    act.wait_ge(S("ffn_product_ready"), i * 2 + (s + 1))
                    fn(fah[:, s, :], fprod[:, s, :], ACT.Copy).then_inc(S("ffn_act_high_ready"), 1)
                    if not last:
                        act.wait_ge(S("ffn_up3_full"), i * 2 + (s + 1))
                        slice_high(s, i + 1)

            act.wait_ge(S("ffn_can_split"), 1)
            slice_high(0, 0)
            slice_high(1, 0)
            with act.Fori(0, F_TILES // 2 - 1) as i:
                turn(i, False)
            turn(F_TILES // 2 - 1, True)
            modulation(1)
            act.wait_ge(S("ffn_y_free"), 1 + KD * F_TILES // 2)
            attention_half(1)

            for r in range(4):
                act.wait_ge(S("htok_full"), r + 1)
                t, hf = divmod(r, 2)
                fn(htok[:, t, hf * 512:(hf + 1) * 512], banks[1 + r][:, :], ACT.Copy).then_inc(S("htok_ready"), 1)
            act.wait_ge(S("gap_ready"), 1)
            fn(R[:, ODDS, 0, 0:2], R[:, GAP, 0, 0:2], ACT.Exp).then_inc(S("odds_ready"), 1)

            def chunk_high(m, u, turn):
                act.wait_ge(S(f"chunk_in{u}"), turn * 16 + 16)
                act.wait_ge(S("moe_up_full"), m + 1)
                fn(m13h[:, u % 2], chunk[u][:, 0:2 * D].rearrange("p (k n) -> p k n", k=KD), ACT.Copy).then_inc(S("moe_up_high"), 1)
                act.wait_ge(S("moe_down_full"), m + 1)
                fn(m2h[:, u, :], chunk[u][:, 2 * D:CHUNK], ACT.Copy).then_inc(S("moe_down_high"), 1)

            def gathered_high(count):
                for hf in range(2):
                    act.wait_ge(S("gather_full"), count + (hf + 1))
                    fn(hgh[:, 4 * hf:4 * hf + 4, :], banks[6 + hf][:, :].rearrange("p (k s) -> p k s", k=4), ACT.Copy) \
                        .then_inc(S("gathered_high"), 1)

            def experts(n):
                for r in range(4):
                    act.wait_ge(S("turned_full"), n * 4 + r + 1)
                    fn(PwT[:, r * 512:(r + 1) * 512], banks[r][:, :], ACT.Copy).then_inc(S("turned_read"), 1)
                gathered_high(n * 2 * (E + 1))
                if n == 0:
                    chunk_high(0, 0, 0)
                with act.Fori(0, E) as e:
                    m0 = e * FE_TILES + n * E * FE_TILES
                    turn0 = e * MOE_TURNS + n * E * MOE_TURNS

                    def silu(m, u):
                        act.wait_ge(S("moe_up_full"), m + 3)
                        fn(msil[:, u % 2, :], banks[u % 2][:, 0:P], ACT.Silu).then_inc(S("moe_silu"), 1)

                    def act_high(m, u):
                        act.wait_ge(S("moe_turned"), m + 1)
                        fn(mah[:, u % 2, :], banks[2 + u % 2][:, 0:SLOTS], ACT.Copy).then_inc(S("moe_act_high"), 1)

                    for u in range(MOE_UNROLL):
                        chunk_high(m0 + (u + 1), (u + 1) % 4, turn0 + (u + 1) // 4)
                        silu(m0 + u, u)
                        if u:
                            act_high(m0 + (u - 1), u - 1)
                    with act.Fori(1, MOE_TURNS) as q:
                        m = m0 + q * MOE_UNROLL
                        for u in range(MOE_UNROLL):
                            chunk_high(m + (u + 1), (u + 1) % 4, turn0 + q + (u + 1) // 4)
                            silu(m + u, u)
                            act_high(m + (u - 1), (u - 1) % 4)
                    gathered_high(e * 2 + (n * 2 * (E + 1) + 2))
                    act_high(m0 + (FE_TILES - 1), 3)

            experts(0)
            act.wait_ge(S("over_ready"), 1)
            over = act.value_load(over_i[0:1, 0:1], min_val=0, max_val=LAT)
            with act.If(over > SLOTS):
                experts(1)

        @blk.vector
        def _(dve):
            nxt = Next(dve)
            own = [0]
            tt, ts, stt = dve.tensor_tensor, dve.tensor_scalar, dve.scalar_tensor_tensor

            def step(ins, lag=0):
                own[0] += 1
                ins.then_inc(S("dve_own"), 1)
                if own[0] > lag:
                    dve.wait_ge(S("dve_own"), own[0] - lag)

            for name, value in BEFORE.items():
                dve.sem_inc(S(name), value)

            def modulation(layer):
                with dve.Fori(0, MOD_BLOCKS // MOD_UNROLL) as i:
                    for u in range(MOD_UNROLL):
                        dve.wait_ge(S("mod_cols_full"), i * MOD_UNROLL + (layer * MOD_BLOCKS + u + 1))
                        a = i * (4 * MOD_UNROLL) + 4 * u
                        bias = vec[:, layer, bass.ds(a, 4)].unsqueeze(2).broadcast_to([P, 4, 2])
                        tt(modT[:, bass.ds(a, 4), :], banks[4 + u][:, 0:8].rearrange("p (q v) -> p q v", v=2), bias, ALU.add) \
                            .then_inc(S("mod_cols_read"), 1)
                dve.wait_ge(S("mod_cols_read"), (layer + 1) * MOD_BLOCKS + 1)
                for n, name in enumerate(("norm1", "norm2")):
                    gain = V(layer, name).unsqueeze(2).broadcast_to([P, KD, 2])
                    a = (1 + 3 * n) * KD
                    step(stt(out=scale[:, n], in0=modT[:, a:a + KD, :], scalar=1.0, in1=gain, op0=ALU.add, op1=ALU.mult))

            def norm(layer, name, n):
                read(dve, layer, name)
                step(dve.reciprocal(rstd[:, 0:n], root[:, 0:n]))
                whole = layer == 1 and name == "norm2"
                shift = 0 if name == "norm1" else 3 * KD
                units = [(s, k) for s in range(n // LAT) for k in range(KD)]

                def low(s, k):
                    nxt("h_high_ready")
                    a = slice(s * LAT, (s + 1) * LAT)
                    stt(out=hl[:, k, a], in0=ht[:, k % 4, :], scalar=modT[:, shift + k, s:s + 1],
                        in1=hh[:, k, a].bitcast(F32), op0=ALU.add, op1=ALU.subtract).then_inc(S("h_ready"), 1)

                for m, (s, k) in enumerate(units):
                    if m >= 4 and not whole:
                        low(*units[m - 4])
                        dve.wait_ge(S("h_ready"), nxt.seen["h_high_ready"])
                    stt(out=hT[:, k, :] if whole else ht[:, k % 4, :], in0=xT[:, k, s * LAT:(s + 1) * LAT],
                        scalar=scale[:, int(name == "norm2"), k, s:s + 1], in1=rstd[:, s * LAT:(s + 1) * LAT],
                        op0=ALU.mult, op1=ALU.mult).then_inc(S("h_scaled"), 1)
                if not whole:
                    for s, k in units[-4:]:
                        low(s, k)

            def split(layer, n):
                if n >= len(TILES):
                    return
                _, idx, col = TILES[n]
                nxt("tile_high_ready")
                r = (layer * len(TILES) + n) % TILE_RING
                tt(wl[:, r], raw_tile(idx, col), wh[:, r].bitcast(F32), ALU.subtract).then_inc(S("tile_low_ready"), 1)

            def attention_half(layer):
                N = T if layer == 0 else LAT
                ns = 2 - layer
                units = attention_units(layer)
                for n in range(TILE_RING):
                    split(layer, n)
                step(dve.memset(ypad[:, :, :, :], 0.0))
                norm(layer, "norm1", T)
                for name in ("k", "v", "q0", "q1", "q2", "q3", "F0", "F1", "ca0", "ca1"):
                    if name == "v":
                        b = filled(dve, layer, name)
                        dve.tensor_copy(vch[:, :], b[:, :]).then_inc(free(layer, name), 1)
                    elif name[0] == "F":
                        b = filled(dve, layer, name)
                        dve.tensor_copy(Xf[:, int(name[1]), 0:N], b[:, 0:N]).then_inc(free(layer, name), 1)
                    elif name[0] == "c":
                        b = filled(dve, layer, name)
                        dve.tensor_copy(ypad[:, int(name[2]), 0:ns, HALO:HALO + LAT], b[:, 0:N].rearrange("p (s t) -> p s t", t=LAT)) \
                            .then_inc(free(layer, name), 1)
                    split(layer, TILE_NO[name] + TILE_RING)
                for t in range(5):
                    n = T if t == 0 else N
                    read(dve, layer, f"heads{t}")
                    step(dve.reciprocal(hsq[:, t, 0:n], hsq[:, t, 0:n]))
                    stt(out=qk[:, t, 0:n], in0=qk[:, t, 0:n], scalar=V(layer, "k_g" if t == 0 else "q_g"),
                        in1=hsq[:, t, 0:n], op0=ALU.mult, op1=ALU.mult).then_inc(S("head_normed"), 1)
                for c in range(2):
                    read(dve, layer, f"ca{c}")
                    read(dve, layer, f"cg{c}")
                    y = ypad[:, c, 0:ns, HALO:HALO + LAT]
                    tt(y, y, sg[:, c, 0:N].rearrange("p (s t) -> p s t", t=LAT), ALU.mult).then_inc(S("conv_gated"), 1)
                    split(layer, TILE_NO[f"cg{c}"] + TILE_RING)
                for c in range(2):
                    b = filled(dve, layer, f"P{c}")
                    dve.tensor_copy(Xp[:, c, 0:N], b[:, 0:N]).then_inc(free(layer, f"P{c}"), 1)
                    split(layer, TILE_NO[f"P{c}"] + TILE_RING)
                b = filled(dve, layer, "vtok")
                dve.tensor_copy(vtok[:, :, :], b[:, :].rearrange("p (c d) -> p c d", c=4)).then_inc(free(layer, "vtok"), 1)
                dve.wait_ge(S("head_normed"), 5 * layer + 5)
                cos = C("cos").unsqueeze(1).broadcast_to([P, 5, LAT])
                step(tt(hsq[:, :, 0:LAT], qk[:, :, 0:LAT], cos, ALU.mult))
                for t in range(5):
                    b = filled(dve, layer, f"rot{t}")
                    tt(hsq[:, t, LAT:T], b[:, 0:LAT], C("sin"), ALU.mult).then_inc(free(layer, f"rot{t}"), 1)
                for t in range(5):
                    read(dve, layer, f"rot{t}")
                tt(qk[:, :, 0:LAT], hsq[:, :, 0:LAT], hsq[:, :, LAT:T], ALU.add).then_inc(S("roped"), 1)
                dve.wait_ge(S("roped"), layer + 1)
                for s in range(ns):
                    for c in range(2):
                        b = filled(dve, layer, f"Y{s}{c}")
                        dve.tensor_copy(Yf[:, 2 * s + c], b[:, :].rearrange("p (t n) -> p t n", t=2)).then_inc(free(layer, f"Y{s}{c}"), 1)
                for s in range(ns):
                    for c in range(2):
                        b = filled(dve, layer, f"Z{s}{c}")
                        dve.tensor_copy(Zp[:, 2 * s + c], b[:, 0:2 * P].rearrange("p (t n) -> p t n", t=2)) \
                            .then_inc(free(layer, f"Z{s}{c}"), 1)
                for s in range(ns):
                    for c in range(2):
                        b = filled(dve, layer, f"f{s}{c}")
                        dve.tensor_copy(fT[:, c, s * LAT:(s + 1) * LAT], b[:, 0:LAT]).then_inc(free(layer, f"f{s}{c}"), 1)
                for s in range(ns):
                    for c in range(2):
                        b = filled(dve, layer, f"p{s}{c}")
                        w = V(layer, "pool_scale")[:, c:c + 1]
                        for h in range(2):
                            part = slice(64 * h, 64 * h + 64)
                            last = ts(plT[part, c, s * LAT:(s + 1) * LAT], b[part, h * LAT:(h + 1) * LAT], w[part], None, ALU.mult)
                        last.then_inc(free(layer, f"p{s}{c}"), 1)
                for g in range(NKV):
                    b = filled(dve, layer, f"dup{g}")
                    dve.tensor_copy(kdup[:, g, :], b[:, :]).then_inc(free(layer, f"dup{g}"), 1)

                def maximum(u):
                    n = T if units[u][0] == 0 else CTX
                    b = filled(dve, layer, f"S{u}")
                    step(dve.tensor_reduce(stat[:, u % 4, 3:4], b[:, 0:n], AX, ALU.max))
                    ts(stat[:, u % 4, 0:1], stat[:, u % 4, 3:4], -HD ** -0.5, None, ALU.mult).then_inc(S("negmax_ready"), 1)

                def normalise(u):
                    n = T if units[u][0] == 0 else CTX
                    read(dve, layer, f"S{u}")
                    step(dve.reciprocal(stat[:, u % 4, 2:3], stat[:, u % 4, 1:2]))
                    ts(prob[:, u % 3, 0:n], prob[:, u % 3, 0:n], stat[:, u % 4, 2:3], None, ALU.mult) \
                        .then_inc(S("prob_ready"), 1)

                def keep_values(v):
                    s, g, qt, _ = units[4 * v]
                    b = filled(dve, layer, f"V{v}")
                    q0 = s * LAT + qt * P
                    dve.tensor_copy(attnT[:, 2 * g:2 * g + 2, q0:q0 + P], b[:, 0:256].rearrange("p (c q) -> p c q", q=P)) \
                        .then_inc(free(layer, f"V{v}"), 1)

                for u in range(len(units) + LAG + 2):
                    if u < len(units):
                        maximum(u)
                    if 1 <= u <= len(units):
                        normalise(u - 1)
                    if u > LAG + 1 and (u - LAG - 2) % 4 == 3:
                        keep_values((u - LAG - 2) // 4)

                dve.wait_ge(S("conv_gated"), 2 * layer + 2)

                def tap(k, c):
                    src = ypad[:, c, 0:ns, k:k + LAT]
                    dst = conv[:, c, 0:N].rearrange("p (s t) -> p s t", t=LAT)
                    w = V(layer, "taps")[:, c * CONV_K + k:c * CONV_K + k + 1]
                    if k == 0:
                        step(ts(dst, src, w, V(layer, "conv_b")[:, c:c + 1], ALU.mult, ALU.add), lag=1)
                    else:
                        step(stt(out=dst, in0=src, scalar=w, in1=dst, op0=ALU.mult, op1=ALU.add), lag=1)

                taps = [(k, c) for k in range(CONV_K) for c in range(2)]
                for bi, i in enumerate(BRANCH_ORDER):
                    if i == 1:
                        read(dve, layer, "convnorm")
                        step(dve.reciprocal(rstd[:, 0:N], root[:, 0:N]))
                        for c in range(2):
                            stt(out=conv[:, c, 0:N], in0=conv[:, c, 0:N], scalar=V(layer, "conv_g")[:, c:c + 1],
                                in1=rstd[:, 0:N], op0=ALU.mult, op1=ALU.mult).then_inc(S("conv_normed"), 1)
                    for j in range(KD):
                        n = KD * bi + j
                        read(dve, layer, f"gate{i}{j}")
                        b = filled(dve, layer, f"branch{i}{j}")
                        if bi == 0:
                            tt(merged[:, j, 0:N], sg[:, n % 2, 0:N], b[:, 0:N], ALU.mult).then_inc(free(layer, f"branch{i}{j}"), 1)
                        else:
                            tt(sq[:, n % 2, 0:N], sg[:, n % 2, 0:N], b[:, 0:N], ALU.mult).then_inc(free(layer, f"branch{i}{j}"), 1)
                            read(dve, layer, f"branch{i}{j}")
                            add = tt(merged[:, j, 0:N], merged[:, j, 0:N], sq[:, n % 2, 0:N], ALU.add)
                            if bi == 3:
                                add.then_inc(S("merged_ready"), 1)
                            else:
                                step(add)
                        split(layer, TILE_NO[f"gate{i}{j}"] + TILE_RING)
                        if taps:
                            for k, c in taps[:4]:
                                tap(k, c)
                            taps = taps[4:]
                            if not taps:
                                dve.wait_ge(S("dve_own"), own[0])
                                dve.sem_inc(S("conv_summed"), 1)
                for j in range(KD):
                    b = filled(dve, layer, f"out{j}")
                    for s in range(ns):
                        x = xT[:, j, s * LAT:(s + 1) * LAT]
                        last = stt(out=x, in0=b[:, s * LAT:(s + 1) * LAT], scalar=modT[:, 2 * KD + j, s:s + 1], in1=x,
                                   op0=ALU.mult, op1=ALU.add)
                    last.then_inc(free(layer, f"out{j}"), 1)
                norm(layer, "norm2", N)

            dve.wait_ge(S("vec_in"), 16)
            dve.wait_ge(S("const_in"), 16)
            modulation(0)
            dve.wait_ge(S("x_in"), 16)
            attention_half(0)
            dve.wait_ge(S("h_ready"), 4 * KD)
            dve.sem_inc(S("ffn_can_split"), 1)

            def slice_low(s, turn):
                dve.wait_ge(S("ffn_high_ready"), 3 * turn + (s + 1))
                tt(f13l[:, s], f13[s], f13h[:, s].bitcast(F32), ALU.subtract).then_inc(S("ffn_low_ready"), 1)

            def turn(i, last):
                dve.wait_ge(S("ffn_high_ready"), 3 * i + 3)
                tt(f2l[:, :, :], f2, f2h[:, :, :].bitcast(F32), ALU.subtract).then_inc(S("ffn_low_ready"), 1)
                for s in range(2):
                    dve.wait_ge(S("ffn_silu_ready"), i * 2 + (s + 1))
                    dve.wait_ge(S("ffn_up3_full"), i * 2 + (s + 1))
                    tt(fprod[:, s, :], fsil[:, s, :], banks[2 * s + 1][:, :], ALU.mult).then_inc(S("ffn_product_ready"), 1)
                    dve.wait_ge(S("ffn_act_high_ready"), i * 2 + (s + 1))
                    tt(fal[:, s, :], fprod[:, s, :], fah[:, s, :].bitcast(F32), ALU.subtract).then_inc(S("ffn_act_ready"), 1)
                    if not last:
                        slice_low(s, i + 1)
                dve.wait_ge(S("ffn_y_free"), i * KD + 1)
                for d in range(KD):
                    dve.wait_ge(S("ffn_y_full"), i * KD + (d + 1))
                    for s in range(2):
                        x = xT[:, d, s * LAT:(s + 1) * LAT]
                        last_ins = stt(out=x, in0=banks[4 + d % 4][:, s * LAT:(s + 1) * LAT],
                                       scalar=modT[:, 5 * KD + d, s:s + 1], in1=x, op0=ALU.mult, op1=ALU.add)
                    last_ins.then_inc(S("ffn_y_free"), 1)

            slice_low(0, 0)
            slice_low(1, 0)
            with dve.Fori(0, F_TILES // 2 - 1) as i:
                turn(i, False)
            turn(F_TILES // 2 - 1, True)
            dve.wait_ge(S("ffn_y_free"), 1 + KD * F_TILES // 2)
            modulation(1)
            attention_half(1)

            dve.wait_ge(S("logits_full"), 1)
            step(dve.tensor_copy(R[:, LOGITS], banks[0][:, 0:2 * E].rearrange("p (t e) -> p t e", t=2)))
            iota8 = C("iota8")
            top = R[:, TOP, 0]

            def choose(src, one, at):
                for t in range(2):
                    step(dve.tensor_reduce(top[:, at + t:at + t + 1], R[:, src, t], AX, ALU.max))
                    step(stt(out=R[:, EQUAL, t], in0=R[:, src, t], scalar=top[:, at + t:at + t + 1], in1=iota8,
                             op0=ALU.is_equal, op1=ALU.mult))
                    step(dve.tensor_reduce(top[:, 6 + t:7 + t], R[:, EQUAL, t], AX, ALU.max))
                    step(ts(R[:, one, t], R[:, EQUAL, t], top[:, 6 + t:7 + t], None, ALU.is_equal))

            choose(LOGITS, FIRST, 0)
            step(stt(out=R[:, REST], in0=R[:, FIRST], scalar=-3.0e38, in1=R[:, LOGITS], op0=ALU.mult, op1=ALU.add))
            choose(REST, SECOND, 2)
            tt(R[:, MASK], R[:, FIRST], R[:, SECOND], ALU.add).then_inc(S("mask_ready"), 1)
            dve.wait_ge(S("mask_ready"), 1)
            tt(R[:, GAP, 0, 0:2], top[:, 2:4], top[:, 0:2], ALU.subtract).then_inc(S("gap_ready"), 1)
            dve.wait_ge(S("odds_ready"), 1)
            odds, w = R[:, ODDS, 0, 0:2], R[:, WEIGHT, 0]
            step(ts(R[:, GAP, 0, 2:4], odds, 1.0, None, ALU.add))
            step(dve.reciprocal(w[:, 0:2], R[:, GAP, 0, 2:4]))
            step(tt(w[:, 2:4], w[:, 0:2], odds, ALU.mult))
            for t in range(2):
                step(ts(R[:, FIRST, t], R[:, FIRST, t], w[:, t:t + 1], None, ALU.mult))
                step(stt(out=R[:, COMB, t], in0=R[:, SECOND, t], scalar=w[:, 2 + t:3 + t], in1=R[:, FIRST, t],
                         op0=ALU.mult, op1=ALU.add))
            dve.wait_ge(S("rank_full"), 1)
            step(ts(R[:, EQUAL], R[:, MASK], -1.0, 1000.0, ALU.add, ALU.mult))
            step(tt(R[:, RANK], banks[5][:, 0:2 * E].rearrange("p (t e) -> p t e", t=2), R[:, MASK], ALU.mult))
            step(tt(R[:, RANK], R[:, RANK], R[:, EQUAL], ALU.add))
            step(dve.tensor_reduce(over_f[:, :], banks[5][:, 2 * E:3 * E], AX, ALU.max))
            dve.tensor_copy(over_i[:, :], over_f[0:1, :]).then_inc(S("over_ready"), 1)

            def chunk_low(m, u):
                dve.wait_ge(S("moe_up_high"), m + 1)
                tt(m13l[:, u % 2], chunk[u][:, 0:2 * D].rearrange("p (k n) -> p k n", k=KD), m13h[:, u % 2].bitcast(F32),
                   ALU.subtract).then_inc(S("moe_up_low"), 1)
                dve.wait_ge(S("moe_down_high"), m + 1)
                tt(m2l[:, u, :], chunk[u][:, 2 * D:CHUNK], m2h[:, u, :].bitcast(F32), ALU.subtract).then_inc(S("moe_split"), 1)

            def gathered_low(count):
                for hf in range(2):
                    dve.wait_ge(S("gathered_high"), count + (hf + 1))
                    tt(hgl[:, 4 * hf:4 * hf + 4, :], banks[6 + hf][:, :].rearrange("p (k s) -> p k s", k=4),
                       hgh[:, 4 * hf:4 * hf + 4, :].bitcast(F32), ALU.subtract).then_inc(S("gathered_low"), 1)

            step(dve.memset(Pm[:, :, E * SLOTS:(E + 1) * SLOTS], 0.0))

            def experts(n):
                if n:
                    step(ts(R[:, RANK], R[:, RANK], -float(SLOTS), None, ALU.add))
                for t in range(2):
                    for e in range(E):
                        rank = R[:, RANK, t, e:e + 1]
                        ts(Pm[:, t, e * SLOTS:(e + 1) * SLOTS], C("iota"), rank, None, ALU.is_equal)
                        last = ts(Pw[:, t, e, :], C("iota"), rank, R[:, COMB, t, e:e + 1], ALU.is_equal, ALU.mult)
                last.then_inc(S("select_ready"), 1)
                gathered_low(n * 2 * (E + 1))
                if n == 0:
                    chunk_low(0, 0)
                with dve.Fori(0, E) as e:
                    m0 = e * FE_TILES + n * E * FE_TILES

                    def product(m, u):
                        dve.wait_ge(S("moe_silu"), m + 1)
                        tt(mprod[:, u % 2, :], msil[:, u % 2, :], banks[u % 2][:, P:2 * P], ALU.mult).then_inc(S("moe_product"), 1)

                    def act_low(m, u):
                        dve.wait_ge(S("moe_act_high"), m + 1)
                        tt(mal[:, u % 2, :], banks[2 + u % 2][:, 0:SLOTS], mah[:, u % 2, :].bitcast(F32), ALU.subtract) \
                            .then_inc(S("moe_act_low"), 1)

                    for u in range(MOE_UNROLL):
                        chunk_low(m0 + (u + 1), (u + 1) % 4)
                        product(m0 + u, u)
                        if u:
                            act_low(m0 + (u - 1), u - 1)
                    with dve.Fori(1, MOE_TURNS) as q:
                        m = m0 + q * MOE_UNROLL
                        for u in range(MOE_UNROLL):
                            chunk_low(m + (u + 1), (u + 1) % 4)
                            product(m + u, u)
                            act_low(m + (u - 1), (u - 1) % 4)
                    gathered_low(e * 2 + (n * 2 * (E + 1) + 2))
                    act_low(m0 + (FE_TILES - 1), 3)
                    dve.wait_ge(S("moe_down_full"), m0 + (FE_TILES + 4))
                    for hf in range(2):
                        last = dve.tensor_copy(ysum[:, hf * 512:(hf + 1) * 512], banks[4 + hf][:, :])
                    last.then_inc(S("sums_read"), 1)
                    dve.wait_ge(S("scatter_free"), e * 4 + (n * 4 * E + 1))
                    for q in range(4):
                        dve.wait_ge(S("scatter_full"), e * 4 + (n * 4 * E + q + 1))
                        for i in range(2):
                            k = 2 * q + i
                            x = xT[:, k, 0:LAT]
                            last = stt(out=x, in0=banks[6 + q % 2][:, i * LAT:(i + 1) * LAT],
                                       scalar=modT[:, 5 * KD + k, 0:1], in1=x, op0=ALU.mult, op1=ALU.add)
                        last.then_inc(S("scatter_free"), 1)

            experts(0)
            dve.wait_ge(S("over_ready"), 1)
            over = dve.value_load(over_i[0:1, 0:1], min_val=0, max_val=LAT)
            with dve.If(over > SLOTS):
                experts(1)


def constants():
    c = np.zeros((P, CONST_LEN), np.float64)

    def put(name, a):
        c[:a.shape[0], CONST[name][0]:CONST[name][1]] = a

    i = np.arange(P)
    put("ident", np.eye(P))
    put("ones", np.ones((P, P)))
    put("heads", (i[:, None] // HD == i[None, :] // HD).astype(float))
    rot = np.zeros((P, P))
    for out_c in range(P):
        rot[out_c + 16 if out_c % 32 < 16 else out_c - 16, out_c] = -1.0 if out_c % 32 < 16 else 1.0
    put("rot", rot)
    for g in range(NKV):
        d = np.zeros((P, P))
        d[HD * g + i % HD, i] = 1.0
        put(f"dup{g}", d)
    ch = np.outer(np.arange(64), np.arange(64)) * (2 * np.pi / 64)
    eye2 = np.eye(2)
    norm = 1.0 / np.sqrt(64.0 * LAT)
    put("chan_cos", np.kron(eye2, np.cos(ch)) * norm)
    put("chan_sin", -np.kron(eye2, np.sin(ch)) * norm)
    put("below", (i[:, None] < i[None, :]).astype(float))
    put("iota", np.tile(i[None, :], (P, 1)))
    put("iota8", np.tile(E - np.arange(E)[None, :], (P, 1)))
    put("eps", np.full((P, 1), EPS))
    t = np.outer(np.arange(LAT), np.arange(LAT)) % LAT * (2 * np.pi / LAT)
    s = np.concatenate([np.cos(t), np.sin(t)], axis=1).reshape(2, P, 512)
    put("seq", s.transpose(1, 0, 2).reshape(P, 1024))
    n_freq = HD // 4
    freqs = (10000.0 ** (-np.arange(n_freq) / n_freq)).astype(np.float32)
    tok = np.arange(LAT)
    where = np.where((i % HD < 32)[:, None], (tok // GRID_W)[None, :], (tok % GRID_W)[None, :])
    angle = where.astype(np.float32) * freqs[i % 16][:, None]
    put("cos", np.cos(angle.astype(np.float64)))
    put("sin", np.sin(angle.astype(np.float64)))
    m = np.zeros((2, 2, P, 2, LAT))
    for g, w in enumerate(WINDOWS):
        full = np.zeros((LAT, LAT))
        for o in range(LAT):
            lo, hi = max(o - w // 2, 0), min(o + w // 2, LAT)
            full[lo:hi, o] = 1.0 / (hi - lo)
            full[o, o] -= 1.0
        m[g // 2, :, :, g % 2, :] = full.reshape(2, P, LAT)
    pool = m.transpose(2, 0, 1, 3, 4).reshape(P, POOL_LEN)
    return c.astype(np.float32), pool.astype(np.float32)


def tiled(w, width):
    k, n = w.shape
    return w.reshape(k // P, P, n // width, width).transpose(2, 1, 0, 3).reshape(n // width, P, k // P * width)


def columns(v):
    return np.ascontiguousarray(v.reshape(-1, P).T)


def layout(a):
    a = {k: np.asarray(v) for k, v in a.items()}
    x = np.concatenate([a["x"][0], a["ctx"][0]], axis=0)
    vec = np.zeros((P, DEPTH, VEC_LEN), np.float32)
    attn = np.zeros((DEPTH, N_BLOCKS, P, SLOT_LEN), np.float32)
    for l in range(DEPTH):
        def put(name, v):
            vec[:, l, COLS[name][0]:COLS[name][1]] = v

        put("b_mod", columns(a["b_mod"][l]))
        put("norm1", columns(a["norm1_g"][l]))
        put("norm2", columns(a["norm2_g"][l]))
        put("conv_b", columns(a["conv_b"][l]))
        put("conv_g", columns(a["conv_norm_g"][l]))
        put("pool_scale", columns(a["pool_scale"][l]))
        put("q_g", np.tile(a["q_norm_g"][l], 2)[:, None])
        put("k_g", np.tile(a["k_norm_g"][l], 2)[:, None])
        put("taps", a["conv_dw"][l].T.reshape(2, P, CONV_K).transpose(1, 0, 2).reshape(P, -1))
        pw = np.zeros((P, 2, P), np.float32)
        for g in range(4):
            h = 64 * (g % 2)
            pw[h:h + 64, g // 2, h:h + 64] = a["pool_w"][l, g]
        put("pool_w", pw.reshape(P, -1))
        w = a["w_in"][l]
        off_q = 1024
        off_k, off_g = off_q + 512, off_q + 768
        attn[l, BLOCK_KV, :, 0:KD * 256] = tiled(w[:, off_k:off_g], 256)[0]
        attn[l, BLOCK_Q, :, 0:KD * 512] = tiled(w[:, off_q:off_k], 512)[0]
        attn[l, BLOCK_FC, :, 0:KD * 512] = tiled(w[:, 0:512], 512)[0]
        attn[l, BLOCK_GP, :, 0:KD * 512] = tiled(w[:, 512:1024], 512)[0]
        branch = [a["w_br_fourier"][l], a["w_br_conv"][l], a["w_br_pool"][l], a["w_br_attn"][l]]
        for b, i in enumerate(BRANCH_ORDER):
            gate = tiled(w[:, off_g + i * D:off_g + (i + 1) * D], 512)
            br = tiled(branch[i], 512)
            for hf in range(2):
                attn[l, BLOCK_BRANCH + 2 * b + hf, :, 0:KD * 512] = gate[hf]
                attn[l, BLOCK_BRANCH + 2 * b + hf, :, KD * 512:(KD + BRANCH_K[i]) * 512] = br[hf]
        attn[l, BLOCK_OUT:, :, 0:KD * 512] = tiled(a["w_out"][l], 512)
    consts, pool = constants()
    cond = np.stack([a["c"][0].reshape(KD, P), a["c_ctx"].reshape(KD, P)], axis=2)
    f1, f3, f2 = a["ffn_w1"][0], a["ffn_w3"][0], a["ffn_w2"][0]
    turns = F_TILES // 2
    ffn13 = np.stack([tiled(f1, P), tiled(f3, P)], axis=2).reshape(turns, 2, P, 2 * D)
    ffn2 = f2.reshape(turns, 2, P, D).transpose(0, 2, 1, 3).reshape(turns, P, 2 * D)
    moe = np.empty((E * FE_TILES + 1, P, CHUNK), np.float32)
    for e in range(E):
        rows = moe[e * FE_TILES:(e + 1) * FE_TILES]
        up = rows[:, :, 0:2 * D].reshape(FE_TILES, P, KD, 2, P)
        up[:, :, :, 0] = tiled(a["moe_w1"][0, e], P).reshape(FE_TILES, P, KD, P)
        up[:, :, :, 1] = tiled(a["moe_w3"][0, e], P).reshape(FE_TILES, P, KD, P)
        rows[:, :, 0:2 * D] = up.reshape(FE_TILES, P, 2 * D)
        rows[:, :, 2 * D:] = a["moe_w2"][0, e].reshape(FE_TILES, P, D)
    moe[-1] = moe[0]
    return {
        "xT": np.ascontiguousarray(x.T.reshape(KD, P, T).transpose(1, 0, 2)),
        "consts": consts,
        "pool_windows": pool,
        "vectors": vec,
        "cond": np.ascontiguousarray(cond.transpose(1, 0, 2).reshape(P, 2 * KD)),
        "router": np.ascontiguousarray(a["moe_router"][0].reshape(KD, P, E).transpose(1, 0, 2)),
        "w_mod_blocks": np.stack([tiled(a["w_mod"][l], 512) for l in range(DEPTH)]),
        "attn_blocks": attn,
        "ffn13": ffn13,
        "ffn2": np.ascontiguousarray(ffn2),
        "moe": moe,
    }


def kernel(**inputs):
    import concourse.bacc as bacc
    from concourse.bass_utils import run_bass_kernel_spmd

    arrays = layout(inputs)
    nc = bacc.Bacc("TRN2", target_bir_lowering=False, num_devices=1)
    args = [nc.dram_tensor(f"in_{name}", v.shape, mybir.dt.from_np(v.dtype), kind="ExternalInput").ap() for name, v in arrays.items()]
    out = nc.dram_tensor("outT", (P, KD, LAT), F32, kind="ExternalOutput").ap()
    build(nc, *args, out)
    got = run_bass_kernel_spmd(nc, [{f"in_{k}": v for k, v in arrays.items()}], core_ids=[0]).results[0]["outT"]
    return np.ascontiguousarray(got.transpose(2, 1, 0).reshape(1, LAT, D))
```

```python
from contextlib import ExitStack

import numpy as np

import concourse.bass as bass
from concourse import mybir

F32 = mybir.dt.float32
F32R = mybir.dt.float32r
I32 = mybir.dt.int32
ALU = mybir.AluOpType
ACT = mybir.ActivationFunctionType
AX = mybir.AxisListType.X

P = 128
DEPTH, D, LAT, CTX = 2, 1024, 256, 256
T = LAT + CTX
KD = D // P
GRID_W = 64
EPS = 1e-6
HD = 64
NH, NKV = 8, 2
CONV_K = 31
HALO = CONV_K // 2
PADT = LAT + 2 * HALO
WINDOWS = (2, 4, 8, 16)
F_TILES = 2816 // P
E, FE_TILES = 8, 3584 // P
SLOTS = P

BLOCK_KV, BLOCK_Q, BLOCK_FC, BLOCK_GP = range(4)
BRANCH_ORDER = (0, 2, 3, 1)
BRANCH_K = (2, 2, 2, 4)
BLOCK_BRANCH, BLOCK_OUT = 4, 12
N_BLOCKS = 14
BLOCK_LEN = [KD * 256] + [KD * 512] * 3 + [(KD + BRANCH_K[i]) * 512 for i in BRANCH_ORDER for _ in range(2)] \
    + [KD * 512] * 2
SLOT_LEN = max(BLOCK_LEN)
RING = 2
MOD_UNROLL = 3
MOD_PARTS = 2
TILE_RING = 3
MOD_BLOCKS = 6 * D // 512
MOD_TURNS = MOD_BLOCKS // MOD_UNROLL
MOE_UNROLL = 4
MOE_TURNS = FE_TILES // MOE_UNROLL
CHUNK = 3 * D
BEFORE = {"mod_row_full": MOD_UNROLL, "ffn_y_free": 1, "scatter_free": 1, "moe_up_full": 2, "moe_down_full": 4,
          "moe_split": 4, "sums_read": 1,
          "ffn_mod_row": 1, "ffn_mod_copied": 1}

COLS = {}
_at = 0
for _name, _n in (("b_mod", 48), ("norm1", 8), ("norm2", 8), ("conv_b", 2), ("conv_g", 2), ("pool_scale", 2),
                  ("q_g", 1), ("k_g", 1), ("taps", 2 * CONV_K), ("pool_w", 2 * P)):
    COLS[_name] = (_at, _at + _n)
    _at += _n
VEC_LEN = _at
CONST = {}
_at = 0
for _name, _n in (("ident", P), ("ones", P), ("heads", P), ("rot", P), ("dup0", P), ("dup1", P), ("chan_cos", P),
                  ("chan_sin", P), ("pair", 2), ("below", P), ("iota", P), ("iota8", 8), ("eps", 1), ("seq", 2 * 512),
                  ("cos", LAT), ("sin", LAT)):
    CONST[_name] = (_at, _at + _n)
    _at += _n
CONST_LEN = _at
POOL_LEN = 2 * 2 * 512
LOGITS, EQUAL, FIRST, REST, SECOND, MASK, COMB, RANK, TOP, GAP, ODDS, WEIGHT = range(12)


LAG = 3


def attention_units(layer):
    return [(s, g, qt, j) for s in range(2 - layer) for g in range(NKV) for qt in range(2) for j in range(4)]


def psum_order(layer):
    streams = range(2 - layer)
    order = ["norm1", "k", "v"] + [f"q{t}" for t in range(4)]
    order += ["F0", "F1", "ca0", "ca1"]
    order += [f"heads{t}" for t in range(5)]
    order += ["cg0", "cg1", "P0", "P1", "vtok"]
    order += [f"rot{t}" for t in range(5)]
    order += [f"Y{s}{c}" for s in streams for c in range(2)] + [f"Z{s}{c}" for s in streams for c in range(2)]
    order += [f"f{s}{c}" for s in streams for c in range(2)] + [f"p{s}{c}" for s in streams for c in range(2)]
    order += ["dup0", "dup1"]
    n = len(attention_units(layer))
    for u in range(n + LAG + 1):
        if u < n:
            order.append(f"S{u}")
        if LAG <= u < n + LAG:
            order.append(f"T{u - LAG}")
        if u > LAG and (u - LAG - 1) % 4 == 3:
            order.append(f"V{(u - LAG - 1) // 4}")
    for i in BRANCH_ORDER:
        if i == 1:
            order.append("convnorm")
        for j in range(KD):
            order += [f"gate{i}{j}", f"branch{i}{j}"]
    order += [f"out{j}" for j in range(KD - 1)]
    if layer == 0:
        order.append("modrow")
    return order + [f"out{KD - 1}", "norm2"]


TILES = [("k", BLOCK_KV, 0), ("v", BLOCK_KV, 1)] + [(f"q{t}", BLOCK_Q, t) for t in range(4)] \
    + [("F0", BLOCK_FC, 0), ("F1", BLOCK_FC, 1), ("ca0", BLOCK_FC, 2), ("ca1", BLOCK_FC, 3)] \
    + [("cg0", BLOCK_GP, 0), ("cg1", BLOCK_GP, 1), ("P0", BLOCK_GP, 2), ("P1", BLOCK_GP, 3)] \
    + [(f"gate{i}{j}", BLOCK_BRANCH + 2 * b + j // 4, j % 4) for b, i in enumerate(BRANCH_ORDER) for j in range(KD)]
H_BEFORE = {(0, "norm1"): 0, (0, "norm2"): 2 * KD, (1, "norm1"): 4 * KD, (1, "norm2"): 6 * KD}
NORMS = list(H_BEFORE)
LAST_GATE = TILES[-1][0]
TILE_NO = {name: n for n, (name, _, _) in enumerate(TILES)}


def build(nc, xT_in, consts_in, pool_in, vec_in, cond_in, router_in, mod_in, attn_in, ffn13_in, ffn2_in, moe_in, out):
    with ExitStack() as ctx:
        def sb(name, shape, dt=F32):
            return ctx.enter_context(nc.sbuf_tensor(name, shape, dt))

        sems = {}

        def S(name):
            if name not in sems:
                sems[name] = ctx.enter_context(nc.semaphore(name))
            return sems[name]

        base = (nc.sbuf_base + 63) // 64 * 64
        room = (nc.sbuf_usable_end - base) // 4
        sb("arena", [P, room - 32])
        top = [0]

        def at(name, shape, off=None, dt=F32, parts=P):
            n = int(np.prod(shape))
            if off is None:
                off = top[0]
                top[0] += (n + 7) // 8 * 8
            assert off + n <= room - 32, (name, off + n, room)
            return nc.alloc_sbuf_tensor_at(name, [parts, *shape], dt, offset=base + 4 * off)

        xT = at("xT", [KD, T])
        const = at("const", [CONST_LEN])
        vec = at("vec", [DEPTH, VEC_LEN])
        cond = at("cond", [2 * KD])
        cs = at("cs", [2 * KD])
        router = at("router", [KD, E])
        cs4 = at("cs4", [KD, 4], dt=F32R)
        modT = at("modT", [DEPTH, 48, 2])
        scale = at("scale", [2, KD, 2])
        stat = at("stat", [4, 4])
        R = at("R", [16, 2, E])
        over_f = at("over_f", [1])
        over_i = at("over_i", [1], dt=I32, parts=1)
        sg = at("sg", [2, T])
        W = at("W", [MOE_UNROLL * CHUNK])
        slots = [W[:, s * SLOT_LEN:(s + 1) * SLOT_LEN] for s in range(RING)]
        poolm = slots[BLOCK_GP % RING][:, KD * 512:KD * 512 + POOL_LEN].rearrange("p (c a t) -> p c a t", c=2, a=2)
        f13 = [W[:, a:a + 2048].rearrange("p (m k f) -> p m k f", m=2, k=KD) for a in (4096, 6144)]
        f2 = W[:, 8192:10240].rearrange("p (s d) -> p s d", s=2)
        fmod = W[:, 0:KD * 512].rearrange("p (k n) -> p k n", k=KD)
        chunk = [W[:, u * CHUNK:(u + 1) * CHUNK] for u in range(MOE_UNROLL)]
        root = at("root", [T])
        rstd = at("rstd", [T])

        shared = top[0]
        hh = at("h_high", [KD, T], dt=F32R)
        hl = at("h_low", [KD, T], dt=F32R)
        after_h = top[0]
        wh = at("tile_high", [TILE_RING, KD, P], dt=F32R)
        wl = at("tile_low", [TILE_RING, KD, P], dt=F32R)
        region = top[0]
        merged = at("merged", [KD, T])
        hsq = at("hsq", [5, T], region)
        Yf = at("Yf", [4, 2, 2 * P], region)
        Zp = at("Zp", [4, 2, P], region + 4 * T)
        pT = at("pT", [2, 4, 4, P], region)
        qk = at("qk", [5, T])
        csq = qk[:, 0:2, :]
        kdup_at = top[0]
        kdup = at("kdup", [NKV, T])
        conv = at("conv", [2, T], kdup_at)
        vtok = at("vtok", [4, P])
        prob_at = top[0]
        prob = at("prob", [3, T])
        sq = at("sq", [2, T], prob_at)
        vch = at("vch", [T], prob_at)
        ypad = at("ypad", [2, 2, PADT])
        fT = at("fT", [2, T])
        plT = at("plT", [2, T])
        attnT_at = top[0]
        attnT = at("attnT", [4, T])
        Xf = at("Xf", [2, T], attnT_at)
        Xp = at("Xp", [2, T], attnT_at + 2 * T)
        ht = at("ht", [4, LAT], attnT_at)
        nsq = at("norm_squares", [2, T])
        top[0] = shared
        mod_raw = W[:, :].rearrange("p (u k n) -> p u k n", u=MOD_UNROLL, k=KD)
        mod_h = at("mod_high", [MOD_UNROLL, KD, 512], dt=F32R)
        mod_l = at("mod_low", [MOD_UNROLL, KD, 512], dt=F32R)
        mrow = at("mrow", [MOD_UNROLL, 512], parts=4)
        top[0] = after_h
        f13s = [[at(f"f13_{part}{s}", [2, KD, P], dt=F32R) for part in ("high", "low")] for s in range(2)]
        f2h = at("f2_high", [2, D], dt=F32R)
        f2l = at("f2_low", [2, D], dt=F32R)
        fmod_h = at("fmod_high", [KD, 256], dt=F32R)
        fmod_l = at("fmod_low", [KD, 256], dt=F32R)
        fsil = at("fsil", [2, T])
        fprod = at("fprod", [2, T])
        fah = at("fact_high", [2, T], dt=F32R)
        fal = at("fact_low", [2, T], dt=F32R)
        fmrow = at("fmod_row", [512], parts=4)
        top[0] = shared
        Pm = at("Pm", [2, (E + 1) * SLOTS])
        PwT = at("PwT", [E * LAT])
        htok = at("htok", [2, D])
        ysum = at("ysum", [D])
        hgh = at("gathered_high", [KD, SLOTS], dt=F32R)
        hgl = at("gathered_low", [KD, SLOTS], dt=F32R)
        msil = at("msil", [2, SLOTS])
        mprod = at("mprod", [2, P])
        mah = at("mact_high", [2, SLOTS], dt=F32R)
        mal = at("mact_low", [2, SLOTS], dt=F32R)
        split_at = top[0]
        m13h = at("m13_high", [2, KD, 2 * P], dt=F32R)
        m13l = at("m13_low", [2, KD, 2 * P], dt=F32R)
        m2h = at("m2_high", [4, D], dt=F32R)
        m2l = at("m2_low", [4, D], dt=F32R)
        top[0] = split_at
        Pw = at("Pw", [2, E, SLOTS])
        hT = at("hT", [KD, LAT])

        banks = [ctx.enter_context(nc.psum_tensor(f"bank{b}", [P, 512], F32)) for b in range(8)]

        def C(name):
            a, b = CONST[name]
            return const[:, a:b]

        def V(layer, name):
            a, b = COLS[name]
            return vec[:, layer, a:b]

        seq = C("seq").rearrange("p (c t) -> p c t", c=2)

        use = {}
        for layer in range(DEPTH):
            for name in psum_order(layer):
                use[layer, name] = (len(use) % 8, len(use) // 8)
        uses_to = [len(psum_order(0)), len(use)]

        def filled(eng, layer, name):
            b, k = use[layer, name]
            eng.wait_ge(S(f"bank_full{b}"), k + 1)
            return banks[b]

        def free(layer, name):
            return S(f"bank_free{use[layer, name][0]}")

        def read(eng, layer, name):
            eng.wait_ge(free(layer, name), use[layer, name][1] + 1)

        class Next:

            def __init__(self, eng):
                self.eng, self.seen = eng, {}

            def __call__(self, name, n=1):
                self.seen[name] = self.seen.get(name, 0) + n
                self.eng.wait_ge(S(name), self.seen[name])

        def block_at(layer, idx):
            n = layer * N_BLOCKS + idx
            return n % RING, n // RING

        def raw_tile(idx, col):
            width = 256 if idx == BLOCK_KV else 512
            w = slots[idx % RING][:, 0:KD * width].rearrange("p (k n) -> p k n", k=KD)
            return w[:, :, col * P:(col + 1) * P]

        blk = ctx.enter_context(nc.Block())

        @blk.sync
        def _(sp):
            sp.dma_start(cond[:, :], cond_in).then_inc(S("cond_in"), 16)
            for layer in range(DEPTH):
                if layer:
                    sp.wait_ge(S("ffn_low_ready"), 3 * F_TILES // 2)
                    sp.wait_ge(S("ffn_mod_low"), MOD_PARTS * MOD_BLOCKS)

                for u in range(MOD_BLOCKS if layer == 0 else 0):
                    r = u % MOD_UNROLL
                    if u >= MOD_UNROLL:
                        sp.wait_ge(S("mod_low_ready"), u + 1 - MOD_UNROLL)
                    sp.dma_start(mod_raw[:, r], mod_in[0, u].rearrange("p (k n) -> p k n", k=KD)).then_inc(S(f"mod_in{r}"), 16)
                    if u == 0:
                        sp.dma_start(const[:, :], consts_in).then_inc(S("const_in"), 16)
                        sp.dma_start(vec[:, :, :], vec_in).then_inc(S("vec_in"), 16)
                    if u == 4:
                        sp.dma_start(xT[:, :, :], xT_in).then_inc(S("x_in"), 16)
                        sp.dma_start(router[:, :, :], router_in).then_inc(S("router_in"), 16)
                for idx in range(N_BLOCKS):
                    s, _ = block_at(layer, idx)
                    n = BLOCK_LEN[idx]
                    last = idx - RING
                    if last < 0:
                        if layer == 0:
                            sp.wait_ge(S("mod_low_ready"), MOD_BLOCKS + last + 1)
                    elif last < BLOCK_GP:
                        tiles = [t for t, (_, b, _) in enumerate(TILES) if b == last]
                        sp.wait_ge(S("tile_low_ready"), layer * len(TILES) + tiles[-1] + 1)
                    elif last == BLOCK_GP:
                        filled(sp, layer, f"p{1 - layer}1")
                    elif last < BLOCK_OUT:
                        b, hf = divmod(last - BLOCK_BRANCH, 2)
                        filled(sp, layer, f"branch{BRANCH_ORDER[b]}{4 * hf + 3}")
                    sp.dma_start(slots[s][:, 0:n], attn_in[layer, idx, :, 0:n]).then_inc(S(f"block_in{s}"), 16)
                    if idx == BLOCK_GP:
                        sp.dma_start(poolm, pool_in.rearrange("p (c a t) -> p c a t", c=2, a=2)).then_inc(S("poolm_in"), 16)
                if layer == 0:
                    filled(sp, layer, "out3")
                    sp.dma_start(f13[0], ffn13_in[0, 0].rearrange("p (m k f) -> p m k f", m=2, k=KD)) \
                        .then_inc(S("ffn13_in0"), 16)
                    sp.dma_start(fmod, mod_in[1, 0].rearrange("p (k n) -> p k n", k=KD)).then_inc(S("ffn_mod_in"), 16)
                filled(sp, layer, "out7")
                if layer == 0:
                    sp.dma_start(f13[1], ffn13_in[0, 1].rearrange("p (m k f) -> p m k f", m=2, k=KD)) \
                        .then_inc(S("ffn13_in1"), 16)
                    sp.dma_start(f2, ffn2_in[0].rearrange("p (s d) -> p s d", s=2)).then_inc(S("ffn2_in"), 16)
                    sp.wait_ge(S("ffn_mod_low"), MOD_PARTS)
                    sp.dma_start(fmod, mod_in[1, 1].rearrange("p (k n) -> p k n", k=KD)).then_inc(S("ffn_mod_in"), 16)
                    with sp.Fori(1, F_TILES // 2) as i:
                        for s in range(2):
                            sp.wait_ge(S("ffn_low_ready"), 3 * i + (s - 2))
                            sp.dma_start(f13[s], ffn13_in[i, s].rearrange("p (m k f) -> p m k f", m=2, k=KD)) \
                                .then_inc(S(f"ffn13_in{s}"), 16)
                        sp.wait_ge(S("ffn_low_ready"), 3 * i)
                        sp.dma_start(f2, ffn2_in[i].rearrange("p (s d) -> p s d", s=2)).then_inc(S("ffn2_in"), 16)
                        sp.wait_ge(S("ffn_mod_low"), i * MOD_PARTS + MOD_PARTS)
                        sp.dma_start(fmod, mod_in[1, i + 1].rearrange("p (k n) -> p k n", k=KD)).then_inc(S("ffn_mod_in"), 16)

            def chunks(n):
                with sp.Fori(0, E * MOE_TURNS) as it:
                    for u in range(MOE_UNROLL):
                        m = it * MOE_UNROLL + (n * E * FE_TILES + u + 1)
                        slot = (u + 1) % MOE_UNROLL
                        sp.wait_ge(S("moe_split"), m + 1)
                        sp.dma_start(chunk[slot], moe_in[it * MOE_UNROLL + (u + 1)]).then_inc(S(f"chunk_in{slot}"), 16)

            sp.dma_start(chunk[0], moe_in[0]).then_inc(S("chunk_in0"), 16)
            chunks(0)
            sp.wait_ge(S("over_ready"), 1)
            over = sp.value_load(over_i[0:1, 0:1], min_val=0, max_val=LAT)
            sp.wait_ge(S("scatter_free"), 1 + 4 * E)
            with sp.If(over > SLOTS):
                chunks(1)
                sp.wait_ge(S("scatter_free"), 1 + 8 * E)
            sp.dma_start(out, xT[:, :, 0:LAT]).then_inc(S("out_done"), 16)
            sp.wait_ge(S("out_done"), 16)

        @blk.tensor
        def _(pe):
            nxt = Next(pe)
            mm = pe.matmul

            def opened(layer, name):
                b, k = use[layer, name]
                if k:
                    pe.wait_ge(S(f"bank_free{b}"), k)
                return banks[b]

            def done(layer, name, ins):
                ins.then_inc(S(f"bank_full{use[layer, name][0]}"), 1)

            def block_ready(layer, idx, width=512):
                s, k = block_at(layer, idx)
                pe.wait_ge(S(f"block_in{s}"), 16 * (k + 1))
                return slots[s][:, 0:KD * width].rearrange("p (k n) -> p k n", k=KD)

            def sum_squares(layer, name, n):
                ni = NORMS.index((layer, name))
                b = opened(layer, name)
                pe.wait_ge(S("square_used"), (ni + 1) * (KD - 1))
                mm(b[:, 0:n], C("ones"), root[:, 0:n], start=True, stop=False)
                pe.wait_ge(S("square_ready"), (ni + 1) * KD)
                done(layer, name, mm(b[:, 0:n], C("ones"), nsq[:, 1, 0:n], start=False, stop=True))

            def modulation():
                def row(i, u):
                    pe.wait_ge(S("mod_low_ready"), i * MOD_UNROLL + (u + 1))
                    for k in range(KD):
                        mm(banks[u][0:4, :], cs4[:, k, :], mod_h[:, u, k, :], start=k == 0, stop=False)
                        last = mm(banks[u][0:4, :], cs4[:, k, :], mod_l[:, u, k, :], start=False, stop=k == KD - 1)
                    last.then_inc(S("mod_row_full"), 1)

                def turned(i, u):
                    pe.wait_ge(S("mod_row_copied"), i * MOD_UNROLL + (u + 1))
                    for q in range(4):
                        last = mm(banks[4 + u][:, 2 * q:2 * q + 2], mrow[:, u, q * P:(q + 1) * P],
                                  C("pair")[0:4, :], start=True, stop=True)
                    last.then_inc(S("mod_cols_full"), 1)

                for u in range(MOD_UNROLL):
                    row(0, u)
                pe.wait_ge(S("const_in"), 16)
                turned(0, 0)
                with pe.Fori(1, MOD_TURNS) as i:
                    for u in range(MOD_UNROLL):
                        row(i, u)
                        if u < 2:
                            turned(i - 1, u + 1)
                        else:
                            turned(i, 0)
                turned(MOD_TURNS - 1, 1)
                sum_squares(0, "norm1", T)
                turned(MOD_TURNS - 1, 2)
                pe.wait_ge(S("mod_cols_read"), MOD_BLOCKS)

            def mod_half(b, half):
                for k in range(KD):
                    out_ = b[0:4, half * 256:(half + 1) * 256]
                    mm(out_, cs4[:, k, :], fmod_h[:, k, :], start=k == 0, stop=False)
                    last = mm(out_, cs4[:, k, :], fmod_l[:, k, :], start=False, stop=k == KD - 1)
                return last

            def attention(layer):
                units = attention_units(layer)
                read(pe, layer, "vtok")
                read(pe, layer, "dup1")

                def scores(u):
                    s, g, qt, j = units[u]
                    h = 4 * g + j
                    half = slice(64 * (h % 2), 64 * (h % 2) + 64)
                    a, z = (0, T) if s == 0 else (LAT, T)
                    q0 = s * LAT + qt * P
                    b = opened(layer, f"S{u}")
                    done(layer, f"S{u}", mm(b[:, 0:z - a], qk[half, 1 + h // 2, q0:q0 + P], kdup[half, g, a:z],
                                            start=True, stop=True))

                def turned(u):
                    s = units[u][0]
                    nxt("prob_ready")
                    b = opened(layer, f"T{u}")
                    for c in range(4 - 2 * s):
                        last = pe.transpose(b[:, c * P:(c + 1) * P], prob[:, u % 3, c * P:(c + 1) * P], C("ident"))
                    done(layer, f"T{u}", last)

                def values(v):
                    s, g, qt, _ = units[4 * v]
                    for u in range(4 * v, 4 * v + 4):
                        read(pe, layer, f"T{u}")
                    b = opened(layer, f"V{v}")
                    n = 4 - 2 * s
                    for half in range(2):
                        for c in range(n):
                            last = mm(b[64 * half:64 * half + 64, 0:256], vtok[:, 2 * s + c, 64 * g:64 * g + 64],
                                      pT[:, v % 2, c, half::2, :], start=c == 0, stop=c == n - 1)
                    done(layer, f"V{v}", last)

                for u in range(len(units) + LAG + 1):
                    if u < len(units):
                        scores(u)
                    if LAG <= u < len(units) + LAG:
                        turned(u - LAG)
                    if u > LAG and (u - LAG - 1) % 4 == 3:
                        values((u - LAG - 1) // 4)

            def attention_half(layer):
                N = T if layer == 0 else LAT
                streams = range(2 - layer)
                last_stream = 1 - layer
                if layer:
                    sum_squares(layer, "norm1", T)
                def project(name, n=N):
                    t = layer * len(TILES) + TILE_NO[name]
                    r = t % TILE_RING
                    pe.wait_ge(S("tile_low_ready"), t + 1)
                    b = opened(layer, name)
                    for k in range(KD):
                        mm(b[:, 0:n], wh[:, r, k, :], hh[:, k, 0:n], start=k == 0, stop=False)
                        mm(b[:, 0:n], wh[:, r, k, :], hl[:, k, 0:n], start=False, stop=False)
                        last = mm(b[:, 0:n], wl[:, r, k, :], hh[:, k, 0:n], start=False, stop=k == KD - 1)
                    done(layer, name, last)

                pair = [(TILE_NO[name] + layer * len(TILES), opened(layer, name)) for name in ("k", "v")]
                for t, _ in pair:
                    pe.wait_ge(S("tile_low_ready"), t + 1)
                for k in range(KD):
                    pe.wait_ge(S("h_ready"), H_BEFORE[layer, "norm1"] + 2 * (k + 1))
                    for (t, b), name in zip(pair, ("k", "v")):
                        r = t % TILE_RING
                        mm(b[:, :], wh[:, r, k, :], hh[:, k, :], start=k == 0, stop=False)
                        mm(b[:, :], wh[:, r, k, :], hl[:, k, :], start=False, stop=False)
                        last = mm(b[:, :], wl[:, r, k, :], hh[:, k, :], start=False, stop=k == KD - 1)
                        if k == KD - 1:
                            done(layer, name, last)
                for name in ("q0", "q1", "q2", "q3", "F0", "F1", "ca0", "ca1"):
                    project(name)
                for t in range(5):
                    n = T if t == 0 else N
                    nxt("head_square_ready")
                    b = opened(layer, f"heads{t}")
                    done(layer, f"heads{t}", mm(b[:, 0:n], C("heads"), hsq[:, t, 0:n], start=True, stop=True))
                for name in ("cg0", "cg1", "P0", "P1"):
                    project(name)
                read(pe, layer, "v")
                b = opened(layer, "vtok")
                for c in range(4):
                    last = pe.transpose(b[:, c * P:(c + 1) * P], vch[:, c * P:(c + 1) * P], C("ident"))
                done(layer, "vtok", last)
                for t in range(5):
                    nxt("head_normed")
                    b = opened(layer, f"rot{t}")
                    done(layer, f"rot{t}", mm(b[:, 0:LAT], C("rot"), qk[:, t, 0:LAT], start=True, stop=True))
                both = const[:, CONST["chan_cos"][0]:CONST["chan_sin"][1]]
                for s in streams:
                    for c in range(2):
                        read(pe, layer, f"F{c}")
                        b = opened(layer, f"Y{s}{c}")
                        for t in range(2):
                            a = s * LAT + t * P
                            last = mm(b[:, t * 256:(t + 1) * 256], Xf[:, c, a:a + P], both, start=True, stop=True)
                        done(layer, f"Y{s}{c}", last)
                for s in streams:
                    for c in range(2):
                        read(pe, layer, f"P{c}")
                        b = opened(layer, f"Z{s}{c}")
                        for t in range(2):
                            a = s * LAT + t * P
                            last = mm(b[:, t * P:(t + 1) * P], Xp[:, c, a:a + P], V(layer, "pool_w")[:, c * P:(c + 1) * P],
                                      start=True, stop=True)
                        done(layer, f"Z{s}{c}", last)
                for s in streams:
                    for c in range(2):
                        read(pe, layer, f"Y{s}{c}")
                        b = opened(layer, f"f{s}{c}")
                        for t in range(2):
                            mm(b[:, 0:LAT], Yf[:, 2 * s + c, t, 0:P], seq[:, t, 0:LAT], start=t == 0, stop=False)
                            last = mm(b[:, 0:LAT], Yf[:, 2 * s + c, t, P:2 * P], seq[:, t, LAT:2 * LAT],
                                      start=False, stop=t == 1)
                        done(layer, f"f{s}{c}", last)
                pe.wait_ge(S("poolm_in"), 16 * (layer + 1))
                for s in streams:
                    for c in range(2):
                        read(pe, layer, f"Z{s}{c}")
                        b = opened(layer, f"p{s}{c}")
                        for t in range(2):
                            last = mm(b[:, :], Zp[:, 2 * s + c, t, :], poolm[:, c, t, :], start=t == 0, stop=t == 1)
                        done(layer, f"p{s}{c}", last)
                nxt("roped")
                for g in range(NKV):
                    b = opened(layer, f"dup{g}")
                    done(layer, f"dup{g}", mm(b[:, :], C(f"dup{g}"), qk[:, 0, :], start=True, stop=True))
                attention(layer)

                for bi, i in enumerate(BRANCH_ORDER):
                    if i == 1:
                        b = opened(layer, "convnorm")
                        for c in range(2):
                            nxt("conv_square_ready")
                            last = mm(b[:, 0:N], C("ones"), csq[:, c, 0:N], start=c == 0, stop=c == 1)
                        done(layer, "convnorm", last)
                    src = (fT, conv, plT, attnT)[i]
                    for j in range(KD):
                        hf, jj = divmod(j, 4)
                        s, k = block_at(layer, BLOCK_BRANCH + 2 * bi + hf)
                        pe.wait_ge(S(f"block_in{s}"), 16 * (k + 1))
                        wb = slots[s][:, KD * 512:(KD + BRANCH_K[i]) * 512].rearrange("p (k n) -> p k n", n=512)
                        project(f"gate{i}{j}")
                        if j == 0:
                            if i == 0:
                                read(pe, layer, f"f{last_stream}1")
                            elif i == 2:
                                read(pe, layer, f"p{last_stream}1")
                            elif i == 3:
                                read(pe, layer, f"V{len(attention_units(layer)) // 4 - 1}")
                            else:
                                nxt("conv_ready", 2)
                        b = opened(layer, f"branch{i}{j}")
                        for k in range(BRANCH_K[i]):
                            last = mm(b[:, 0:N], wb[:, k, jj * P:(jj + 1) * P], src[:, k, 0:N],
                                      start=k == 0, stop=k == BRANCH_K[i] - 1)
                        done(layer, f"branch{i}{j}", last)
                nxt("merged_ready", KD)
                for j in range(KD):
                    hf, jj = divmod(j, 4)
                    w = block_ready(layer, BLOCK_OUT + hf)
                    b = opened(layer, f"out{j}")
                    for k in range(KD):
                        last = mm(b[:, 0:N], w[:, k, jj * P:(jj + 1) * P], merged[:, k, 0:N], start=k == 0, stop=k == KD - 1)
                    done(layer, f"out{j}", last)
                    if layer == 0 and j == KD - 2:
                        pe.wait_ge(S("ffn_mod_low"), 1)
                        mod_half(opened(layer, "modrow"), 0).then_inc(S("ffn_mod_row"), 1)
                if layer == 0:
                    pe.wait_ge(S("ffn_mod_low"), 2)
                    done(layer, "modrow", mod_half(banks[use[layer, "modrow"][0]], 1))
                sum_squares(layer, "norm2", N)
                for b in range(8):
                    pe.wait_ge(S(f"bank_free{b}"), len(range(b, uses_to[layer], 8)))

            pe.wait_ge(S("cs_low_ready"), 1)
            modulation()
            pe.wait_ge(S("vec_in"), 16)
            attention_half(0)

            def mod_row(n, half):
                pe.wait_ge(S("ffn_mod_low"), n * MOD_PARTS + (half + 1))
                mod_half(banks[7], half).then_inc(S("ffn_mod_row"), 1)

            def mod_turned(n):
                pe.wait_ge(S("ffn_mod_copied"), n + 1)
                for q in range(4):
                    last = mm(banks[6][:, 2 * q:2 * q + 2], fmrow[:, q * P:(q + 1) * P], C("pair")[0:4, :],
                              start=True, stop=True)
                last.then_inc(S("ffn_mod_turned"), 1)

            with pe.Fori(0, F_TILES // 2) as i:
                pe.wait_ge(S("ffn_low_ready"), 3 * i + 1)
                for k in range(KD):
                    pe.wait_ge(S("h_ready"), H_BEFORE[0, "norm2"] + 2 * (k + 1))
                    for m in range(2):
                        b = banks[m]
                        mm(b[:, :], f13s[0][0][:, m, k, :], hh[:, k, :], start=k == 0, stop=False)
                        mm(b[:, :], f13s[0][0][:, m, k, :], hl[:, k, :], start=False, stop=False)
                        last = mm(b[:, :], f13s[0][1][:, m, k, :], hh[:, k, :], start=False, stop=k == KD - 1)
                        if k == KD - 1:
                            last.then_inc(S(("ffn_up1_full", "ffn_up3_full")[m]), 1)
                for s in range(1, 2):
                    pe.wait_ge(S("ffn_low_ready"), 3 * i + (s + 1))
                    for m in range(2):
                        if s and m == 0:
                            pe.wait_ge(S("ffn_y_free"), i * KD + 1)
                            mod_turned(i)
                            mod_row(i + 1, 0)
                        elif s:
                            mod_row(i + 1, 1)
                        b = banks[2 * s + m]
                        for k in range(KD):
                            mm(b[:, :], f13s[s][0][:, m, k, :], hh[:, k, :], start=k == 0, stop=False)
                            mm(b[:, :], f13s[s][0][:, m, k, :], hl[:, k, :], start=False, stop=False)
                            last = mm(b[:, :], f13s[s][1][:, m, k, :], hh[:, k, :], start=False, stop=k == KD - 1)
                        last.then_inc(S(("ffn_up1_full", "ffn_up3_full")[m]), 1)
                pe.wait_ge(S("ffn_low_ready"), 3 * i + 3)
                pe.wait_ge(S("ffn_y_free"), i * KD + 1)
                for half in range(2):
                    for s in range(2):
                        if half == 0:
                            pe.wait_ge(S("ffn_act_ready"), i * 2 + (s + 1))
                        for d in range(4 * half, 4 * half + 4):
                            if half == 0 and s == 0 and d == 2:
                                pe.wait_ge(S("ffn_mod_read"), i + 1)
                            if half == 0 and s == 0 and d == 3:
                                pe.wait_ge(S("ffn_mod_copied"), i + 2)
                            if half and s == 0:
                                pe.wait_ge(S("ffn_y_free"), i * KD + (d - 2))
                            w = slice(d * P, (d + 1) * P)
                            b = banks[4 + d % 4]
                            mm(b[:, :], f2h[:, s, w], fah[:, s, :], start=s == 0, stop=False)
                            mm(b[:, :], f2h[:, s, w], fal[:, s, :], start=False, stop=False)
                            last = mm(b[:, :], f2l[:, s, w], fah[:, s, :], start=False, stop=s == 1)
                            if s:
                                last.then_inc(S("ffn_y_full"), 1)
            pe.wait_ge(S("ffn_y_free"), 1 + KD * F_TILES // 2)
            mod_turned(MOD_BLOCKS - 1)
            pe.wait_ge(S("ffn_mod_read"), MOD_BLOCKS)
            attention_half(1)

            pe.wait_ge(S("router_in"), 16)
            for k in range(KD):
                pe.wait_ge(S("h_ready"), H_BEFORE[1, "norm2"] + k + 1)
                for t in range(2):
                    logit = mm(banks[6 * t][:, 0:E], hT[:, k, t * P:(t + 1) * P], router[:, k, :], start=k == 0, stop=k == KD - 1)
                if k == KD - 1:
                    logit.then_inc(S("logits_full"), 1)
                hf, kk = divmod(k, 4)
                for t in range(2):
                    last = pe.transpose(banks[1 + 2 * hf + t][:, kk * P:(kk + 1) * P], hT[:, k, t * P:(t + 1) * P], C("ident"))
                    if kk == 3:
                        last.then_inc(S("htok_full"), 1)
            pe.wait_ge(S("mask_ready"), 1)
            m = R[:, MASK]
            mm(banks[5][:, 0:E], C("below"), m[:, 0, :], start=True, stop=True)
            mm(banks[5][:, E:2 * E], C("ones"), m[:, 0, :], start=True, stop=False)
            mm(banks[5][:, E:2 * E], C("below"), m[:, 1, :], start=False, stop=True)
            mm(banks[5][:, 2 * E:3 * E], C("ones"), m[:, 0, :], start=True, stop=False)
            mm(banks[5][:, 2 * E:3 * E], C("ones"), m[:, 1, :], start=False, stop=True).then_inc(S("rank_full"), 1)

            def gather(col):
                for hf in range(2):
                    for kk in range(4):
                        k = 4 * hf + kk
                        for t in range(2):
                            last = mm(banks[6 + hf][:, kk * P:(kk + 1) * P], htok[:, t, k * P:(k + 1) * P],
                                      Pm[:, t, bass.ds(col, SLOTS)], start=t == 0, stop=t == 1)
                    last.then_inc(S("gather_full"), 1)

            def experts(n):
                pe.wait_ge(S("select_ready"), n + 1)
                if n == 0:
                    pe.wait_ge(S("htok_ready"), 4)
                for r in range(4):
                    for i in range(4):
                        e, t = divmod(4 * r + i, 2)
                        last = pe.transpose(banks[r][:, i * P:(i + 1) * P], Pw[:, t, e, :], C("ident"))
                    last.then_inc(S("turned_full"), 1)
                gather(0)
                pe.wait_ge(S("turned_read"), 4 * n + 4)

                def scatter(e, half):
                    if half == 0:
                        pe.wait_ge(S("sums_read"), e + (n * E + 2))
                    for q in range(2 * half, 2 * half + 2):
                        pe.wait_ge(S("scatter_free"), e * 4 + (n * 4 * E + 1 + max(0, q - 1)))
                        for i in range(2):
                            k = 2 * q + i
                            last = mm(banks[6 + q % 2][:, i * LAT:(i + 1) * LAT], ysum[:, k * P:(k + 1) * P],
                                      PwT[:, bass.ds(e * LAT, LAT)], start=True, stop=True)
                        last.then_inc(S("scatter_full"), 1)

                def expert(e, first=False):
                    m0 = e * FE_TILES + n * E * FE_TILES

                    def up(m, u):
                        pe.wait_ge(S("moe_up_low"), m + 1)
                        b = banks[u % 2]
                        for k in range(KD):
                            mm(b[:, 0:256], hgh[:, k, :], m13h[:, u % 2, k, :], start=k == 0, stop=False)
                            mm(b[:, 0:256], hgl[:, k, :], m13h[:, u % 2, k, :], start=False, stop=False)
                            last = mm(b[:, 0:256], hgh[:, k, :], m13l[:, u % 2, k, :], start=False, stop=k == KD - 1)
                        last.then_inc(S("moe_up_full"), 1)

                    def turned(m, u):
                        pe.wait_ge(S("moe_product"), m + 1)
                        pe.transpose(banks[2 + u % 2][:, 0:SLOTS], mprod[:, u % 2, :], C("ident")).then_inc(S("moe_turned"), 1)

                    def down(m, u, start=False, stop=False):
                        pe.wait_ge(S("moe_act_low"), m + 1)
                        for hf in range(2):
                            b = banks[4 + hf]
                            w = slice(hf * 512, (hf + 1) * 512)
                            mm(b[:, :], mah[:, u % 2, :], m2h[:, u, w], start=start, stop=False, skip_group_check=True)
                            mm(b[:, :], mal[:, u % 2, :], m2h[:, u, w], start=False, stop=False, skip_group_check=True)
                            last = mm(b[:, :], mah[:, u % 2, :], m2l[:, u, w], start=False, stop=stop, skip_group_check=True)
                        last.then_inc(S("moe_down_full"), 1)

                    pe.wait_ge(S("gathered_low"), e * 2 + (n * 2 * (E + 1) + 2))
                    up(m0, 0)
                    up(m0 + 1, 1)
                    turned(m0, 0)
                    up(m0 + 2, 2)
                    turned(m0 + 1, 1)
                    if not first:
                        scatter(e - 1, 0)
                    pe.wait_ge(S("sums_read"), e + (n * E + 1))
                    down(m0, 0, start=True)
                    up(m0 + 3, 3)
                    turned(m0 + 2, 2)
                    down(m0 + 1, 1)
                    if not first:
                        scatter(e - 1, 1)
                    with pe.Fori(1, MOE_TURNS) as q:
                        m = m0 + q * MOE_UNROLL
                        for u in range(MOE_UNROLL):
                            up(m + u, u)
                            turned(m + (u - 1), (u - 1) % 4)
                            down(m + (u - 2), (u - 2) % 4)
                    m = m0 + FE_TILES
                    pe.wait_ge(S("scatter_free"), e * 4 + (n * 4 * E + 1))
                    gather(e * SLOTS + SLOTS)
                    turned(m - 1, 3)
                    down(m - 2, 2)
                    down(m - 1, 3, stop=True)

                expert(0, first=True)
                with pe.Fori(1, E) as e:
                    expert(e)
                pe.wait_ge(S("gathered_low"), (n + 1) * 2 * (E + 1))
                for half in range(2):
                    scatter(E - 1, half)
                pe.wait_ge(S("scatter_free"), 4 * E * (n + 1) + 1)

            experts(0)
            pe.wait_ge(S("over_ready"), 1)
            over = pe.value_load(over_i[0:1, 0:1], min_val=0, max_val=LAT)
            with pe.If(over > SLOTS):
                experts(1)

        @blk.scalar
        def _(act):
            nxt = Next(act)
            fn = nc.scalar.activation
            act.wait_ge(S("cond_in"), 16)
            fn(cs[:, :], cond[:, :], ACT.Silu).then_inc(S("cs_ready"), 1)
            act.wait_ge(S("cs_ready"), 1)
            fn(cs4[:, :, 0:2], cs[:, :].rearrange("p (k v) -> p k v", k=KD), ACT.Copy).then_inc(S("cs_high_ready"), 1)

            def modulation():
                def high(i, u):
                    act.wait_ge(S(f"mod_in{u}"), i * 16 + 16)
                    act.wait_ge(S("mod_row_full"), i * MOD_UNROLL + (u + 1))
                    fn(mod_h[:, u], mod_raw[:, u],
                       ACT.Copy).then_inc(S("mod_high_ready"), 1)

                def copy(i, u, again):
                    act.wait_ge(S("mod_row_full"), i * MOD_UNROLL + (MOD_UNROLL + u + 1))
                    if again:
                        act.wait_ge(S("mod_cols_read"), i * MOD_UNROLL + (u + 1 - MOD_UNROLL))
                    fn(mrow[:, u, :], banks[u][0:4, :], ACT.Copy).then_inc(S("mod_row_copied"), 1)

                for u in range(MOD_UNROLL):
                    high(0, u)
                copy(0, 0, False)
                high(1, 0)
                copy(0, 1, False)
                high(1, 1)
                copy(0, 2, False)
                high(1, 2)
                copy(1, 0, True)
                with act.Fori(2, MOD_TURNS) as i:
                    for u in range(MOD_UNROLL):
                        high(i, u)
                        if u < 2:
                            copy(i - 1, u + 1, True)
                        else:
                            copy(i, 0, True)
                act.wait_ge(S("x_in"), 16)
                squares(0, "norm1", T)
                copy(MOD_TURNS - 1, 1, True)
                copy(MOD_TURNS - 1, 2, True)

            def slice_high(s, turn):
                act.wait_ge(S(f"ffn13_in{s}"), turn * 16 + 16)
                fn(f13s[s][0][:], f13[s], ACT.Copy).then_inc(S("ffn_high_ready"), 1)

            def mod_high(n, half):
                if half == 0:
                    act.wait_ge(S("ffn_mod_in"), n * 16 + 16)
                fn(fmod_h[:, :, :], fmod[:, :, half * 256:(half + 1) * 256], ACT.Copy).then_inc(S("ffn_mod_high"), 1)

            def squares(layer, name, n):
                for k in range(KD):
                    if layer == 0 and name == "norm2":
                        if k == 4:
                            filled(act, layer, LAST_GATE)
                            slice_high(0, 0)
                        if k == 5:
                            mod_high(0, 0)
                        if k == 7:
                            act.wait_ge(S("ffn_mod_row"), 2)
                            mod_high(0, 1)
                    if name == "norm2":
                        read(act, layer, f"out{k}")
                    elif layer:
                        act.wait_ge(S("ffn_y_free"), 1 + KD * (F_TILES // 2 - 1) + k + 1)
                    if k >= 2:
                        nxt("square_used")
                    fn(nsq[:, k % 2, 0:n], xT[:, k, 0:n], ACT.Square).then_inc(S("square_ready"), 1)
                nxt("square_used")

            def norm(layer, name, n):
                if layer or name == "norm2":
                    squares(layer, name, n)
                b = filled(act, layer, name)
                fn(root[:, 0:n], b[:, 0:n], ACT.Sqrt, bias=C("eps"), scale=1.0 / D).then_inc(free(layer, name), 1)
                if layer == 0 and name == "norm2":
                    fn(fmrow[:, :], filled(act, 0, "modrow")[0:4, :], ACT.Copy).then_inc(free(0, "modrow"), 1)
                shift = 0 if name == "norm1" else 3 * KD
                for k in range(KD):
                    for s in range(n // LAT):
                        nxt("h_scaled")
                        bias = modT[:, layer, shift + k, s:s + 1]
                        if layer and name == "norm2":
                            fn(hT[:, k, :], hT[:, k, :], ACT.Identity, bias=bias).then_inc(S("h_ready"), 1)
                        else:
                            fn(hh[:, k, s * LAT:(s + 1) * LAT], ht[:, (2 * k + s) % 4, :], ACT.Identity, bias=bias) \
                                .then_inc(S("h_high_ready"), 1)

            def split(layer, n):
                if n >= len(TILES):
                    return
                _, idx, col = TILES[n]
                s, use0 = block_at(layer, idx)
                act.wait_ge(S(f"block_in{s}"), 16 * (use0 + 1))
                if n >= TILE_RING:
                    filled(act, layer, TILES[n - TILE_RING][0])
                fn(wh[:, (layer * len(TILES) + n) % TILE_RING], raw_tile(idx, col), ACT.Copy).then_inc(S("tile_high_ready"), 1)

            def attention_half(layer):
                N = T if layer == 0 else LAT
                for n in range(TILE_RING):
                    split(layer, n)
                norm(layer, "norm1", T)
                for name in ("k", "v", "q0", "q1", "q2", "q3", "F0", "F1", "ca0", "ca1"):
                    if name in ("k", "q0", "q1", "q2", "q3"):
                        t = 0 if name == "k" else int(name[1]) + 1
                        n = T if t == 0 else N
                        b = filled(act, layer, name)
                        fn(hsq[:, t, 0:n], b[:, 0:n], ACT.Square).then_inc(S("head_square_ready"), 1)
                        fn(qk[:, t, 0:n], b[:, 0:n], ACT.Copy).then_inc(free(layer, name), 1)
                    split(layer, TILE_NO[name] + TILE_RING)
                for t in range(5):
                    n = T if t == 0 else N
                    b = filled(act, layer, f"heads{t}")
                    fn(hsq[:, t, 0:n], b[:, 0:n], ACT.Sqrt, bias=C("eps"), scale=1.0 / HD) \
                        .then_inc(free(layer, f"heads{t}"), 1)
                for c in range(2):
                    b = filled(act, layer, f"cg{c}")
                    fn(sg[:, c, 0:N], b[:, 0:N], ACT.Sigmoid).then_inc(free(layer, f"cg{c}"), 1)
                    split(layer, TILE_NO[f"cg{c}"] + TILE_RING)
                for c in range(2):
                    split(layer, TILE_NO[f"P{c}"] + TILE_RING)

                units = attention_units(layer)

                def keep_turned(u):
                    s, g, qt, j = units[u]
                    n = 4 - 2 * s
                    v = u // 4
                    if j == 0 and v >= 2:
                        filled(act, layer, f"V{v - 2}")
                    b = filled(act, layer, f"T{u}")
                    fn(pT[:, v % 2, 0:n, j, :], b[:, 0:n * P].rearrange("p (c q) -> p c q", q=P), ACT.Copy) \
                        .then_inc(free(layer, f"T{u}"), 1)

                for u in range(len(units) + LAG):
                    if u >= LAG:
                        keep_turned(u - LAG)
                    if u < len(units):
                        n = T if units[u][0] == 0 else CTX
                        nxt("negmax_ready")
                        b = filled(act, layer, f"S{u}")
                        fn(prob[:, u % 3, 0:n], b[:, 0:n], ACT.Exp, bias=stat[:, u % 4, 0:1], scale=HD ** -0.5,
                           accum_out=stat[:, u % 4, 1:2]).then_inc(free(layer, f"S{u}"), 1)

                step = 0
                for i in BRANCH_ORDER:
                    if i == 1:
                        act.wait_ge(S("conv_summed"), layer + 1)
                        for c in range(2):
                            fn(csq[:, c, 0:N], conv[:, c, 0:N], ACT.Square).then_inc(S("conv_square_ready"), 1)
                        b = filled(act, layer, "convnorm")
                        fn(root[:, 0:N], b[:, 0:N], ACT.Sqrt, bias=C("eps"), scale=1.0 / 256) \
                            .then_inc(free(layer, "convnorm"), 1)
                        for c in range(2):
                            nxt("conv_normed")
                            fn(conv[:, c, 0:N], conv[:, c, 0:N], ACT.Silu).then_inc(S("conv_ready"), 1)
                    for j in range(KD):
                        if step == 0:
                            act.wait_ge(S("conv_gated"), 2 * layer + 2)
                        if step >= 2:
                            pi, pj = BRANCH_ORDER[(step - 2) // KD], (step - 2) % KD
                            read(act, layer, f"branch{pi}{pj}")
                        b = filled(act, layer, f"gate{i}{j}")
                        fn(sg[:, step % 2, 0:N], b[:, 0:N], ACT.Sigmoid).then_inc(free(layer, f"gate{i}{j}"), 1)
                        split(layer, TILE_NO[f"gate{i}{j}"] + TILE_RING)
                        step += 1
                norm(layer, "norm2", N)

            modulation()
            act.wait_ge(S("const_in"), 16)
            act.wait_ge(S("x_in"), 16)
            attention_half(0)

            def mod_copy(n):
                act.wait_ge(S("ffn_mod_row"), n * MOD_PARTS + MOD_PARTS)
                fn(fmrow[:, :], banks[7][0:4, :], ACT.Copy).then_inc(S("ffn_mod_copied"), 1)

            def turn(i, last):
                act.wait_ge(S("ffn2_in"), i * 16 + 16)
                act.wait_ge(S("ffn_y_free"), i * KD + 1)
                fn(f2h[:, :, :], f2, ACT.Copy).then_inc(S("ffn_high_ready"), 1)
                mod_high(i + 1, 0)
                for s in range(2):
                    if s:
                        act.wait_ge(S("ffn_mod_row"), i * MOD_PARTS + (MOD_PARTS + 1))
                        mod_high(i + 1, 1)
                        act.wait_ge(S("ffn_mod_turned"), i + 1)
                        mod_copy(i + 1)
                    act.wait_ge(S("ffn_up1_full"), i * 2 + (s + 1))
                    fn(fsil[:, s, :], banks[2 * s][:, :], ACT.Silu).then_inc(S("ffn_silu_ready"), 1)
                    act.wait_ge(S("ffn_product_ready"), i * 2 + (s + 1))
                    fn(fah[:, s, :], fprod[:, s, :], ACT.Copy).then_inc(S("ffn_act_high_ready"), 1)
                    if not last:
                        act.wait_ge(S("ffn_up3_full"), i * 2 + (s + 1))
                        slice_high(s, i + 1)

            slice_high(1, 0)
            with act.Fori(0, F_TILES // 2 - 1) as i:
                turn(i, False)
            turn(F_TILES // 2 - 1, True)
            attention_half(1)

            for r in range(4):
                act.wait_ge(S("htok_full"), r + 1)
                hf, t = divmod(r, 2)
                fn(htok[:, t, hf * 512:(hf + 1) * 512], banks[1 + r][:, :], ACT.Copy).then_inc(S("htok_ready"), 1)
            act.wait_ge(S("gap_ready"), 1)
            fn(R[:, ODDS, 0, 0:2], R[:, GAP, 0, 0:2], ACT.Exp).then_inc(S("odds_ready"), 1)

            def chunk_high(m, u, turn):
                act.wait_ge(S(f"chunk_in{u}"), turn * 16 + 16)
                act.wait_ge(S("moe_up_full"), m + 1)
                fn(m13h[:, u % 2], chunk[u][:, 0:2 * D].rearrange("p (k n) -> p k n", k=KD), ACT.Copy).then_inc(S("moe_up_high"), 1)
                act.wait_ge(S("moe_down_full"), m + 1)
                fn(m2h[:, u, :], chunk[u][:, 2 * D:CHUNK], ACT.Copy).then_inc(S("moe_down_high"), 1)

            def gathered_high(count):
                for hf in range(2):
                    act.wait_ge(S("gather_full"), count + (hf + 1))
                    fn(hgh[:, 4 * hf:4 * hf + 4, :], banks[6 + hf][:, :].rearrange("p (k s) -> p k s", k=4), ACT.Copy) \
                        .then_inc(S("gathered_high"), 1)

            def experts(n):
                for r in range(4):
                    act.wait_ge(S("turned_full"), n * 4 + r + 1)
                    fn(PwT[:, r * 512:(r + 1) * 512], banks[r][:, :], ACT.Copy).then_inc(S("turned_read"), 1)
                gathered_high(n * 2 * (E + 1))
                if n == 0:
                    chunk_high(0, 0, 0)
                def sums(e):
                    act.wait_ge(S("moe_down_full"), e * FE_TILES + (n * E * FE_TILES + FE_TILES + 4))
                    fn(ysum[:, 0:512], banks[4][:, :], ACT.Copy)
                    fn(ysum[:, 512:D], banks[5][:, :], ACT.Copy).then_inc(S("sums_read"), 1)

                def expert(e, first=False):
                    m0 = e * FE_TILES + n * E * FE_TILES
                    turn0 = e * MOE_TURNS + n * E * MOE_TURNS

                    def silu(m, u):
                        act.wait_ge(S("moe_up_full"), m + 3)
                        fn(msil[:, u % 2, :], banks[u % 2][:, 0:P], ACT.Silu).then_inc(S("moe_silu"), 1)

                    def act_high(m, u):
                        act.wait_ge(S("moe_turned"), m + 1)
                        fn(mah[:, u % 2, :], banks[2 + u % 2][:, 0:SLOTS], ACT.Copy).then_inc(S("moe_act_high"), 1)

                    for u in range(MOE_UNROLL):
                        chunk_high(m0 + (u + 1), (u + 1) % 4, turn0 + (u + 1) // 4)
                        if u == 1 and not first:
                            sums(e - 1)
                        silu(m0 + u, u)
                        if u:
                            act_high(m0 + (u - 1), u - 1)
                    with act.Fori(1, MOE_TURNS) as q:
                        m = m0 + q * MOE_UNROLL
                        for u in range(MOE_UNROLL):
                            chunk_high(m + (u + 1), (u + 1) % 4, turn0 + q + (u + 1) // 4)
                            silu(m + u, u)
                            act_high(m + (u - 1), (u - 1) % 4)
                    gathered_high(e * 2 + (n * 2 * (E + 1) + 2))
                    act_high(m0 + (FE_TILES - 1), 3)

                expert(0, first=True)
                with act.Fori(1, E) as e:
                    expert(e)
                sums(E - 1)

            experts(0)
            act.wait_ge(S("over_ready"), 1)
            over = act.value_load(over_i[0:1, 0:1], min_val=0, max_val=LAT)
            with act.If(over > SLOTS):
                experts(1)

        @blk.vector
        def _(dve):
            nxt = Next(dve)
            own = [0]
            tt, ts, stt = dve.tensor_tensor, dve.tensor_scalar, dve.scalar_tensor_tensor

            def step(ins, lag=0):
                own[0] += 1
                ins.then_inc(S("dve_own"), 1)
                if own[0] > lag:
                    dve.wait_ge(S("dve_own"), own[0] - lag)

            for name, value in BEFORE.items():
                dve.sem_inc(S(name), value)

            def add_square(layer, name, k, n):
                if k < 1:
                    return
                ni = NORMS.index((layer, name))
                dve.wait_ge(S("square_ready"), ni * KD + k + 1)
                if k > 1:
                    dve.wait_ge(S("square_used"), ni * (KD - 1) + k)
                tt(root[:, 0:n], nsq[:, 0, 0:n] if k == 1 else root[:, 0:n], nsq[:, k % 2, 0:n], ALU.add) \
                    .then_inc(S("square_used"), 2 if k == 1 else 1)

            def add_bias(layer, a, bank):
                bias = vec[:, layer, bass.ds(a, 4)].unsqueeze(2).broadcast_to([P, 4, 2])
                return tt(modT[:, layer, bass.ds(a, 4), :], bank[:, 0:8].rearrange("p (q v) -> p q v", v=2), bias, ALU.add)

            def modulation():
                def low(n, u):
                    dve.wait_ge(S("mod_high_ready"), n + 1)
                    tt(mod_l[:, u], mod_raw[:, u],
                       mod_h[:, u].bitcast(F32), ALU.subtract).then_inc(S("mod_low_ready"), 1)

                def cols(i, u):
                    dve.wait_ge(S("mod_cols_full"), i * MOD_UNROLL + (u + 1))
                    add_bias(0, i * (4 * MOD_UNROLL) + 4 * u, banks[4 + u]).then_inc(S("mod_cols_read"), 1)

                for u in range(MOD_UNROLL):
                    low(u, u)
                with dve.Fori(1, MOD_TURNS) as i:
                    for u in range(MOD_UNROLL):
                        low(i * MOD_UNROLL + u, u)
                        cols(i - 1, u)
                for k in range(1, KD - 1):
                    add_square(0, "norm1", k, T)
                for u in range(MOD_UNROLL):
                    cols(MOD_TURNS - 1, u)
                dve.wait_ge(S("mod_cols_read"), MOD_BLOCKS)

            def gains(layer):
                for n, name in enumerate(("norm1", "norm2")):
                    gain = V(layer, name).unsqueeze(2).broadcast_to([P, KD, 2])
                    a = (1 + 3 * n) * KD
                    step(stt(out=scale[:, n], in0=modT[:, layer, a:a + KD, :], scalar=1.0, in1=gain, op0=ALU.add, op1=ALU.mult))

            def slice_low(s, turn):
                dve.wait_ge(S("ffn_high_ready"), 3 * turn + (s + 1))
                tt(f13s[s][1][:], f13[s], f13s[s][0][:].bitcast(F32), ALU.subtract).then_inc(S("ffn_low_ready"), 1)

            def mod_low(n, half):
                dve.wait_ge(S("ffn_mod_high"), n * MOD_PARTS + (half + 1))
                tt(fmod_l[:, :, :], fmod[:, :, half * 256:(half + 1) * 256], fmod_h[:, :, :].bitcast(F32), ALU.subtract) \
                    .then_inc(S("ffn_mod_low"), 1)

            def norm(layer, name, n):
                read(dve, layer, name)
                step(dve.reciprocal(rstd[:, 0:n], root[:, 0:n]))
                whole = layer == 1 and name == "norm2"
                shift = 0 if name == "norm1" else 3 * KD
                units = [(s, k) for k in range(KD) for s in range(n // LAT)]

                def low(s, k):
                    nxt("h_high_ready")
                    a = slice(s * LAT, (s + 1) * LAT)
                    stt(out=hl[:, k, a], in0=ht[:, (2 * k + s) % 4, :], scalar=modT[:, layer, shift + k, s:s + 1],
                        in1=hh[:, k, a].bitcast(F32), op0=ALU.add, op1=ALU.subtract).then_inc(S("h_ready"), 1)

                for m, (s, k) in enumerate(units):
                    if m >= 4 and not whole:
                        low(*units[m - 4])
                        dve.wait_ge(S("h_ready"), nxt.seen["h_high_ready"])
                    stt(out=hT[:, k, :] if whole else ht[:, (2 * k + s) % 4, :], in0=xT[:, k, s * LAT:(s + 1) * LAT],
                        scalar=scale[:, int(name == "norm2"), k, s:s + 1], in1=rstd[:, s * LAT:(s + 1) * LAT],
                        op0=ALU.mult, op1=ALU.mult).then_inc(S("h_scaled"), 1)
                if not whole:
                    for s, k in units[-4:]:
                        low(s, k)

            def split(layer, n):
                if n >= len(TILES):
                    return
                _, idx, col = TILES[n]
                nxt("tile_high_ready")
                r = (layer * len(TILES) + n) % TILE_RING
                tt(wl[:, r], raw_tile(idx, col), wh[:, r].bitcast(F32), ALU.subtract).then_inc(S("tile_low_ready"), 1)

            def attention_half(layer):
                N = T if layer == 0 else LAT
                ns = 2 - layer
                units = attention_units(layer)
                for n in range(TILE_RING):
                    split(layer, n)
                step(dve.memset(ypad[:, :, :, :], 0.0))
                norm(layer, "norm1", T)
                for name in ("k", "v", "q0", "q1", "q2", "q3", "F0", "F1", "ca0", "ca1"):
                    if name == "v":
                        b = filled(dve, layer, name)
                        dve.tensor_copy(vch[:, :], b[:, :]).then_inc(free(layer, name), 1)
                    elif name[0] == "F":
                        b = filled(dve, layer, name)
                        dve.tensor_copy(Xf[:, int(name[1]), 0:N], b[:, 0:N]).then_inc(free(layer, name), 1)
                    elif name[0] == "c":
                        b = filled(dve, layer, name)
                        dve.tensor_copy(ypad[:, int(name[2]), 0:ns, HALO:HALO + LAT], b[:, 0:N].rearrange("p (s t) -> p s t", t=LAT)) \
                            .then_inc(free(layer, name), 1)
                    split(layer, TILE_NO[name] + TILE_RING)
                for t in range(5):
                    n = T if t == 0 else N
                    read(dve, layer, f"heads{t}")
                    step(dve.reciprocal(hsq[:, t, 0:n], hsq[:, t, 0:n]))
                    stt(out=qk[:, t, 0:n], in0=qk[:, t, 0:n], scalar=V(layer, "k_g" if t == 0 else "q_g"),
                        in1=hsq[:, t, 0:n], op0=ALU.mult, op1=ALU.mult).then_inc(S("head_normed"), 1)
                for c in range(2):
                    read(dve, layer, f"ca{c}")
                    read(dve, layer, f"cg{c}")
                    y = ypad[:, c, 0:ns, HALO:HALO + LAT]
                    tt(y, y, sg[:, c, 0:N].rearrange("p (s t) -> p s t", t=LAT), ALU.mult).then_inc(S("conv_gated"), 1)
                    split(layer, TILE_NO[f"cg{c}"] + TILE_RING)
                for c in range(2):
                    b = filled(dve, layer, f"P{c}")
                    dve.tensor_copy(Xp[:, c, 0:N], b[:, 0:N]).then_inc(free(layer, f"P{c}"), 1)
                    split(layer, TILE_NO[f"P{c}"] + TILE_RING)
                b = filled(dve, layer, "vtok")
                dve.tensor_copy(vtok[:, :, :], b[:, :].rearrange("p (c d) -> p c d", c=4)).then_inc(free(layer, "vtok"), 1)
                dve.wait_ge(S("head_normed"), 5 * layer + 5)
                cos = C("cos").unsqueeze(1).broadcast_to([P, 5, LAT])
                step(tt(hsq[:, :, 0:LAT], qk[:, :, 0:LAT], cos, ALU.mult))
                for t in range(5):
                    b = filled(dve, layer, f"rot{t}")
                    tt(hsq[:, t, LAT:T], b[:, 0:LAT], C("sin"), ALU.mult).then_inc(free(layer, f"rot{t}"), 1)
                for t in range(5):
                    read(dve, layer, f"rot{t}")
                tt(qk[:, :, 0:LAT], hsq[:, :, 0:LAT], hsq[:, :, LAT:T], ALU.add).then_inc(S("roped"), 1)
                dve.wait_ge(S("roped"), layer + 1)
                for s in range(ns):
                    for c in range(2):
                        b = filled(dve, layer, f"Y{s}{c}")
                        dve.tensor_copy(Yf[:, 2 * s + c], b[:, :].rearrange("p (t n) -> p t n", t=2)).then_inc(free(layer, f"Y{s}{c}"), 1)
                for s in range(ns):
                    for c in range(2):
                        b = filled(dve, layer, f"Z{s}{c}")
                        dve.tensor_copy(Zp[:, 2 * s + c], b[:, 0:2 * P].rearrange("p (t n) -> p t n", t=2)) \
                            .then_inc(free(layer, f"Z{s}{c}"), 1)
                for s in range(ns):
                    for c in range(2):
                        b = filled(dve, layer, f"f{s}{c}")
                        dve.tensor_copy(fT[:, c, s * LAT:(s + 1) * LAT], b[:, 0:LAT]).then_inc(free(layer, f"f{s}{c}"), 1)
                for s in range(ns):
                    for c in range(2):
                        b = filled(dve, layer, f"p{s}{c}")
                        w = V(layer, "pool_scale")[:, c:c + 1]
                        for h in range(2):
                            part = slice(64 * h, 64 * h + 64)
                            last = ts(plT[part, c, s * LAT:(s + 1) * LAT], b[part, h * LAT:(h + 1) * LAT], w[part], None, ALU.mult)
                        last.then_inc(free(layer, f"p{s}{c}"), 1)
                for g in range(NKV):
                    b = filled(dve, layer, f"dup{g}")
                    dve.tensor_copy(kdup[:, g, :], b[:, :]).then_inc(free(layer, f"dup{g}"), 1)

                def maximum(u):
                    n = T if units[u][0] == 0 else CTX
                    b = filled(dve, layer, f"S{u}")
                    step(dve.tensor_reduce(stat[:, u % 4, 3:4], b[:, 0:n], AX, ALU.max))
                    ts(stat[:, u % 4, 0:1], stat[:, u % 4, 3:4], -HD ** -0.5, None, ALU.mult).then_inc(S("negmax_ready"), 1)

                def normalise(u):
                    n = T if units[u][0] == 0 else CTX
                    read(dve, layer, f"S{u}")
                    step(dve.reciprocal(stat[:, u % 4, 2:3], stat[:, u % 4, 1:2]))
                    ts(prob[:, u % 3, 0:n], prob[:, u % 3, 0:n], stat[:, u % 4, 2:3], None, ALU.mult) \
                        .then_inc(S("prob_ready"), 1)

                def keep_values(v):
                    s, g, qt, _ = units[4 * v]
                    b = filled(dve, layer, f"V{v}")
                    q0 = s * LAT + qt * P
                    dve.tensor_copy(attnT[:, 2 * g:2 * g + 2, q0:q0 + P], b[:, 0:256].rearrange("p (c q) -> p c q", q=P)) \
                        .then_inc(free(layer, f"V{v}"), 1)

                for u in range(len(units) + LAG + 2):
                    if u < len(units):
                        maximum(u)
                    if 1 <= u <= len(units):
                        normalise(u - 1)
                    if u > LAG + 1 and (u - LAG - 2) % 4 == 3:
                        keep_values((u - LAG - 2) // 4)

                dve.wait_ge(S("conv_gated"), 2 * layer + 2)

                def tap(k, c):
                    src = ypad[:, c, 0:ns, k:k + LAT]
                    dst = conv[:, c, 0:N].rearrange("p (s t) -> p s t", t=LAT)
                    w = V(layer, "taps")[:, c * CONV_K + k:c * CONV_K + k + 1]
                    if k == 0:
                        step(ts(dst, src, w, V(layer, "conv_b")[:, c:c + 1], ALU.mult, ALU.add), lag=1)
                    else:
                        step(stt(out=dst, in0=src, scalar=w, in1=dst, op0=ALU.mult, op1=ALU.add), lag=1)

                taps = [(k, c) for k in range(CONV_K) for c in range(2)]
                for bi, i in enumerate(BRANCH_ORDER):
                    if i == 1:
                        read(dve, layer, "convnorm")
                        step(dve.reciprocal(rstd[:, 0:N], root[:, 0:N]))
                        for c in range(2):
                            stt(out=conv[:, c, 0:N], in0=conv[:, c, 0:N], scalar=V(layer, "conv_g")[:, c:c + 1],
                                in1=rstd[:, 0:N], op0=ALU.mult, op1=ALU.mult).then_inc(S("conv_normed"), 1)
                    for j in range(KD):
                        n = KD * bi + j
                        read(dve, layer, f"gate{i}{j}")
                        b = filled(dve, layer, f"branch{i}{j}")
                        if bi == 0:
                            tt(merged[:, j, 0:N], sg[:, n % 2, 0:N], b[:, 0:N], ALU.mult).then_inc(free(layer, f"branch{i}{j}"), 1)
                        else:
                            tt(sq[:, n % 2, 0:N], sg[:, n % 2, 0:N], b[:, 0:N], ALU.mult).then_inc(free(layer, f"branch{i}{j}"), 1)
                            read(dve, layer, f"branch{i}{j}")
                            add = tt(merged[:, j, 0:N], merged[:, j, 0:N], sq[:, n % 2, 0:N], ALU.add)
                            if bi == 3:
                                add.then_inc(S("merged_ready"), 1)
                            else:
                                step(add)
                        split(layer, TILE_NO[f"gate{i}{j}"] + TILE_RING)
                        if taps:
                            for k, c in taps[:4]:
                                tap(k, c)
                            taps = taps[4:]
                            if not taps:
                                dve.wait_ge(S("dve_own"), own[0])
                                dve.sem_inc(S("conv_summed"), 1)
                for j in range(KD):
                    add_square(layer, "norm2", j - 1, N)
                    if layer == 0 and j == 6:
                        slice_low(0, 0)
                        mod_low(0, 0)
                    if layer == 0 and j == 7:
                        mod_low(0, 1)
                    b = filled(dve, layer, f"out{j}")
                    for s in range(ns):
                        x = xT[:, j, s * LAT:(s + 1) * LAT]
                        last = stt(out=x, in0=b[:, s * LAT:(s + 1) * LAT], scalar=modT[:, layer, 2 * KD + j, s:s + 1], in1=x,
                                   op0=ALU.mult, op1=ALU.add)
                    last.then_inc(free(layer, f"out{j}"), 1)
                norm(layer, "norm2", N)

            dve.wait_ge(S("cs_high_ready"), 1)
            tt(cs4[:, :, 2:4], cs[:, :].rearrange("p (k v) -> p k v", k=KD), cs4[:, :, 0:2].bitcast(F32), ALU.subtract) \
                .then_inc(S("cs_low_ready"), 1)
            dve.wait_ge(S("vec_in"), 16)
            dve.wait_ge(S("const_in"), 16)
            modulation()
            gains(0)
            dve.wait_ge(S("x_in"), 16)
            attention_half(0)
            def mod_cols(n, a):
                dve.wait_ge(S("ffn_mod_turned"), n + 1)
                add_bias(1, a, banks[6]).then_inc(S("ffn_mod_read"), 1)

            def turn(i, last):
                dve.wait_ge(S("ffn_high_ready"), 3 * i + 3)
                tt(f2l[:, :, :], f2, f2h[:, :, :].bitcast(F32), ALU.subtract).then_inc(S("ffn_low_ready"), 1)
                mod_low(i + 1, 0)
                for s in range(2):
                    if s:
                        mod_cols(i, i * 4)
                        mod_low(i + 1, 1)
                    dve.wait_ge(S("ffn_silu_ready"), i * 2 + (s + 1))
                    dve.wait_ge(S("ffn_up3_full"), i * 2 + (s + 1))
                    tt(fprod[:, s, :], fsil[:, s, :], banks[2 * s + 1][:, :], ALU.mult).then_inc(S("ffn_product_ready"), 1)
                    dve.wait_ge(S("ffn_act_high_ready"), i * 2 + (s + 1))
                    tt(fal[:, s, :], fprod[:, s, :], fah[:, s, :].bitcast(F32), ALU.subtract).then_inc(S("ffn_act_ready"), 1)
                    if not last:
                        slice_low(s, i + 1)
                dve.wait_ge(S("ffn_y_free"), i * KD + 1)
                for d in range(KD):
                    if last:
                        add_square(1, "norm1", d - 1, T)
                    dve.wait_ge(S("ffn_y_full"), i * KD + (d + 1))
                    for s in range(2):
                        x = xT[:, d, s * LAT:(s + 1) * LAT]
                        last_ins = stt(out=x, in0=banks[4 + d % 4][:, s * LAT:(s + 1) * LAT],
                                       scalar=modT[:, 0, 5 * KD + d, s:s + 1], in1=x, op0=ALU.mult, op1=ALU.add)
                    last_ins.then_inc(S("ffn_y_free"), 1)

            slice_low(1, 0)
            with dve.Fori(0, F_TILES // 2 - 1) as i:
                turn(i, False)
            turn(F_TILES // 2 - 1, True)
            dve.wait_ge(S("ffn_y_free"), 1 + KD * F_TILES // 2)
            mod_cols(MOD_BLOCKS - 1, 4 * (MOD_BLOCKS - 1))
            dve.wait_ge(S("ffn_mod_read"), MOD_BLOCKS)
            gains(1)
            attention_half(1)

            dve.wait_ge(S("logits_full"), 1)
            for t in range(2):
                step(dve.tensor_copy(R[:, LOGITS, t], banks[6 * t][:, 0:E]))
            iota8 = C("iota8")
            top = R[:, TOP, 0]

            def choose(src, one, at):
                for t in range(2):
                    step(dve.tensor_reduce(top[:, at + t:at + t + 1], R[:, src, t], AX, ALU.max))
                    step(stt(out=R[:, EQUAL, t], in0=R[:, src, t], scalar=top[:, at + t:at + t + 1], in1=iota8,
                             op0=ALU.is_equal, op1=ALU.mult))
                    step(dve.tensor_reduce(top[:, 6 + t:7 + t], R[:, EQUAL, t], AX, ALU.max))
                    step(ts(R[:, one, t], R[:, EQUAL, t], top[:, 6 + t:7 + t], None, ALU.is_equal))

            choose(LOGITS, FIRST, 0)
            step(stt(out=R[:, REST], in0=R[:, FIRST], scalar=-3.0e38, in1=R[:, LOGITS], op0=ALU.mult, op1=ALU.add))
            choose(REST, SECOND, 2)
            tt(R[:, MASK], R[:, FIRST], R[:, SECOND], ALU.add).then_inc(S("mask_ready"), 1)
            dve.wait_ge(S("mask_ready"), 1)
            tt(R[:, GAP, 0, 0:2], top[:, 2:4], top[:, 0:2], ALU.subtract).then_inc(S("gap_ready"), 1)
            dve.wait_ge(S("odds_ready"), 1)
            odds, w = R[:, ODDS, 0, 0:2], R[:, WEIGHT, 0]
            step(ts(R[:, GAP, 0, 2:4], odds, 1.0, None, ALU.add))
            step(dve.reciprocal(w[:, 0:2], R[:, GAP, 0, 2:4]))
            step(tt(w[:, 2:4], w[:, 0:2], odds, ALU.mult))
            for t in range(2):
                step(ts(R[:, FIRST, t], R[:, FIRST, t], w[:, t:t + 1], None, ALU.mult))
                step(stt(out=R[:, COMB, t], in0=R[:, SECOND, t], scalar=w[:, 2 + t:3 + t], in1=R[:, FIRST, t],
                         op0=ALU.mult, op1=ALU.add))
            dve.wait_ge(S("rank_full"), 1)
            step(ts(R[:, EQUAL], R[:, MASK], -1.0, 1000.0, ALU.add, ALU.mult))
            step(tt(R[:, RANK], banks[5][:, 0:2 * E].rearrange("p (t e) -> p t e", t=2), R[:, MASK], ALU.mult))
            step(tt(R[:, RANK], R[:, RANK], R[:, EQUAL], ALU.add))
            step(dve.tensor_reduce(over_f[:, :], banks[5][:, 2 * E:3 * E], AX, ALU.max))
            dve.tensor_copy(over_i[:, :], over_f[0:1, :]).then_inc(S("over_ready"), 1)

            def chunk_low(m, u):
                dve.wait_ge(S("moe_up_high"), m + 1)
                tt(m13l[:, u % 2], chunk[u][:, 0:2 * D].rearrange("p (k n) -> p k n", k=KD), m13h[:, u % 2].bitcast(F32),
                   ALU.subtract).then_inc(S("moe_up_low"), 1)
                dve.wait_ge(S("moe_down_high"), m + 1)
                tt(m2l[:, u, :], chunk[u][:, 2 * D:CHUNK], m2h[:, u, :].bitcast(F32), ALU.subtract).then_inc(S("moe_split"), 1)

            def gathered_low(count):
                for hf in range(2):
                    dve.wait_ge(S("gathered_high"), count + (hf + 1))
                    tt(hgl[:, 4 * hf:4 * hf + 4, :], banks[6 + hf][:, :].rearrange("p (k s) -> p k s", k=4),
                       hgh[:, 4 * hf:4 * hf + 4, :].bitcast(F32), ALU.subtract).then_inc(S("gathered_low"), 1)

            step(dve.memset(Pm[:, :, E * SLOTS:(E + 1) * SLOTS], 0.0))

            def experts(n):
                if n:
                    step(ts(R[:, RANK], R[:, RANK], -float(SLOTS), None, ALU.add))
                for t in range(2):
                    for e in range(E):
                        rank = R[:, RANK, t, e:e + 1]
                        ts(Pm[:, t, e * SLOTS:(e + 1) * SLOTS], C("iota"), rank, None, ALU.is_equal)
                        last = ts(Pw[:, t, e, :], C("iota"), rank, R[:, COMB, t, e:e + 1], ALU.is_equal, ALU.mult)
                last.then_inc(S("select_ready"), 1)
                gathered_low(n * 2 * (E + 1))
                if n == 0:
                    chunk_low(0, 0)
                def update(e, half):
                    if half == 0:
                        dve.wait_ge(S("scatter_free"), e * 4 + (n * 4 * E + 1))
                    for q in range(2 * half, 2 * half + 2):
                        dve.wait_ge(S("scatter_full"), e * 4 + (n * 4 * E + q + 1))
                        for i in range(2):
                            k = 2 * q + i
                            x = xT[:, k, 0:LAT]
                            last = stt(out=x, in0=banks[6 + q % 2][:, i * LAT:(i + 1) * LAT],
                                       scalar=modT[:, 1, 5 * KD + k, 0:1], in1=x, op0=ALU.mult, op1=ALU.add)
                        last.then_inc(S("scatter_free"), 1)

                def expert(e, first=False):
                    m0 = e * FE_TILES + n * E * FE_TILES

                    def product(m, u):
                        dve.wait_ge(S("moe_silu"), m + 1)
                        tt(mprod[:, u % 2, :], msil[:, u % 2, :], banks[u % 2][:, P:2 * P], ALU.mult).then_inc(S("moe_product"), 1)

                    def act_low(m, u):
                        dve.wait_ge(S("moe_act_high"), m + 1)
                        tt(mal[:, u % 2, :], banks[2 + u % 2][:, 0:SLOTS], mah[:, u % 2, :].bitcast(F32), ALU.subtract) \
                            .then_inc(S("moe_act_low"), 1)

                    for u in range(MOE_UNROLL):
                        chunk_low(m0 + (u + 1), (u + 1) % 4)
                        product(m0 + u, u)
                        if u:
                            act_low(m0 + (u - 1), u - 1)
                        if u >= 2 and not first:
                            update(e - 1, u - 2)
                    with dve.Fori(1, MOE_TURNS) as q:
                        m = m0 + q * MOE_UNROLL
                        for u in range(MOE_UNROLL):
                            chunk_low(m + (u + 1), (u + 1) % 4)
                            product(m + u, u)
                            act_low(m + (u - 1), (u - 1) % 4)
                    gathered_low(e * 2 + (n * 2 * (E + 1) + 2))
                    act_low(m0 + (FE_TILES - 1), 3)

                expert(0, first=True)
                with dve.Fori(1, E) as e:
                    expert(e)
                for half in range(2):
                    update(E - 1, half)

            experts(0)
            dve.wait_ge(S("over_ready"), 1)
            over = dve.value_load(over_i[0:1, 0:1], min_val=0, max_val=LAT)
            with dve.If(over > SLOTS):
                experts(1)


def constants():
    c = np.zeros((P, CONST_LEN), np.float64)

    def put(name, a):
        c[:a.shape[0], CONST[name][0]:CONST[name][1]] = a

    i = np.arange(P)
    put("ident", np.eye(P))
    put("ones", np.ones((P, P)))
    put("heads", (i[:, None] // HD == i[None, :] // HD).astype(float))
    rot = np.zeros((P, P))
    for out_c in range(P):
        rot[out_c + 16 if out_c % 32 < 16 else out_c - 16, out_c] = -1.0 if out_c % 32 < 16 else 1.0
    put("rot", rot)
    for g in range(NKV):
        d = np.zeros((P, P))
        d[HD * g + i % HD, i] = 1.0
        put(f"dup{g}", d)
    ch = np.outer(np.arange(64), np.arange(64)) * (2 * np.pi / 64)
    eye2 = np.eye(2)
    norm = 1.0 / np.sqrt(64.0 * LAT)
    put("chan_cos", np.kron(eye2, np.cos(ch)) * norm)
    put("chan_sin", -np.kron(eye2, np.sin(ch)) * norm)
    put("pair", np.tile(np.eye(2), (2, 1)))
    put("below", (i[:, None] < i[None, :]).astype(float))
    put("iota", np.tile(i[None, :], (P, 1)))
    put("iota8", np.tile(E - np.arange(E)[None, :], (P, 1)))
    put("eps", np.full((P, 1), EPS))
    t = np.outer(np.arange(LAT), np.arange(LAT)) % LAT * (2 * np.pi / LAT)
    s = np.concatenate([np.cos(t), np.sin(t)], axis=1).reshape(2, P, 512)
    put("seq", s.transpose(1, 0, 2).reshape(P, 1024))
    n_freq = HD // 4
    freqs = (10000.0 ** (-np.arange(n_freq) / n_freq)).astype(np.float32)
    tok = np.arange(LAT)
    where = np.where((i % HD < 32)[:, None], (tok // GRID_W)[None, :], (tok % GRID_W)[None, :])
    angle = where.astype(np.float32) * freqs[i % 16][:, None]
    put("cos", np.cos(angle.astype(np.float64)))
    put("sin", np.sin(angle.astype(np.float64)))
    m = np.zeros((2, 2, P, 2, LAT))
    for g, w in enumerate(WINDOWS):
        full = np.zeros((LAT, LAT))
        for o in range(LAT):
            lo, hi = max(o - w // 2, 0), min(o + w // 2, LAT)
            full[lo:hi, o] = 1.0 / (hi - lo)
            full[o, o] -= 1.0
        m[g // 2, :, :, g % 2, :] = full.reshape(2, P, LAT)
    pool = m.transpose(2, 0, 1, 3, 4).reshape(P, POOL_LEN)
    return c.astype(np.float32), pool.astype(np.float32)


def tiled(w, width):
    k, n = w.shape
    return w.reshape(k // P, P, n // width, width).transpose(2, 1, 0, 3).reshape(n // width, P, k // P * width)


def columns(v):
    return np.ascontiguousarray(v.reshape(-1, P).T)


def layout(a):
    a = {k: np.asarray(v) for k, v in a.items()}
    x = np.concatenate([a["x"][0], a["ctx"][0]], axis=0)
    vec = np.zeros((P, DEPTH, VEC_LEN), np.float32)
    attn = np.zeros((DEPTH, N_BLOCKS, P, SLOT_LEN), np.float32)
    for l in range(DEPTH):
        def put(name, v):
            vec[:, l, COLS[name][0]:COLS[name][1]] = v

        put("b_mod", columns(a["b_mod"][l]))
        put("norm1", columns(a["norm1_g"][l]))
        put("norm2", columns(a["norm2_g"][l]))
        put("conv_b", columns(a["conv_b"][l]))
        put("conv_g", columns(a["conv_norm_g"][l]))
        put("pool_scale", columns(a["pool_scale"][l]))
        put("q_g", np.tile(a["q_norm_g"][l], 2)[:, None])
        put("k_g", np.tile(a["k_norm_g"][l], 2)[:, None])
        put("taps", a["conv_dw"][l].T.reshape(2, P, CONV_K).transpose(1, 0, 2).reshape(P, -1))
        pw = np.zeros((P, 2, P), np.float32)
        for g in range(4):
            h = 64 * (g % 2)
            pw[h:h + 64, g // 2, h:h + 64] = a["pool_w"][l, g]
        put("pool_w", pw.reshape(P, -1))
        w = a["w_in"][l]
        off_q = 1024
        off_k, off_g = off_q + 512, off_q + 768
        attn[l, BLOCK_KV, :, 0:KD * 256] = tiled(w[:, off_k:off_g], 256)[0]
        attn[l, BLOCK_Q, :, 0:KD * 512] = tiled(w[:, off_q:off_k], 512)[0]
        attn[l, BLOCK_FC, :, 0:KD * 512] = tiled(w[:, 0:512], 512)[0]
        attn[l, BLOCK_GP, :, 0:KD * 512] = tiled(w[:, 512:1024], 512)[0]
        branch = [a["w_br_fourier"][l], a["w_br_conv"][l], a["w_br_pool"][l], a["w_br_attn"][l]]
        for b, i in enumerate(BRANCH_ORDER):
            gate = tiled(w[:, off_g + i * D:off_g + (i + 1) * D], 512)
            br = tiled(branch[i], 512)
            for hf in range(2):
                attn[l, BLOCK_BRANCH + 2 * b + hf, :, 0:KD * 512] = gate[hf]
                attn[l, BLOCK_BRANCH + 2 * b + hf, :, KD * 512:(KD + BRANCH_K[i]) * 512] = br[hf]
        attn[l, BLOCK_OUT:, :, 0:KD * 512] = tiled(a["w_out"][l], 512)
    consts, pool = constants()
    cond = np.stack([a["c"][0].reshape(KD, P), a["c_ctx"].reshape(KD, P)], axis=2)
    f1, f3, f2 = a["ffn_w1"][0], a["ffn_w3"][0], a["ffn_w2"][0]
    turns = F_TILES // 2
    ffn13 = np.stack([tiled(f1, P), tiled(f3, P)], axis=2).reshape(turns, 2, P, 2 * D)
    ffn2 = f2.reshape(turns, 2, P, D).transpose(0, 2, 1, 3).reshape(turns, P, 2 * D)
    moe = np.empty((E * FE_TILES + 1, P, CHUNK), np.float32)
    for e in range(E):
        rows = moe[e * FE_TILES:(e + 1) * FE_TILES]
        up = rows[:, :, 0:2 * D].reshape(FE_TILES, P, KD, 2, P)
        up[:, :, :, 0] = tiled(a["moe_w1"][0, e], P).reshape(FE_TILES, P, KD, P)
        up[:, :, :, 1] = tiled(a["moe_w3"][0, e], P).reshape(FE_TILES, P, KD, P)
        rows[:, :, 0:2 * D] = up.reshape(FE_TILES, P, 2 * D)
        rows[:, :, 2 * D:] = a["moe_w2"][0, e].reshape(FE_TILES, P, D)
    moe[-1] = moe[0]
    return {
        "xT": np.ascontiguousarray(x.T.reshape(KD, P, T).transpose(1, 0, 2)),
        "consts": consts,
        "pool_windows": pool,
        "vectors": vec,
        "cond": np.ascontiguousarray(cond.transpose(1, 0, 2).reshape(P, 2 * KD)),
        "router": np.ascontiguousarray(a["moe_router"][0].reshape(KD, P, E).transpose(1, 0, 2)),
        "w_mod_blocks": np.stack([tiled(a["w_mod"][l], 512) for l in range(DEPTH)]),
        "attn_blocks": attn,
        "ffn13": ffn13,
        "ffn2": np.ascontiguousarray(ffn2),
        "moe": moe,
    }


def kernel(**inputs):
    import concourse.bacc as bacc
    from concourse.bass_utils import run_bass_kernel_spmd

    arrays = layout(inputs)
    nc = bacc.Bacc("TRN2", target_bir_lowering=False, num_devices=1)
    args = [nc.dram_tensor(f"in_{name}", v.shape, mybir.dt.from_np(v.dtype), kind="ExternalInput").ap() for name, v in arrays.items()]
    out = nc.dram_tensor("outT", (P, KD, LAT), F32, kind="ExternalOutput").ap()
    build(nc, *args, out)
    got = run_bass_kernel_spmd(nc, [{f"in_{k}": v for k, v in arrays.items()}], core_ids=[0]).results[0]["outT"]
    return np.ascontiguousarray(got.transpose(2, 1, 0).reshape(1, LAT, D))
```
